# Optimizing a Trainium2 kernel written in Bass

```python
import math
import jax, jax.numpy as jnp
from jax import lax
import numpy as np

D_MODEL = 1024
BATCH = 1
SEQ = 512
DEPTH = 1

HEAD_DIM = 64
D_ATTN = D_MODEL // 2
D_RWKV = D_MODEL - D_ATTN
N_Q_HEADS = D_ATTN // HEAD_DIM
N_KV_HEADS = max(1, N_Q_HEADS // 4)
Q_PER_KV = N_Q_HEADS // N_KV_HEADS
D_KV = N_KV_HEADS * HEAD_DIM
WINDOW = 128
BLOCK = 128
N_BUCKETS = 32
MAX_DISTANCE = 128
N_RWKV_HEADS = D_RWKV // HEAD_DIM
LORA_DECAY = 64
LORA_ICLR = 64
LORA_GATE = 128
RWKV_COLS = 3 * D_RWKV + LORA_DECAY + LORA_ICLR + LORA_GATE
RWKV_SPLITS = (D_RWKV, 2 * D_RWKV, 3 * D_RWKV, 3 * D_RWKV + LORA_DECAY, 3 * D_RWKV + LORA_DECAY + LORA_ICLR)
D_IN = D_ATTN + 2 * D_KV + RWKV_COLS
D_FF = 4 * D_MODEL
CONV_WIDTH = 3
NORM_EPS = 1e-6
GN_EPS = 64e-5
NEG_INF = -1e30


def rms_norm(x, g):
    xf = x.astype(jnp.float32)
    y = xf * lax.rsqrt(jnp.mean(xf * xf, axis=-1, keepdims=True) + NORM_EPS) * g.astype(jnp.float32)
    return y.astype(x.dtype)

def t5_bucket(rel):
    n = jnp.maximum(rel, 0)
    max_exact = N_BUCKETS // 2
    large = max_exact + (jnp.log(jnp.maximum(n, 1).astype(jnp.float32) / max_exact)
                         / math.log(MAX_DISTANCE / max_exact) * (N_BUCKETS - max_exact)).astype(jnp.int32)
    large = jnp.minimum(large, N_BUCKETS - 1)
    return jnp.where(n < max_exact, n, large)

def sliding_window_sink_attention(q, k, v, rel_bias, sinks):
    B, S, _ = q.shape
    NB = S // BLOCK
    q = q.reshape(B, NB, BLOCK, N_KV_HEADS, Q_PER_KV, HEAD_DIM)

    def band(t):
        t = t.reshape(B, NB, BLOCK, N_KV_HEADS, HEAD_DIM)
        prev = jnp.concatenate([jnp.zeros_like(t[:, :1]), t[:, :-1]], axis=1)
        return jnp.concatenate([prev, t], axis=2)

    kb, vb = band(k), band(v)
    rel = (jnp.arange(BLOCK)[:, None] + BLOCK) - jnp.arange(2 * BLOCK)[None, :]
    in_window = (rel >= 0) & (rel < WINDOW)
    key_pos = (jnp.arange(NB)[:, None] - 1) * BLOCK + jnp.arange(2 * BLOCK)[None, :]
    mask = in_window[None] & (key_pos >= 0)[:, None, :]
    bias = rel_bias.astype(jnp.float32)[t5_bucket(rel)]
    bias = bias.transpose(2, 0, 1).reshape(N_KV_HEADS, Q_PER_KV, BLOCK, 2 * BLOCK)
    scores = jnp.einsum('bnqhgd,bnkhd->bnhgqk', q, kb).astype(jnp.float32) * (HEAD_DIM ** -0.5) + bias
    scores = jnp.where(mask[None, :, None, None], scores, NEG_INF)
    sink = sinks.astype(jnp.float32).reshape(N_KV_HEADS, Q_PER_KV)[:, :, None, None]
    m = jnp.maximum(scores.max(axis=-1, keepdims=True), sink)
    p = jnp.exp(scores - m)
    probs = p / (p.sum(axis=-1, keepdims=True) + jnp.exp(sink - m))
    out = jnp.einsum('bnhgqk,bnkhd->bnqhgd', probs.astype(v.dtype), vb)
    return out.reshape(B, S, D_ATTN)

def rwkv7_time_mix(p, w0, w_decay_up, a0, w_iclr_up, w_gate_up, k_k, k_a, r_k, ln_x_g, ln_x_b):
    B, S, _ = p.shape
    H, N = N_RWKV_HEADS, HEAD_DIM
    p = p.astype(jnp.float32)
    r, k, v, zw, za, zg = jnp.split(p, RWKV_SPLITS, axis=-1)
    w_log = -jax.nn.softplus(-(w0 + jnp.tanh(zw) @ w_decay_up)) - 0.5
    decay = jnp.exp(-jnp.exp(w_log))
    a = jax.nn.sigmoid(a0 + za @ w_iclr_up)
    g = jax.nn.sigmoid(zg) @ w_gate_up
    kk = (k * k_k).reshape(B, S, H, N)
    kk = kk / jnp.maximum(jnp.sqrt(jnp.sum(kk * kk, axis=-1, keepdims=True)), 1e-12)
    k = k * (1.0 + (a - 1.0) * k_a)

    def heads(t):
        return t.reshape(B, S, H, N)

    def tmaj(t):
        return t.swapaxes(0, 1)

    rh, kh, vh = heads(r), heads(k), heads(v)

    def step(state, inp):
        r_t, w_t, k_t, v_t, kk_t, a_t = inp
        sa = jnp.einsum('bhvk,bhk->bhv', state, -kk_t)
        state = (state * w_t[:, :, None, :]
                 + sa[..., None] * (kk_t * a_t)[:, :, None, :]
                 + v_t[..., None] * k_t[:, :, None, :])
        return state, jnp.einsum('bhvk,bhk->bhv', state, r_t)

    state0 = jnp.zeros((B, H, N, N), jnp.float32)
    _, o = lax.scan(step, state0, (tmaj(rh), tmaj(heads(decay)), tmaj(kh), tmaj(vh), tmaj(kk), tmaj(heads(a))))
    o = o.swapaxes(0, 1)
    mu = jnp.mean(o, axis=-1, keepdims=True)
    var = jnp.mean(jnp.square(o - mu), axis=-1, keepdims=True)
    o = ((o - mu) * lax.rsqrt(var + GN_EPS)).reshape(B, S, D_RWKV) * ln_x_g + ln_x_b
    bonus = jnp.sum(rh * kh * r_k, axis=-1, keepdims=True) * vh
    o = o + bonus.reshape(B, S, D_RWKV)
    return o * g

def conv_gated_ffn(h, w_up, conv_w, conv_b, w_down):
    S = h.shape[1]
    u = h @ w_up
    u_pad = jnp.pad(u, ((0, 0), (CONV_WIDTH - 1, 0), (0, 0)))
    u = conv_b + sum(conv_w[j] * u_pad[:, j:j + S] for j in range(CONV_WIDTH))
    gate, val = jnp.split(u, 2, axis=-1)
    return (jax.nn.gelu(gate, approximate=True) * val) @ w_down

def first_inputs(seed: int = 0) -> dict:
    key = jax.random.key(seed)
    ks = jax.random.split(key, 24)
    L = DEPTH
    nrm = lambda k, shape, s: jax.random.normal(k, shape, jnp.float32) * s
    return {
        "x": jax.random.normal(ks[0], (BATCH, SEQ, D_MODEL), jnp.float32),
        "norm_mix_pre": 1.0 + nrm(ks[1], (L, D_MODEL), 0.02),
        "norm_mix_post": 1.0 + nrm(ks[2], (L, D_MODEL), 0.02),
        "norm_ffn_pre": 1.0 + nrm(ks[3], (L, D_MODEL), 0.02),
        "norm_ffn_post": 1.0 + nrm(ks[4], (L, D_MODEL), 0.02),
        "w_in": nrm(ks[5], (L, D_MODEL, D_IN), D_MODEL ** -0.5),
        "rel_bias": nrm(ks[6], (N_BUCKETS, N_Q_HEADS), 0.5),
        "sinks": nrm(ks[7], (L, N_Q_HEADS), 0.5),
        "rwkv_shift_mix": jax.random.uniform(ks[8], (L, RWKV_COLS), jnp.float32),
        "w0": jax.random.uniform(ks[9], (L, D_RWKV), jnp.float32, -5.0, 0.0),
        "w_decay_up": nrm(ks[10], (L, LORA_DECAY, D_RWKV), 0.5 * LORA_DECAY ** -0.5),
        "a0": nrm(ks[11], (L, D_RWKV), 0.1),
        "w_iclr_up": nrm(ks[12], (L, LORA_ICLR, D_RWKV), 0.5 * LORA_ICLR ** -0.5),
        "w_gate_up": nrm(ks[13], (L, LORA_GATE, D_RWKV), LORA_GATE ** -0.5),
        "k_k": 0.85 + nrm(ks[14], (L, D_RWKV), 0.05),
        "k_a": 1.0 + nrm(ks[15], (L, D_RWKV), 0.05),
        "r_k": nrm(ks[16], (L, N_RWKV_HEADS, HEAD_DIM), 0.1),
        "ln_x_g": 1.0 + nrm(ks[17], (L, D_RWKV), 0.02),
        "ln_x_b": nrm(ks[18], (L, D_RWKV), 0.02),
        "w_out": nrm(ks[19], (L, D_MODEL, D_MODEL), D_MODEL ** -0.5),
        "w_ffn_up": nrm(ks[20], (L, D_MODEL, 2 * D_FF), D_MODEL ** -0.5),
        "conv_w": nrm(ks[21], (L, CONV_WIDTH, 2 * D_FF), CONV_WIDTH ** -0.5),
        "conv_b": nrm(ks[22], (L, 2 * D_FF), 0.02),
        "w_ffn_down": nrm(ks[23], (L, D_FF, D_MODEL), D_FF ** -0.5),
    }

def first_block(x, norm_mix_pre, norm_mix_post, norm_ffn_pre, norm_ffn_post, w_in, rel_bias, sinks,
              rwkv_shift_mix, w0, w_decay_up, a0, w_iclr_up, w_gate_up, k_k, k_a, r_k, ln_x_g, ln_x_b,
              w_out, w_ffn_up, conv_w, conv_b, w_ffn_down):
    for l in range(DEPTH):
        h = rms_norm(x, norm_mix_pre[l])
        proj = h @ w_in[l]
        q, k, v, p = jnp.split(proj, (D_ATTN, D_ATTN + D_KV, D_ATTN + 2 * D_KV), axis=-1)
        attn = sliding_window_sink_attention(q, k, v, rel_bias, sinks[l])
        p_prev = jnp.concatenate([jnp.zeros_like(p[:, :1]), p[:, :-1]], axis=1)
        p = p + (p_prev - p) * rwkv_shift_mix[l]
        rw = rwkv7_time_mix(p, w0[l], w_decay_up[l], a0[l], w_iclr_up[l], w_gate_up[l],
                            k_k[l], k_a[l], r_k[l], ln_x_g[l], ln_x_b[l])
        mix = jnp.concatenate([attn, rw.astype(x.dtype)], axis=-1) @ w_out[l]
        x = x + rms_norm(mix, norm_mix_post[l])
        f = conv_gated_ffn(rms_norm(x, norm_ffn_pre[l]), w_ffn_up[l], conv_w[l], conv_b[l], w_ffn_down[l])
        x = x + rms_norm(f, norm_ffn_post[l])
    return x


DEPTH_2 = 2

ROT_DIM = HEAD_DIM // 4
ROPE_THETA = 500000.0
Q_BLOCK = 128
EPS = 1e-6

FOX_HEADS = D_MODEL // (2 * HEAD_DIM)
FOX_WIDTH = FOX_HEADS * HEAD_DIM
FOX_FGATE_BIAS = 3.0
DIFF_V_DIM = 2 * HEAD_DIM
DIFF_HEADS = D_MODEL // (2 * DIFF_V_DIM)
DIFF_WIDTH = DIFF_HEADS * DIFF_V_DIM
DSA_HEADS = D_MODEL // (2 * HEAD_DIM)
DSA_NOPE = HEAD_DIM - ROT_DIM
DSA_WIDTH = DSA_HEADS * HEAD_DIM
DSA_KV_RANK = 128
IDX_HEADS = 4
IDX_DIM = 64
IDX_TOPK_MAX = 256
SB_HEADS = D_MODEL // (2 * HEAD_DIM)
SB_WIDTH = SB_HEADS * HEAD_DIM
D_FF_2 = 2816

EVEN_SPLITS = (FOX_WIDTH, FOX_WIDTH, FOX_WIDTH, FOX_HEADS,
               DIFF_WIDTH, DIFF_WIDTH, DIFF_WIDTH)
ODD_SPLITS = (DSA_WIDTH, DSA_KV_RANK, ROT_DIM, IDX_HEADS * IDX_DIM, IDX_HEADS, IDX_DIM,
              SB_WIDTH, SB_WIDTH, SB_WIDTH)
EVEN_IN = sum(EVEN_SPLITS)
ODD_IN = sum(ODD_SPLITS)
N_EVEN = (DEPTH_2 + 1) // 2
N_ODD = DEPTH_2 // 2


def rms_norm_2(x, g):
    xf = x.astype(jnp.float32)
    y = xf * lax.rsqrt(jnp.mean(xf * xf, axis=-1, keepdims=True) + EPS)
    return (y * g.astype(jnp.float32)).astype(x.dtype)

def split_cols(z, sizes):
    cuts = []
    acc = 0
    for s in sizes[:-1]:
        acc += s
        cuts.append(acc)
    return jnp.split(z, cuts, axis=-1)

def rope_tables(positions):
    inv_freq = ROPE_THETA ** (-jnp.arange(0, ROT_DIM, 2, dtype=jnp.float32) / ROT_DIM)
    ang = positions.astype(jnp.float32)[..., None] * inv_freq
    return jnp.cos(ang), jnp.sin(ang)

def apply_partial_rope(x, cos, sin):
    half = ROT_DIM // 2
    xr = x[..., :ROT_DIM].astype(jnp.float32)
    x1, x2 = xr[..., :half], xr[..., half:]
    rot = jnp.concatenate([x1 * cos - x2 * sin, x2 * cos + x1 * sin], axis=-1)
    return jnp.concatenate([rot.astype(x.dtype), x[..., ROT_DIM:]], axis=-1)

def sweep(block_fn, seq_len):
    out = lax.map(block_fn, jnp.arange(seq_len // Q_BLOCK))
    out = jnp.moveaxis(out, 0, 1)
    return out.reshape((out.shape[0], seq_len) + out.shape[3:])

def gather_rows(table, idx):
    return jax.vmap(lambda t, i: jnp.take(t, i, axis=0))(table, idx)

def fox_attention(q, k, v, log_f):
    seq_len = q.shape[1]
    scale = HEAD_DIM ** -0.5
    c = jnp.transpose(jnp.cumsum(log_f, axis=1), (0, 2, 1))
    kpos = jnp.arange(seq_len)

    def block(i):
        start = i * Q_BLOCK
        qpos = start + jnp.arange(Q_BLOCK)
        qb = lax.dynamic_slice_in_dim(q, start, Q_BLOCK, axis=1)
        cb = lax.dynamic_slice_in_dim(c, start, Q_BLOCK, axis=2)
        s = jnp.einsum('bqhd,bkhd->bhqk', qb, k).astype(jnp.float32) * scale
        s = s + (cb[..., :, None] - c[..., None, :])
        s = jnp.where(qpos[:, None] >= kpos[None, :], s, -jnp.inf)
        p = jax.nn.softmax(s, axis=-1).astype(v.dtype)
        return jnp.einsum('bhqk,bkhd->bqhd', p, v)

    return sweep(block, seq_len)

def diff_attention(q1, q2, k1, k2, v, lam):
    seq_len = q1.shape[1]
    scale = HEAD_DIM ** -0.5
    kpos = jnp.arange(seq_len)

    def block(i):
        start = i * Q_BLOCK
        qpos = start + jnp.arange(Q_BLOCK)
        mask = qpos[:, None] >= kpos[None, :]
        q1b = lax.dynamic_slice_in_dim(q1, start, Q_BLOCK, axis=1)
        q2b = lax.dynamic_slice_in_dim(q2, start, Q_BLOCK, axis=1)
        s1 = jnp.einsum('bqhd,bkhd->bhqk', q1b, k1).astype(jnp.float32) * scale
        s2 = jnp.einsum('bqhd,bkhd->bhqk', q2b, k2).astype(jnp.float32) * scale
        p1 = jax.nn.softmax(jnp.where(mask, s1, -jnp.inf), axis=-1)
        p2 = jax.nn.softmax(jnp.where(mask, s2, -jnp.inf), axis=-1)
        p = (p1 - lam * p2).astype(v.dtype)
        return jnp.einsum('bhqk,bkhd->bqhd', p, v)

    return sweep(block, seq_len)

def stick_breaking_attention(q, k, v):
    seq_len = q.shape[1]
    scale = HEAD_DIM ** -0.5
    kpos = jnp.arange(seq_len)

    def block(i):
        start = i * Q_BLOCK
        qpos = start + jnp.arange(Q_BLOCK)
        mask = kpos[None, :] < qpos[:, None]
        qb = lax.dynamic_slice_in_dim(q, start, Q_BLOCK, axis=1)
        z = jnp.einsum('bqhd,bkhd->bhqk', qb, k).astype(jnp.float32) * scale
        log1m = jnp.where(mask, jax.nn.log_sigmoid(-z), 0.0)
        after = lax.cumsum(log1m, axis=3, reverse=True) - log1m
        a = jnp.where(mask, jnp.exp(jax.nn.log_sigmoid(z) + after), 0.0)
        return jnp.einsum('bhqk,bkhd->bqhd', a.astype(v.dtype), v)

    return sweep(block, seq_len)

def dsa_attention(q_abs, q_rope, c_kv, k_rope, iq, iw, ik, top_k):
    seq_len = q_abs.shape[1]
    scale = HEAD_DIM ** -0.5
    kpos = jnp.arange(seq_len)

    def block(i):
        start = i * Q_BLOCK
        qpos = start + jnp.arange(Q_BLOCK)
        iqb = lax.dynamic_slice_in_dim(iq, start, Q_BLOCK, axis=1)
        iwb = lax.dynamic_slice_in_dim(iw, start, Q_BLOCK, axis=1)
        logits = jnp.einsum('bqhd,bkd->bqhk', iqb, ik).astype(jnp.float32)
        score = jnp.einsum('bqhk,bqh->bqk', jax.nn.relu(logits), iwb.astype(jnp.float32))
        score = jnp.where(kpos[None, None, :] <= qpos[None, :, None], score, -jnp.inf)
        _, sel = lax.top_k(score, top_k)
        valid = sel <= qpos[None, :, None]
        c_sel = gather_rows(c_kv, sel)
        kr_sel = gather_rows(k_rope, sel)
        qab = lax.dynamic_slice_in_dim(q_abs, start, Q_BLOCK, axis=1)
        qrb = lax.dynamic_slice_in_dim(q_rope, start, Q_BLOCK, axis=1)
        s = (jnp.einsum('bqhr,bqkr->bqhk', qab, c_sel)
             + jnp.einsum('bqhd,bqkd->bqhk', qrb, kr_sel)).astype(jnp.float32) * scale
        s = jnp.where(valid[:, :, None, :], s, -jnp.inf)
        p = jax.nn.softmax(s, axis=-1).astype(c_kv.dtype)
        return jnp.einsum('bqhk,bqkr->bqhr', p, c_sel)

    return sweep(block, seq_len)

def even_mixer(h, cos, sin, w_in, fgate_b, lq1, lk1, lq2, lk2, subln, w_out, layer_idx):
    b, s, _ = h.shape
    aq, ak, av, af, bq, bk, bv = split_cols(h @ w_in, EVEN_SPLITS)
    log_f = jax.nn.log_sigmoid((af + fgate_b).astype(jnp.float32))
    o_a = fox_attention(aq.reshape(b, s, FOX_HEADS, HEAD_DIM),
                        ak.reshape(b, s, FOX_HEADS, HEAD_DIM),
                        av.reshape(b, s, FOX_HEADS, HEAD_DIM), log_f)
    cs, sn = cos[:, :, None, :], sin[:, :, None, :]
    bq = bq.reshape(b, s, DIFF_HEADS, 2, HEAD_DIM)
    bk = bk.reshape(b, s, DIFF_HEADS, 2, HEAD_DIM)
    q1 = apply_partial_rope(bq[..., 0, :], cs, sn)
    q2 = apply_partial_rope(bq[..., 1, :], cs, sn)
    k1 = apply_partial_rope(bk[..., 0, :], cs, sn)
    k2 = apply_partial_rope(bk[..., 1, :], cs, sn)
    lam_init = 0.8 - 0.6 * math.exp(-0.3 * layer_idx)
    lam = (jnp.exp(jnp.sum(lq1.astype(jnp.float32) * lk1.astype(jnp.float32)))
           - jnp.exp(jnp.sum(lq2.astype(jnp.float32) * lk2.astype(jnp.float32))) + lam_init)
    o_b = diff_attention(q1, q2, k1, k2, bv.reshape(b, s, DIFF_HEADS, DIFF_V_DIM), lam)
    o_b = rms_norm_2(o_b, subln) * (1.0 - lam_init)
    o = jnp.concatenate([o_a.reshape(b, s, FOX_WIDTH), o_b.reshape(b, s, DIFF_WIDTH)], axis=-1)
    return o @ w_out

def odd_mixer(h, cos, sin, w_in, kv_norm, w_uk, w_uv, w_out, top_k):
    b, s, _ = h.shape
    cq, ckv, ckr, ciq, ciw, cik, sq, sk, sv = split_cols(h @ w_in, ODD_SPLITS)
    cs, sn = cos[:, :, None, :], sin[:, :, None, :]
    cq = apply_partial_rope(cq.reshape(b, s, DSA_HEADS, HEAD_DIM), cs, sn)
    q_rope, q_nope = cq[..., :ROT_DIM], cq[..., ROT_DIM:]
    c_kv = rms_norm_2(ckv, kv_norm)
    k_rope = apply_partial_rope(ckr, cos, sin)
    q_abs = jnp.einsum('bshn,rhn->bshr', q_nope, w_uk)
    iq = apply_partial_rope(ciq.reshape(b, s, IDX_HEADS, IDX_DIM), cs, sn)
    ik = apply_partial_rope(cik, cos, sin)
    iw = ciw * (IDX_HEADS ** -0.5)
    o_lat = dsa_attention(q_abs, q_rope, c_kv, k_rope, iq, iw, ik, top_k)
    o_c = jnp.einsum('bshr,rhd->bshd', o_lat, w_uv).reshape(b, s, DSA_WIDTH)
    o_d = stick_breaking_attention(sq.reshape(b, s, SB_HEADS, HEAD_DIM),
                                   sk.reshape(b, s, SB_HEADS, HEAD_DIM),
                                   sv.reshape(b, s, SB_HEADS, HEAD_DIM)).reshape(b, s, SB_WIDTH)
    return jnp.concatenate([o_c, o_d], axis=-1) @ w_out

def conv_ffn(h, w_in, conv_w, conv_b, w_out):
    u = h @ w_in
    u = lax.conv_general_dilated(u, conv_w[:, None, :], window_strides=(1,),
                                 padding=[(CONV_WIDTH - 1, 0)],
                                 dimension_numbers=('NWC', 'WIO', 'NWC'),
                                 feature_group_count=u.shape[-1]) + conv_b
    g, v = jnp.split(u, 2, axis=-1)
    return (jax.nn.silu(g) * v) @ w_out

def second_inputs(seed: int = 0) -> dict:
    key = jax.random.key(seed)
    ks = jax.random.split(key, 24)
    f32 = jnp.float32

    def nrm(k, shape, scale):
        return jax.random.normal(k, shape, f32) * scale

    return {
        "x": nrm(ks[0], (BATCH, SEQ, D_MODEL), 1.0),
        "positions": jnp.broadcast_to(jnp.arange(SEQ, dtype=jnp.int32), (BATCH, SEQ)),
        "attn_norm": 1.0 + nrm(ks[1], (DEPTH_2, D_MODEL), 0.02),
        "ffn_norm": 1.0 + nrm(ks[2], (DEPTH_2, D_MODEL), 0.02),
        "final_norm": 1.0 + nrm(ks[3], (D_MODEL,), 0.02),
        "ev_w_in": nrm(ks[4], (N_EVEN, D_MODEL, EVEN_IN), D_MODEL ** -0.5),
        "ev_fgate_b": FOX_FGATE_BIAS + nrm(ks[5], (N_EVEN, FOX_HEADS), 0.1),
        "ev_lambda_q1": nrm(ks[6], (N_EVEN, HEAD_DIM), 0.1),
        "ev_lambda_k1": nrm(ks[7], (N_EVEN, HEAD_DIM), 0.1),
        "ev_lambda_q2": nrm(ks[8], (N_EVEN, HEAD_DIM), 0.1),
        "ev_lambda_k2": nrm(ks[9], (N_EVEN, HEAD_DIM), 0.1),
        "ev_subln": 1.0 + nrm(ks[10], (N_EVEN, DIFF_V_DIM), 0.02),
        "ev_w_out": nrm(ks[11], (N_EVEN, D_MODEL, D_MODEL), D_MODEL ** -0.5),
        "od_w_in": nrm(ks[12], (N_ODD, D_MODEL, ODD_IN), D_MODEL ** -0.5),
        "od_kv_norm": 1.0 + nrm(ks[13], (N_ODD, DSA_KV_RANK), 0.02),
        "od_w_uk": nrm(ks[14], (N_ODD, DSA_KV_RANK, DSA_HEADS, DSA_NOPE), DSA_KV_RANK ** -0.5),
        "od_w_uv": nrm(ks[15], (N_ODD, DSA_KV_RANK, DSA_HEADS, HEAD_DIM), DSA_KV_RANK ** -0.5),
        "od_w_out": nrm(ks[16], (N_ODD, D_MODEL, D_MODEL), D_MODEL ** -0.5),
        "ffn_w_in": nrm(ks[17], (DEPTH_2, D_MODEL, 2 * D_FF_2), D_MODEL ** -0.5),
        "ffn_conv_w": nrm(ks[18], (DEPTH_2, CONV_WIDTH, 2 * D_FF_2), CONV_WIDTH ** -0.5),
        "ffn_conv_b": nrm(ks[19], (DEPTH_2, 2 * D_FF_2), 0.02),
        "ffn_w_out": nrm(ks[20], (DEPTH_2, D_FF_2, D_MODEL), D_FF_2 ** -0.5),
    }

def second_block(x, positions, attn_norm, ffn_norm, final_norm,
              ev_w_in, ev_fgate_b, ev_lambda_q1, ev_lambda_k1, ev_lambda_q2, ev_lambda_k2,
              ev_subln, ev_w_out,
              od_w_in, od_kv_norm, od_w_uk, od_w_uv, od_w_out,
              ffn_w_in, ffn_conv_w, ffn_conv_b, ffn_w_out):
    cos, sin = rope_tables(positions)
    top_k = min(IDX_TOPK_MAX, x.shape[1] // 4)
    for layer in range(DEPTH_2):
        j = layer // 2
        h = rms_norm_2(x, attn_norm[layer])
        if layer % 2 == 0:
            x = x + even_mixer(h, cos, sin, ev_w_in[j], ev_fgate_b[j],
                               ev_lambda_q1[j], ev_lambda_k1[j], ev_lambda_q2[j], ev_lambda_k2[j],
                               ev_subln[j], ev_w_out[j], layer)
        else:
            x = x + odd_mixer(h, cos, sin, od_w_in[j], od_kv_norm[j], od_w_uk[j], od_w_uv[j],
                              od_w_out[j], top_k)
        h = rms_norm_2(x, ffn_norm[layer])
        x = x + conv_ffn(h, ffn_w_in[layer], ffn_conv_w[layer], ffn_conv_b[layer], ffn_w_out[layer])
    return rms_norm_2(x, final_norm)


def setup_inputs(seed=0):
    out = dict(first_inputs(seed))
    for name, value in second_inputs(seed + 1).items():
        if name != "x":
            out[name + "_2"] = value
    return out


def reference(
    x, norm_mix_pre, norm_mix_post, norm_ffn_pre, norm_ffn_post, w_in, rel_bias, sinks,
    rwkv_shift_mix, w0, w_decay_up, a0, w_iclr_up, w_gate_up, k_k, k_a, r_k, ln_x_g, ln_x_b,
    w_out, w_ffn_up, conv_w, conv_b, w_ffn_down, positions_2, attn_norm_2, ffn_norm_2,
    final_norm_2, ev_w_in_2, ev_fgate_b_2, ev_lambda_q1_2, ev_lambda_k1_2, ev_lambda_q2_2,
    ev_lambda_k2_2, ev_subln_2, ev_w_out_2, od_w_in_2, od_kv_norm_2, od_w_uk_2, od_w_uv_2,
    od_w_out_2, ffn_w_in_2, ffn_conv_w_2, ffn_conv_b_2, ffn_w_out_2,
):
    x = first_block(
        x, norm_mix_pre, norm_mix_post, norm_ffn_pre, norm_ffn_post, w_in, rel_bias, sinks,
        rwkv_shift_mix, w0, w_decay_up, a0, w_iclr_up, w_gate_up, k_k, k_a, r_k, ln_x_g, ln_x_b,
        w_out, w_ffn_up, conv_w, conv_b, w_ffn_down,
    )
    return second_block(
        x, positions_2, attn_norm_2, ffn_norm_2, final_norm_2, ev_w_in_2, ev_fgate_b_2,
        ev_lambda_q1_2, ev_lambda_k1_2, ev_lambda_q2_2, ev_lambda_k2_2, ev_subln_2, ev_w_out_2,
        od_w_in_2, od_kv_norm_2, od_w_uk_2, od_w_uv_2, od_w_out_2, ffn_w_in_2, ffn_conv_w_2,
        ffn_conv_b_2, ffn_w_out_2,
    )


_drawn_inputs = setup_inputs


def setup_inputs(seed=0):
    import zlib

    import numpy as np

    out = dict(_drawn_inputs(seed))
    spreads = {}
    factors = {'norm_mix_post': 2.691,
     'norm_ffn_pre': 2.943,
     'norm_ffn_post': 3.988,
     'sinks': 4.297,
     'ln_x_g': 3.039,
     'attn_norm_2': 3.798,
     'ffn_norm_2': 4.288,
     'final_norm_2': 2.848,
     'ev_fgate_b_2': 5.496,
     'ev_lambda_q1_2': 3.653,
     'ev_lambda_k1_2': 2.684,
     'ev_subln_2': 7.25,
     'od_kv_norm_2': 8.0,
     'ffn_conv_b_2': 4.213}
    for name, (base, spread) in spreads.items():
        noise = np.random.default_rng([zlib.crc32(name.encode()), seed]).standard_normal(out[name].shape)
        drawn = base * np.exp(spread * noise) if base else spread * noise
        out[name] = __import__('jax').numpy.asarray(drawn.astype(out[name].dtype))
    for name, factor in factors.items():
        out[name] = (out[name] * factor).astype(out[name].dtype)
    return out
```

```python
from contextlib import ExitStack, contextmanager
import math

import numpy as np
import concourse.bass as bass
from concourse import mybir

ALU = mybir.AluOpType
ACT = mybir.ActivationFunctionType
AX = mybir.AxisListType
F32 = mybir.dt.float32
F32R = mybir.dt.float32r

P = 128
D = 1024
KD = D // P
S = 512
NT = S // P
HD = 64
NH = 8
C = 64
NCH = S // C
LEVELS = int(math.log2(C))
FF1, FF2 = 4096, 2816
TOPK = 128
ROT = 16
NEG = -1e30
BUCKETS, WINDOW = 32, 128
RLEN = 384
EPS = 1e-6
GN_EPS = 64e-5
EHALF = math.exp(-0.5)

CST = {}
_at = 0
for _name, _w in (("ident", P), ("ones", P), ("pair", P), ("swap", P), ("level", P * LEVELS),
                  ("before", P), ("upto", P), ("future", P), ("past_t", P), ("after_t", P),
                  ("inside", S), ("freq", 2), ("onehot", RLEN)):
    CST[_name] = (_at, _at + _w)
    _at += _w
CST_W = _at


def t5_bucket(n):
    exact = BUCKETS // 2
    if n < exact:
        return n
    f = np.float32
    large = exact + int(f(np.log(f(n) / f(exact))) / f(math.log(P / exact)) * f(BUCKETS - exact))
    return min(large, BUCKETS - 1)


def constants():
    c = np.zeros((P, CST_W), np.float32)

    def put(name, a):
        lo, hi = CST[name]
        c[:a.shape[0], lo:hi] = a

    i = np.arange(P)
    row, col = i[:, None], i[None, :]
    same = row // C == col // C
    put("ident", np.eye(P))
    put("ones", np.ones((P, P)))
    put("pair", row // HD == col // HD)
    half = ROT // 2
    swap = np.zeros((P, P))
    for m in range(P):
        if m % HD < ROT:
            swap[m - m % HD + (m % HD + half) % ROT, m] = 1
    put("swap", swap)
    put("level", np.concatenate(
        [(row >> l + 1 == col >> l + 1) & (row >> l & 1 == 1) & (col >> l & 1 == 0) for l in range(LEVELS)], 1))
    put("before", same & (row < col))
    put("upto", same & (row <= col))
    put("future", np.where(col > row, NEG, 0))
    put("past_t", row < col)
    put("after_t", row >= col)
    put("inside", np.tile(np.arange(S) % C != 0, (P, 1)))
    inv = np.float32(500000.0) ** (-np.arange(0, ROT, 2, dtype=np.float32) / np.float32(ROT))
    f = np.zeros((P, 2), np.float32)
    for m in range(P):
        if m % HD < ROT:
            f[m] = inv[m % HD % half], (-1 if m % HD < half else 1)
    put("freq", f)
    hot = np.zeros((BUCKETS + 1, RLEN), np.float32)
    for x in range(RLEN):
        n = 2 * P - 1 - x
        if 0 <= n < WINDOW:
            hot[t5_bucket(n), x] = 1
        else:
            hot[BUCKETS, x] = NEG
    put("onehot", hot)
    return c


class Signal:

    def __init__(self, handle):
        self.h, self.n = handle, 0

    def by(self, ins):
        ins.then_inc(self.h, 1)
        self.n += 1
        return ins


class Chain:

    def __init__(self, eng, signal, turn=None):
        self.eng, self.s, self.turn = eng, signal, turn

    def __call__(self, ins):
        self.s.by(ins)
        self.eng.wait_ge(self.s.h, self.s.n if self.turn is None else self.turn + self.s.n)


def program(nc, a, out):
    whole = ExitStack()
    with whole:
        _program(nc, a, out, whole)


def _program(nc, a, out, whole):
    names = [0]

    def sb(ctx, name, shape, dt=F32):
        names[0] += 1
        return ctx.enter_context(nc.sbuf_tensor(f"{name}_{names[0]}", shape, dt))

    here, stale, clear = [], [], []

    def sig(name, kept=False):
        names[0] += 1
        h = clear.pop() if clear and not kept else whole.enter_context(nc.semaphore(f"{name}_{names[0]}"))
        if not kept:
            here.append(h)
        return Signal(h)

    @contextmanager
    def stage(params=None):
        with nc.Block() as block:
            yield block
            old = list(stale)

            @block.gpsimd
            def _(pool):
                for h in old:
                    pool.sem_clear(h)
                if params:
                    params(pool)
        clear.extend(stale)
        stale[:] = here
        here.clear()

    banks = whole.enter_context(nc.psum_tensor("banks", [P, 8, 512], F32))
    bank = [banks[:, i, :] for i in range(8)]

    scratch = nc.dram_tensor("scratch", (NH, P, RLEN), F32, kind="Internal").ap()
    xT = sb(whole, "xT", [P, KD, S])
    cst = sb(whole, "cst", [P, 3 * P])
    ident, ones, pair = (cst[:, i * P:(i + 1) * P] for i in range(3))
    NROW = 116
    pcol = sb(whole, "pcol", [P, NROW])
    conv1 = sb(whole, "conv1", [P, 4, 2 * FF1 // P])
    conv2 = [sb(whole, f"conv2{i}", [P, 4, 2 * FF2 // P]) for i in range(2)]

    vec, rows_of = {}, []
    at = 0
    for name, ap in (("norm_mix_pre", a["norm_mix_pre"]), ("norm_mix_post", a["norm_mix_post"]),
                     ("norm_ffn_pre", a["norm_ffn_pre"]), ("norm_ffn_post", a["norm_ffn_post"]),
                     ("mix", a["rwkv_shift_mix"]), ("w0", a["w0"]), ("a0", a["a0"]), ("k_k", a["k_k"]),
                     ("k_a", a["k_a"]), ("r_k", a["r_k"].rearrange("a h d -> a (h d)")),
                     ("ln_g", a["ln_x_g"]), ("ln_b", a["ln_x_b"]),
                     ("attn_norm", a["attn_norm_2"].rearrange("(o l) d -> o (l d)", o=1)),
                     ("ffn_norm", a["ffn_norm_2"].rearrange("(o l) d -> o (l d)", o=1)),
                     ("final_norm", a["final_norm_2"].rearrange("(o d) -> o d", o=1)),
                     ("subln", a["ev_subln_2"]), ("kv_norm", a["od_kv_norm_2"])):
        n = ap.shape[1] // P
        vec[name] = at
        rows_of.append((at, n, ap.rearrange("o (m p) -> (o m) p", p=P)))
        at += n
    assert at == NROW, at

    def col(name, m=0):
        return pcol[:, vec[name] + m:vec[name] + m + 1]

    RAW, CUT = 4, 2
    raw = [sb(whole, f"raw{i}", [P, KD, P]) for i in range(RAW)]
    whi = [sb(whole, f"whi{i}", [P, KD, P], F32R) for i in range(CUT)]
    wlo = [sb(whole, f"wlo{i}", [P, KD, P], F32R) for i in range(CUT)]
    loaded = [sig(f"w_loaded{i}", True) for i in range(RAW)]
    w_hi, w_lo, w_used = (sig(n, True) for n in ("w_hi", "w_lo", "w_used"))

    def rows(w, r0, nr, c0, nc_=P):
        return w[r0:r0 + nr * P, bass.ds(c0, nc_)].rearrange("(k p) n -> p k n", p=P)

    def tile_of(w, c0, r0=0, nr=KD):
        return lambda slot: [(slot[:, 0:nr, :], rows(w, r0, nr, c0))]

    def twice(w, c0):
        return lambda slot: [(slot[:, :, 0:HD], rows(w, 0, KD, c0, HD)), (slot[:, :, HD:P], rows(w, 0, KD, c0, HD))]

    w1, wo1 = a["w_in"][0], a["w_out"][0]
    wu1, wd1 = a["w_ffn_up"][0], a["w_ffn_down"][0]
    we, woe = a["ev_w_in_2"][0], a["ev_w_out_2"][0]
    wd, wod = a["od_w_in_2"][0], a["od_w_out_2"][0]
    wu2, wd2 = a["ffn_w_in_2"], a["ffn_w_out_2"]

    in1 = [tile_of(w1, 128 * m) for m in range(4)] + [twice(w1, 512), twice(w1, 576), tile_of(w1, 640)] \
        + [tile_of(w1, 768 + 128 * m) for m in range(14)]
    EV = [0, 512, 1024, 1536, 1544, 2056, 2568]
    in_ev = [tile_of(we, 128 * m) for m in range(12)] + [tile_of(we, 1536)] \
        + [tile_of(we, 1544 + 128 * m) for m in range(12)]
    in_od = [tile_of(wd, 128 * m) for m in range(4)] + [tile_of(wd, 512), twice(wd, 640)] \
        + [tile_of(wd, 656 + 128 * m) for m in range(2)] + [tile_of(wd, 912), twice(wd, 916)] \
        + [tile_of(wd, 980 + 128 * m) for m in range(12)]

    def up_slots(w, ff, first, pairs):
        return [tile_of(w, o + 128 * (first + m)) for m in range(pairs) for o in (0, ff)]

    def down_slots(w, first, parts):
        return [tile_of(w, 128 * m, 128 * (first + k), n) for m in range(KD) for k, n in parts]

    PARTS1 = [(0, 8), (8, 8)]
    PARTS2 = [(0, 6), (6, 6), (12, 5), (17, 5)]
    plan = list(in1) + [tile_of(wo1, 128 * m) for m in range(8)]
    for ch in range(2):
        plan += up_slots(wu1, FF1, 16 * ch, 16) + down_slots(wd1, 16 * ch, PARTS1)
    for layer in range(2):
        plan += (in_ev, in_od)[layer] + [tile_of((woe, wod)[layer], 128 * m) for m in range(8)]
        plan += up_slots(wu2[layer], FF2, 0, 22) + down_slots(wd2[layer], 0, PARTS2)
    plan.append(tile_of(wo1, 0))
    state = {"s": 0}

    def load(sp, s):
        if s >= len(plan):
            return
        if s >= RAW:
            sp.wait_ge(w_lo.h, s - RAW + 1)
        for dst, src in plan[s](raw[s % RAW]):
            sp.dma_start(dst, src).then_inc(loaded[s % RAW].h, 16)

    arrived = {}
    for s_ in range(len(plan)):
        n_ = len(plan[s_](raw[s_ % RAW]))
        arrived[s_] = (arrived[s_ - RAW] if s_ >= RAW else 0) + 16 * n_

    def split_hi(act, s):
        act.wait_ge(loaded[s % RAW].h, arrived[s])
        if s >= CUT:
            act.wait_ge(w_used.h, s - CUT + 1)
        w_hi.by(act.activation(whi[s % CUT][:], raw[s % RAW][:], ACT.Copy))

    def split_lo(dve, s):
        dve.wait_ge(w_hi.h, s + 1)
        w_lo.by(dve.tensor_tensor(wlo[s % CUT][:], raw[s % RAW][:], whi[s % CUT][:].bitcast(F32), ALU.subtract))

    def three_passes(pe, acc, b, n, hi, lo, first, last):
        for k in range(n):
            pe.matmul(acc, whi[b][:, k, :], hi(k), start=first and k == 0, stop=False)
            pe.matmul(acc, whi[b][:, k, :], lo(k), start=False, stop=False)
            mm = pe.matmul(acc, wlo[b][:, k, :], hi(k), start=False, stop=last and k == n - 1)
        return mm

    act_chain, dve_chain = sig("act_chain", True), sig("dve_chain", True)

    def cst_dma(sp, dst, name, signal, rows_=P):
        lo, hi = CST[name]
        sp.dma_start(dst, a["cst"][0:rows_, lo:hi]).then_inc(signal.h, 16)

    def setup():
        with ExitStack() as ctx:
            xin = sb(ctx, "xin", [P, NT, D])
            prow = sb(ctx, "prow", [P, P])
            c1row = sb(ctx, "c1row", [2 * FF1 // P, 4, P])
            c2row = sb(ctx, "c2row", [2 * FF2 // P, 2, 4, P])
            s_x, s_p, turned, taken = sig("s_x"), sig("s_p", True), sig("turned"), sig("taken")

            def params(pool):
                for first, n, ap in rows_of:
                    pool.dma_start(prow[first:first + n, :], ap).then_inc(s_p.h, 16)
                for t in range(3):
                    pool.dma_start(c1row[:, t, :], a["conv_w"][0, t:t + 1, :].rearrange("o (m p) -> (o m) p", p=P)).then_inc(s_p.h, 16)
                pool.dma_start(c1row[:, 3, :], a["conv_b"][0:1, :].rearrange("o (m p) -> (o m) p", p=P)).then_inc(s_p.h, 16)
                for l in range(2):
                    for t in range(3):
                        pool.dma_start(c2row[:, l, t, :], a["ffn_conv_w_2"][l, t:t + 1, :].rearrange("o (m p) -> (o m) p", p=P)).then_inc(s_p.h, 16)
                    pool.dma_start(c2row[:, l, 3, :], a["ffn_conv_b_2"][l:l + 1, :].rearrange("o (m p) -> (o m) p", p=P)).then_inc(s_p.h, 16)
            block = ctx.enter_context(stage(params))

            @block.sync
            def _(sp):
                sp.dma_start(cst[:, :], a["cst"][:, 0:3 * P]).then_inc(s_x.h, 16)
                sp.dma_start(xin[:, :, :], a["x"][0].rearrange("(t p) d -> p t d", p=P)).then_inc(s_x.h, 16)
                for s in range(RAW):
                    load(sp, s)

            n_params = 16 * (len(rows_of) + 12)

            @block.tensor
            def _(pe):
                pe.wait_ge(s_x.h, 32)
                for k in range(KD):
                    for t in range(NT):
                        mm = pe.transpose(bank[k][:, t * P:(t + 1) * P], xin[:, t, k * P:(k + 1) * P], ident)
                    mm.then_inc(turned.h, 1)
                pe.wait_ge(s_p.h, n_params)
                pe.wait_ge(taken.h, 4)
                mm = pe.transpose(bank[0][:, 0:NROW], prow[0:NROW, :], ident[0:NROW, 0:NROW])
                mm.then_inc(turned.h, 1)
                n1, n2 = 2 * FF1 // P, 2 * FF2 // P
                for t in range(4):
                    mm = pe.transpose(bank[1][:, t * n1:(t + 1) * n1], c1row[:, t, :], ident[0:n1, 0:n1])
                mm.then_inc(turned.h, 1)
                for l in range(2):
                    for t in range(4):
                        mm = pe.transpose(bank[2 + l][:, t * n2:(t + 1) * n2], c2row[:, l, t, :], ident[0:n2, 0:n2])
                    mm.then_inc(turned.h, 1)

            @block.vector
            def _(dve):
                for k in range(KD):
                    dve.wait_ge(turned.h, k + 1)
                    dve.tensor_copy(xT[:, k, :], bank[k][:, :]).then_inc(taken.h, 1)
                n1, n2 = 2 * FF1 // P, 2 * FF2 // P
                dve.wait_ge(turned.h, KD + 1)
                dve.tensor_copy(pcol[:, :], bank[0][:, 0:NROW])
                dve.wait_ge(turned.h, KD + 2)
                dve.tensor_copy(conv1[:, :, :].rearrange("p t n -> p (t n)"), bank[1][:, 0:4 * n1])
                dve.wait_ge(turned.h, KD + 4)
                for l in range(2):
                    dve.tensor_copy(conv2[l][:, :, :].rearrange("p t n -> p (t n)"), bank[2 + l][:, 0:4 * n2])
                split_lo(dve, 0)

            @block.scalar
            def _(act):
                split_hi(act, 0)

    def norm(src, n, g, gname_m, width, eps, finish, groups=1, stat=None):
        stat = ones if stat is None else stat
        with ExitStack() as ctx:
            sq = sb(ctx, "sq", [P, n, S])
            ms = sb(ctx, "ms", [P, groups, S])
            rt = sb(ctx, "rt", [P, groups, S])
            rstd = sb(ctx, "rstd", [P, groups, S])
            squared, summed, meaned, rooted = sig("squared"), sig("summed"), sig("meaned"), sig("rooted")
            per = n // groups
            block = ctx.enter_context(stage())

            @block.sync
            def _(sp):
                pass

            @block.scalar
            def _(act):
                for k in range(n):
                    squared.by(act.activation(sq[:, k, :], src(k), ACT.Square))
                for q in range(groups):
                    act.wait_ge(meaned.h, q + 1)
                    rooted.by(act.activation(rt[:, q, :], ms[:, q, :], ACT.Sqrt))

            @block.tensor
            def _(pe):
                for k in range(n):
                    pe.wait_ge(squared.h, k + 1)
                    mm = pe.matmul(bank[k // per][:, :], stat, sq[:, k, :], start=k % per == 0, stop=k % per == per - 1)
                    if k % per == per - 1:
                        summed.by(mm)

            @block.vector
            def _(dve):
                chain = Chain(dve, dve_chain)
                for q in range(groups):
                    dve.wait_ge(summed.h, q + 1)
                    meaned.by(dve.tensor_scalar(ms[:, q, :], bank[q][:, :], 1.0 / width, eps, ALU.mult, ALU.add))
                for q in range(groups):
                    dve.wait_ge(rooted.h, q + 1)
                    chain(dve.reciprocal(rstd[:, q, :], rt[:, q, :]))
                for k in range(n):
                    finish(dve, chain, k, rstd[:, k // per, :])

    def norm_split(gname, hi, lo):
        with ExitStack() as ctx:
            h = sb(ctx, "h", [P, KD, S])

            def finish(dve, chain, k, rstd):
                chain(dve.scalar_tensor_tensor(h[:, k, :], xT[:, k, :], col(*gname(k)), rstd, ALU.mult, ALU.mult))
                chain(dve.tensor_copy(hi[:, k, :], h[:, k, :]))
                dve.tensor_tensor(lo[:, k, :], h[:, k, :], hi[:, k, :].bitcast(F32), ALU.subtract)
            norm(lambda k: xT[:, k, :], KD, None, None, D, EPS, finish)

    def split(src, n, hi, lo):
        with ExitStack() as ctx:
            upper = sig("upper")
            block = ctx.enter_context(stage())

            @block.scalar
            def _(act):
                for k in range(n):
                    upper.by(act.activation(hi[:, k, :], src(k), ACT.Copy))

            @block.vector
            def _(dve):
                for k in range(n):
                    dve.wait_ge(upper.h, k + 1)
                    dve.tensor_tensor(lo[:, k, :], src(k), hi[:, k, :].bitcast(F32), ALU.subtract)

    def project(n, hi, lo, put, post=None):
        s0 = state["s"]
        done, free = sig("done"), sig("free")
        with ExitStack() as ctx:
            block = ctx.enter_context(stage())

            @block.sync
            def _(sp):
                for m in range(n):
                    load(sp, s0 + RAW + m)

            @block.tensor
            def _(pe):
                for m in range(n):
                    s = s0 + m
                    pe.wait_ge(w_lo.h, s + 1)
                    if m >= 4:
                        pe.wait_ge(free.h, m - 3)
                    w_used.by(three_passes(pe, bank[m % 4][:, :], s % CUT, KD, lambda k: hi[:, k, :], lambda k: lo[:, k, :], True, True))

            @block.scalar
            def _(act):
                for m in range(n):
                    split_hi(act, s0 + m + 1)
                    if put:
                        act.wait_ge(w_used.h, s0 + m + 1)
                        free.by(put(act, m, bank[m % 4][:, :]))

            @block.vector
            def _(dve):
                chain = Chain(dve, dve_chain)
                for m in range(n):
                    split_lo(dve, s0 + m + 1)
                    if not put:
                        dve.wait_ge(w_used.h, s0 + m + 1)
                        free.by(post(dve, chain, m, bank[m % 4][:, :]))
                    elif post:
                        dve.wait_ge(free.h, m + 1)
                        post(dve, chain, m)
        state["s"] += n

    def ffn(w_up, ff, w_down, conv, first, pairs, parts, hi, lo, func, add, acc_to):
        with ExitStack() as ctx:
            ghi = sb(ctx, "ghi", [P, pairs, S], F32R)
            glo = sb(ctx, "glo", [P, pairs, S], F32R)
            with ExitStack() as up:
                cb = [sb(up, f"cb{j}", [P, S]) for j in range(4)]
                gate = [sb(up, f"gate{j}", [P, S]) for j in range(2)]
                gv = [sb(up, f"gv{j}", [P, S]) for j in range(2)]
                s0, turns = state["s"], pairs // 2
                sa = [s0 % RAW, s0 % CUT]
                tapped, conved, gated, products = sig("tapped"), sig("conved"), sig("gated"), sig("products")
                chain0 = dve_chain.n
                ff_tiles = ff // P
                half = [0, ff_tiles, 1, ff_tiles + 1]
                block = up.enter_context(stage())

                @block.sync
                def _(sp):
                    with sp.Fori(1, turns) as i:
                        for j in range(4):
                            sp.wait_ge(w_lo.h, i * 4 + (s0 + j - RAW + 1))
                            b = (s0 + j) % RAW
                            sp.dma_start(raw[b][:, :, :], rows(w_up, 0, KD, i * (2 * P) + P * (first + half[j])))\
                              .then_inc(loaded[b].h, 16)
                    for s in range(s0 + 4 * turns, s0 + 4 * turns + RAW):
                        load(sp, s)

                @block.tensor
                def _(pe):
                    def one(i, j, hold):
                        pe.wait_ge(w_lo.h, i * 4 + (s0 + j + 1))
                        if hold:
                            pe.wait_ge(conved.h, i * 4 + (j - 3))
                        three_passes(pe, bank[j][:, :], (s0 + j) % CUT, KD, lambda k: hi[:, k, :], lambda k: lo[:, k, :], True, True)\
                            .then_inc(w_used.h, 1)
                    for j in range(4):
                        one(0, j, False)
                    with pe.Fori(1, turns) as i:
                        for j in range(4):
                            one(i, j, True)

                @block.scalar
                def _(act):
                    def hi_of(i, j):
                        s = s0 + j
                        act.wait_ge(loaded[s % RAW].h, i * 16 + arrived[s])
                        act.wait_ge(w_used.h, i * 4 + (s - CUT + 1))
                        act.activation(whi[s % CUT][:], raw[s % RAW][:], ACT.Copy).then_inc(w_hi.h, 1)

                    def tap(i, j, hold):
                        act.wait_ge(w_used.h, i * 4 + (s0 + j + 1))
                        if hold:
                            act.wait_ge(products.h, i * 2 + (j // 2 - 1))
                        c = i * 2 + (first + half[j])
                        act.activation(cb[j][:, :], bank[j][:, :], ACT.Identity,
                                       scale=conv[:, 2, bass.ds(c, 1)], bias=conv[:, 3, bass.ds(c, 1)])\
                           .then_inc(tapped.h, 1)

                    def turn(i, hold):
                        for j in range(4):
                            hi_of(i, j + 1)
                            if j % 2 == 1:
                                act.wait_ge(conved.h, i * 4 + j)
                                act.activation(gate[j // 2][:, :], cb[j - 1][:, :], func).then_inc(gated.h, 1)
                            tap(i, j, hold)
                    turn(0, False)
                    with act.Fori(1, turns) as i:
                        turn(i, True)

                @block.vector
                def _(dve):
                    def turn(i, base):
                        chain = Chain(dve, dve_chain, base)
                        for j in range(4):
                            s = s0 + j + 1
                            dve.wait_ge(w_hi.h, i * 4 + (s + 1))
                            dve.tensor_tensor(wlo[s % CUT][:], raw[s % RAW][:], whi[s % CUT][:].bitcast(F32), ALU.subtract)\
                               .then_inc(w_lo.h, 1)
                            dve.wait_ge(tapped.h, i * 4 + (j + 1))
                            c = i * 2 + (first + half[j])
                            chain(dve.scalar_tensor_tensor(cb[j][:, 1:S], bank[j][:, 0:S - 1], conv[:, 1, bass.ds(c, 1)],
                                                           cb[j][:, 1:S], ALU.mult, ALU.add))
                            dve.scalar_tensor_tensor(cb[j][:, 2:S], bank[j][:, 0:S - 2], conv[:, 0, bass.ds(c, 1)],
                                                     cb[j][:, 2:S], ALU.mult, ALU.add).then_inc(conved.h, 1)
                            if j % 2 == 1:
                                q = j // 2
                                dve.wait_ge(conved.h, i * 4 + (j + 1))
                                dve.wait_ge(gated.h, i * 2 + (q + 1))
                                dve.tensor_tensor(gv[q][:, :], gate[q][:, :], cb[j][:, :], ALU.mult).then_inc(products.h, 1)
                                dve.wait_ge(products.h, i * 2 + (q + 1))
                                chain(dve.tensor_copy(ghi[:, i * 2 + q, :], gv[q][:, :]))
                                chain(dve.tensor_tensor(glo[:, i * 2 + q, :], gv[q][:, :], ghi[:, i * 2 + q, :].bitcast(F32), ALU.subtract))
                    turn(0, 0)
                    per = dve_chain.n - chain0
                    dve_chain.n = chain0
                    with dve.Fori(1, turns) as i:
                        turn(i, i * per)
                    dve_chain.n = chain0 + per * turns
                used = 4 * turns
                w_used.n += used
                w_hi.n += used
                w_lo.n += used
                state["s"] += used

            s0 = state["s"]
            mts = 4 // len(parts)
            slots = [(mt, k0, n) for mt in range(mts) for k0, n in parts]
            turns = KD // mts
            taken = sig("taken")
            with ExitStack() as dn:
                block = dn.enter_context(stage())

                @block.sync
                def _(sp):
                    with sp.Fori(1, turns) as i:
                        for j, (mt, k0, n) in enumerate(slots):
                            sp.wait_ge(w_lo.h, i * 4 + (s0 + j - RAW + 1))
                            b = (s0 + j) % RAW
                            sp.dma_start(raw[b][:, 0:n, :], rows(w_down, P * (first + k0), n, i * (mts * P) + P * mt))\
                              .then_inc(loaded[b].h, 16)
                    for s in range(s0 + 4 * turns, s0 + 4 * turns + RAW):
                        load(sp, s)

                @block.tensor
                def _(pe):
                    def turn(i, hold):
                        for j, (mt, k0, n) in enumerate(slots):
                            pe.wait_ge(w_lo.h, i * 4 + (s0 + j + 1))
                            if hold and k0 == 0:
                                pe.wait_ge(taken.h, (i - 1) * mts + (mt + 1))
                            three_passes(pe, bank[4 + mt][:, :], (s0 + j) % CUT, n, lambda k: ghi[:, k0 + k, :],
                                         lambda k: glo[:, k0 + k, :], k0 == 0, k0 + n == pairs).then_inc(w_used.h, 1)
                    turn(0, False)
                    with pe.Fori(1, turns) as i:
                        turn(i, True)

                @block.scalar
                def _(act):
                    def turn(i, last=False):
                        for j in range(4):
                            s = s0 + j + 1
                            n = KD if last and j == 3 else (slots * 2)[j + 1][2]
                            act.wait_ge(loaded[s % RAW].h, i * 16 + (arrived[s] if not last or j < 3 else arrived[s0 + 4 * turns] - 16 * (turns - 1)))
                            act.wait_ge(w_used.h, i * 4 + (s - CUT + 1))
                            act.activation(whi[s % CUT][:, 0:n, :], raw[s % RAW][:, 0:n, :], ACT.Copy).then_inc(w_hi.h, 1)
                    with act.Fori(0, turns - 1) as i:
                        turn(i)
                    turn(turns - 1, True)

                @block.vector
                def _(dve):
                    def turn(i, last=False):
                        for j, (mt, k0, n) in enumerate(slots):
                            s = s0 + j + 1
                            nn = KD if last and j == 3 else (slots * 2)[j + 1][2]
                            dve.wait_ge(w_hi.h, i * 4 + (s + 1))
                            dve.tensor_tensor(wlo[s % CUT][:, 0:nn, :], raw[s % RAW][:, 0:nn, :], whi[s % CUT][:, 0:nn, :].bitcast(F32), ALU.subtract)\
                               .then_inc(w_lo.h, 1)
                            if k0 + n == pairs:
                                dve.wait_ge(w_used.h, i * 4 + (s0 + j + 1))
                                m = i * mts + mt
                                if add:
                                    dve.tensor_tensor(acc_to[:, m, :], bank[4 + mt][:, :], acc_to[:, m, :], ALU.add).then_inc(taken.h, 1)
                                else:
                                    dve.tensor_copy(acc_to[:, m, :], bank[4 + mt][:, :]).then_inc(taken.h, 1)
                    with dve.Fori(0, turns - 1) as i:
                        turn(i)
                    turn(turns - 1, True)
                used = 4 * turns
                w_used.n += used
                w_hi.n += used
                w_lo.n += used
                state["s"] += used

    def attend(units, dst_of, width_v=P, sink=None, lam=None):
        U, G = len(units), len(units[0][0])
        scored, ready, exped, normed, flipped, ptaken, weighed, otaken = (
            sig(n) for n in ("scored", "ready", "exped", "normed", "flipped", "ptaken", "weighed", "otaken"))
        with ExitStack() as ctx:
            sm = [sb(ctx, f"sm{i}", [P, G, S]) for i in range(2)]
            ex = [sb(ctx, f"ex{i}", [P, G, S]) for i in range(3)]
            pt = [sb(ctx, f"pt{i}", [P, S]) for i in range(2)]
            mx = [sb(ctx, f"mx{i}", [P, 6 * G]) for i in range(3)]
            block = ctx.enter_context(stage())

            def f(i, what, g=None):
                o = ("max", "neg", "sum", "sink", "den", "inv").index(what) * G
                return mx[i % 3][:, o:o + G] if g is None else mx[i % 3][:, o + g:o + g + 1]

            @block.tensor
            def _(pe):
                for i in range(U + 3):
                    if i < U:
                        maps, w = units[i][0], units[i][1]
                        if i >= 2:
                            pe.wait_ge(ready.h, i - 1)
                        for g, pairs in enumerate(maps):
                            for n, (q, k) in enumerate(pairs):
                                mm = pe.matmul(bank[i % 2 * 2 + g][:, 0:w], q, k, start=n == 0, stop=n == len(pairs) - 1)
                        mm.then_inc(scored.h, 1)
                    u = i - 2
                    if 0 <= u < U:
                        pe.wait_ge(normed.h, u + 1)
                        if u >= 2:
                            pe.wait_ge(ptaken.h, u - 1)
                        for b in range(units[u][1] // P):
                            mm = pe.transpose(bank[4 + u % 2][:, b * P:(b + 1) * P], ex[u % 3][:, 0, b * P:(b + 1) * P], ident)
                        mm.then_inc(flipped.h, 1)
                    u = i - 3
                    if 0 <= u < U:
                        _, w, _, values, (r0, r1) = units[u]
                        pe.wait_ge(ptaken.h, u + 1)
                        if u >= 2:
                            pe.wait_ge(otaken.h, u - 1)
                        for b, v in enumerate(values):
                            mm = pe.matmul(bank[6 + u % 2][r0:r1, 0:P], v, pt[u % 2][:, b * P:(b + 1) * P],
                                           start=b == 0, stop=b == len(values) - 1)
                        mm.then_inc(weighed.h, 1)

            @block.vector
            def _(dve):
                chain = Chain(dve, dve_chain)
                for i in range(U + 1):
                    if i < U:
                        _, w, bias, _, _ = units[i]
                        dve.wait_ge(scored.h, i + 1)
                        if i >= 2:
                            dve.wait_ge(exped.h, i - 1)
                        s = sm[i % 2]
                        for g in range(G):
                            ins = dve.scalar_tensor_tensor(s[:, g, 0:w], bank[i % 2 * 2 + g][:, 0:w], HD ** -0.5, bias[0],
                                                           ALU.mult, ALU.add)
                        chain(ins)
                        if bias[1] is not None:
                            chain(dve.tensor_tensor(s[:, 0, w - P:w], s[:, 0, w - P:w], bias[1], ALU.add))
                        chain(dve.tensor_reduce(f(i, "max"), s[:, :, 0:w], AX.X, ALU.max))
                        if sink is None:
                            ready.by(dve.tensor_scalar(f(i, "neg"), f(i, "max"), -1.0, None, ALU.mult))
                        else:
                            ready.by(dve.tensor_scalar(f(i, "neg"), f(i, "max"), sink(i), -1.0, ALU.max, ALU.mult))
                    u = i - 1
                    if 0 <= u < U:
                        w = units[u][1]
                        dve.wait_ge(exped.h, u + 1)
                        den = f(u, "sum")
                        if sink is not None:
                            chain(dve.tensor_tensor(f(u, "den"), f(u, "sum"), f(u, "sink"), ALU.add))
                            den = f(u, "den")
                        chain(dve.reciprocal(f(u, "inv"), den))
                        e = ex[u % 3]
                        if G == 1:
                            normed.by(dve.tensor_scalar(e[:, 0, 0:w], e[:, 0, 0:w], f(u, "inv"), None, ALU.mult))
                        else:
                            chain(dve.tensor_scalar(e[:, 0, 0:w], e[:, 0, 0:w], f(u, "inv", 0), None, ALU.mult))
                            chain(dve.tensor_scalar(f(u, "den", 1), f(u, "inv", 1), lam, -1.0, ALU.mult, ALU.mult))
                            normed.by(dve.scalar_tensor_tensor(e[:, 0, 0:w], e[:, 1, 0:w], f(u, "den", 1), e[:, 0, 0:w],
                                                               ALU.mult, ALU.add))

            @block.scalar
            def _(act):
                for i in range(U + 3):
                    if i < U:
                        w = units[i][1]
                        act.wait_ge(ready.h, i + 1)
                        if i >= 3:
                            act.wait_ge(flipped.h, i - 2)
                        if sink is not None:
                            act.activation(f(i, "sink"), sink(i), ACT.Exp, bias=f(i, "neg"))
                        for g in range(G):
                            ins = act.activation(ex[i % 3][:, g, 0:w], sm[i % 2][:, g, 0:w], ACT.Exp, bias=f(i, "neg", g),
                                                 accum_out=f(i, "sum", g))
                        exped.by(ins)
                    u = i - 2
                    if 0 <= u < U:
                        w = units[u][1]
                        act.wait_ge(flipped.h, u + 1)
                        if u >= 2:
                            act.wait_ge(weighed.h, u - 1)
                        ptaken.by(act.activation(pt[u % 2][:, 0:w], bank[4 + u % 2][:, 0:w], ACT.Copy))
                    u = i - 3
                    if 0 <= u < U:
                        r0, r1 = units[u][4]
                        act.wait_ge(weighed.h, u + 1)
                        otaken.by(act.activation(dst_of(u), bank[6 + u % 2][r0:r1, 0:P], ACT.Copy))

    def turn(pairs):
        flipped, taken = sig("flipped"), sig("taken")
        with ExitStack() as ctx:
            block = ctx.enter_context(stage())

            @block.tensor
            def _(pe):
                for n, (_, srcs) in enumerate(pairs):
                    if n >= 8:
                        pe.wait_ge(taken.h, n - 7)
                    for q, src in enumerate(srcs):
                        mm = pe.transpose(bank[n % 8][:, q * P:(q + 1) * P], src, ident)
                    mm.then_inc(flipped.h, 1)

            @block.vector
            def _(dve):
                for n, (dst, srcs) in enumerate(pairs):
                    dve.wait_ge(flipped.h, n + 1)
                    dve.tensor_copy(dst, bank[n % 8][:, 0:len(srcs) * P].rearrange("p (q c) -> p q c", q=len(srcs))).then_inc(taken.h, 1)

    def rwkv(r, k, v, zt, zg, oT, outer):
        with ExitStack() as ctx:
            cs, aa, ep, em, kk, tmp = (sb(ctx, n, [P, 4, S]) for n in ("cs", "aa", "ep", "em", "kk", "tmp"))
            lora = sb(ctx, "lora", [P, S])
            wgu = sb(ctx, "wgu", [P, S])
            level = sb(ctx, "level", [P, LEVELS, P])
            before, upto = sb(ctx, "before", [P, P]), sb(ctx, "upto", [P, P])
            pc = sb(ctx, "pc", [P, 4, NCH])
            with ExitStack() as c1:
                inside = sb(c1, "inside", [P, S])
                s_in, pre, sg1, sg2, scan, expd, sq, sm_, mxd, rtd, pr, bsum = (
                    sig(n) for n in ("s_in", "pre", "sg1", "sg2", "scan", "expd", "sq", "sm_", "mxd", "rtd", "pr", "bsum"))
                block = c1.enter_context(stage())

                @block.sync
                def _(sp):
                    sp.dma_start(lora[0:HD, :], a["w_decay_up"][0]).then_inc(s_in.h, 16)
                    sp.dma_start(lora[HD:P, :], a["w_iclr_up"][0]).then_inc(s_in.h, 16)
                    sp.dma_start(wgu[:, :], a["w_gate_up"][0]).then_inc(s_in.h, 16)
                    cst_dma(sp, level[:, :, :].rearrange("p l n -> p (l n)"), "level", s_in)
                    cst_dma(sp, before[:, :], "before", s_in)
                    cst_dma(sp, upto[:, :], "upto", s_in)
                    cst_dma(sp, inside[:, :], "inside", s_in)

                @block.scalar
                def _(act):
                    act.activation(zt[0:HD, :], zt[0:HD, :], ACT.Tanh).then_inc(sg1.h, 1)
                    act.activation(zg[:, :], zg[:, :], ACT.Sigmoid)
                    for m in range(8):
                        act.wait_ge(pre.h, m + 1)
                        dst, b = (cs, "w0") if m < 4 else (aa, "a0")
                        act.activation(dst[:, m % 4, :], bank[m][:, :], ACT.Sigmoid, bias=col(b, m % 4)).then_inc(sg2.h, 1)
                    for m in range(4):
                        act.wait_ge(scan.h, m + 1)
                        act.activation(ep[:, m, :], tmp[:, m, :], ACT.Exp, scale=-EHALF).then_inc(expd.h, 1)
                        act.activation(em[:, m, :], tmp[:, m, :], ACT.Exp, scale=EHALF).then_inc(expd.h, 1)
                    for m in range(4):
                        act.wait_ge(mxd.h, m + 1)
                        act.activation(cs[:, m, :], cs[:, m, :], ACT.Sqrt).then_inc(rtd.h, 1)

                @block.tensor
                def _(pe):
                    pe.wait_ge(s_in.h, 16 * 7)
                    pe.wait_ge(sg1.h, 1)
                    for m in range(8):
                        lo_, hi_ = (0, HD) if m < 4 else (HD, P)
                        pe.matmul(bank[m][:, :], lora[lo_:hi_, (m % 4) * P:(m % 4 + 1) * P], zt[lo_:hi_, :],
                                  start=True, stop=True).then_inc(pre.h, 1)
                    for m in range(4):
                        pe.wait_ge(sq.h, m + 1)
                        pe.wait_ge(sg2.h, m + 1)
                        pe.matmul(bank[m][:, :], pair, cs[:, m, :], start=True, stop=True).then_inc(sm_.h, 1)
                    for m in range(4):
                        pe.wait_ge(pr.h, m + 1)
                        pe.wait_ge(sg2.h, 4 + m + 1)
                        pe.matmul(bank[4 + m][:, :], pair, cs[:, m, :], start=True, stop=True).then_inc(bsum.h, 1)

                @block.vector
                def _(dve):
                    chain = Chain(dve, dve_chain)
                    dve.wait_ge(s_in.h, 16 * 7)
                    for m in range(4):
                        chain(dve.tensor_scalar(kk[:, m, :], k[:, m, :], col("k_k", m), None, ALU.mult))
                    for m in range(4):
                        dve.wait_ge(sg2.h, m + 1)
                        scan.by(dve.tensor_tensor_scan(tmp[:, m, :], inside[:, :], cs[:, m, :], 0.0, ALU.mult, ALU.add))
                    dve.wait_ge(scan.h, 4)
                    for m in range(4):
                        sq.by(dve.tensor_tensor(cs[:, m, :], kk[:, m, :], kk[:, m, :], ALU.mult))
                    for m in range(4):
                        dve.wait_ge(sm_.h, m + 1)
                        mxd.by(dve.tensor_scalar(cs[:, m, :], bank[m][:, :], 1e-24, None, ALU.max))
                    dve.wait_ge(expd.h, 8)
                    for m in range(4):
                        dve.wait_ge(rtd.h, m + 1)
                        chain(dve.reciprocal(tmp[:, m, :], cs[:, m, :]))
                        chain(dve.tensor_tensor(kk[:, m, :], kk[:, m, :], tmp[:, m, :], ALU.mult))
                    for m in range(4):
                        dve.wait_ge(sg2.h, 4 + m + 1)
                        chain(dve.tensor_scalar(tmp[:, m, :], aa[:, m, :], -1.0, col("k_a", m), ALU.add, ALU.mult))
                        chain(dve.scalar_tensor_tensor(k[:, m, :], tmp[:, m, :], 1.0, k[:, m, :], ALU.add, ALU.mult))
                        pr.by(dve.scalar_tensor_tensor(cs[:, m, :], r[:, m, :], col("r_k", m), k[:, m, :], ALU.mult, ALU.mult))
                    for m in range(4):
                        chain(dve.tensor_tensor(aa[:, m, :], aa[:, m, :], kk[:, m, :], ALU.mult))
                    dve.wait_ge(pr.h, 4)
                    chain(dve.tensor_tensor(r[:, :, :], r[:, :, :], ep[:, :, :], ALU.mult))
                    chain(dve.tensor_tensor(k[:, :, :], k[:, :, :], em[:, :, :], ALU.mult))
                    chain(dve.tensor_tensor(aa[:, :, :], aa[:, :, :], em[:, :, :], ALU.mult))
                    for m in range(4):
                        kc = kk[:, m, :].rearrange("p (c t) -> p c t", t=C)
                        ec = ep[:, m, :].rearrange("p (c t) -> p c t", t=C)
                        chain(dve.tensor_scalar(kk[:, m, :], kk[:, m, :], -1.0, None, ALU.mult))
                        chain(dve.tensor_tensor(kc[:, :, 1:C], kc[:, :, 1:C], ec[:, :, 0:C - 1], ALU.mult))
                        chain(dve.tensor_copy(pc[:, m, :], ec[:, :, C - 1]))
                    for m in range(4):
                        dve.wait_ge(bsum.h, m + 1)
                        chain(dve.tensor_tensor(cs[:, m, :], bank[4 + m][:, :], v[:, m, :], ALU.mult))
            vt, kt, bt, at_ = tmp, ep, em, v
            turn([(dst[:, t, :].rearrange("p (q c) -> p q c", q=4), [src[:, m, t * P:(t + 1) * P] for m in range(4)])
                  for dst, src in ((vt, v), (kt, k), (bt, aa)) for t in range(NT)])
            turn([(at_[:, t, :].rearrange("p (q c) -> p q c", q=4), [kk[:, m, t * P:(t + 1) * P] for m in range(4)])
                  for t in range(NT)])
            wt = sb(ctx, "wt", [P, NT, 4, P])
            u0 = sb(ctx, "u0", [P, NT, 2, 4 * HD])
            z = sb(ctx, "z", [P, NCH, 4, HD])

            def uat(h):
                return slice(h % 2 * 4 * HD + h // 2 * HD, h % 2 * 4 * HD + h // 2 * HD + HD)

            def u_of(h, t, r0=0, r1=P):
                return u0[r0:r1, t, h % 2, h // 2 * HD:(h // 2 + 1) * HD]

            def head(x, h, t):
                return x[h % 2 * HD:h % 2 * HD + HD, h // 2, t * P:(t + 1) * P]

            with ExitStack() as c2:
                NG = 4
                T, Tt, pm = (sb(c2, n, [P, NG, 4, P]) for n in ("T", "Tt", "pm"))
                nt = oT.rearrange("p g (h n) -> p g h n", h=4)
                made, took = sig("made"), sig("took")
                block = c2.enter_context(stage())
                i4 = ident.rearrange("p (o n) -> p o n", o=1).broadcast_to([P, 4, P])
                flat = lambda b: b.rearrange("p (h n) -> p h n", h=4)

                def m4(mask):
                    return mask.rearrange("p (o n) -> p o n", o=1).broadcast_to([P, 4, P])

                order = []
                for hf in range(2):
                    for kind in ("nt", "p0", "t0"):
                        order += [(kind, hf, g, 0) for g in range(NG)]
                    for l in range(1, LEVELS):
                        for kind in ("p", "t", "tt") if l < LEVELS - 1 else ("p", "tt"):
                            order += [(kind, hf, g, l) for g in range(NG)]
                    order += [("ak", hf, g, 0) for g in range(NG)]
                    order += [("y", hf, x, 0) for x in range(2)]
                    order += [("u", hf, x, 0) for x in range(2)]
                    order += [("w", hf, x, 0) for x in range(2)]
                where = {x: n for n, x in enumerate(order)}

                @block.tensor
                def _(pe):
                    for n, (kind, hf, g, l) in enumerate(order):
                        t = hf * 2 + g // 2
                        need = n - 7
                        if kind == "t0":
                            need = max(need, where["p0", hf, g, 0] + 1)
                        elif kind == "p":
                            need = max(need, where["t0" if l == 1 else "tt", hf, g, l - 1] + 1)
                        elif kind in ("t", "tt"):
                            need = max(need, where["p", hf, g, l] + 1)
                        elif kind == "y":
                            need = max(need, where["ak", hf, 2 * g + 1, 0] + 1)
                        elif kind in ("u", "w"):
                            need = max(need, where["y", hf, g, 0] + 1)
                        if need > 0:
                            pe.wait_ge(took.h, need)
                        acc = bank[n % 8]
                        if kind in ("y", "u", "w"):
                            t = hf * 2 + g
                            for h in range(NH):
                                gg, hh = 2 * g + h % 2, h // 2
                                if kind == "y":
                                    mm = pe.matmul(acc[:, h * HD:(h + 1) * HD], pm[:, gg, hh, :], vt[:, t, h * HD:(h + 1) * HD],
                                                   start=True, stop=True)
                                elif kind == "u":
                                    mm = pe.matmul(acc[:, uat(h)], Tt[:, gg, hh, :], nt[:, g, :, :].rearrange("p a b -> p (a b)")[:, h * HD:(h + 1) * HD],
                                                   start=True, stop=True)
                                else:
                                    mm = pe.matmul(acc[h % 2 * HD:h % 2 * HD + HD, h // 2 * P:(h // 2 + 1) * P],
                                                   at_[:, t, h * HD:(h + 1) * HD], Tt[:, gg, hh, :], start=True, stop=True)
                        else:
                            for hh in range(4):
                                h = 2 * hh + g % 2
                                o = acc[:, hh * P:(hh + 1) * P]
                                if kind == "nt":
                                    mm = pe.matmul(o, head(aa, h, t), head(kk, h, t), start=True, stop=True)
                                elif kind == "p0":
                                    mm = pe.matmul(o, head(kk, h, t), head(aa, h, t), start=True, stop=True)
                                elif kind == "ak":
                                    mm = pe.matmul(o, head(k, h, t), head(kk, h, t), start=True, stop=True)
                                elif kind == "t0":
                                    mm = pe.matmul(o, pm[:, g, hh, :], ident, start=True, stop=True)
                                elif kind == "p":
                                    mm = pe.matmul(o, nt[:, g, hh, :], T[:, g, hh, :], start=True, stop=True)
                                elif kind == "t":
                                    mm = pe.matmul(o, Tt[:, g, hh, :], pm[:, g, hh, :], start=True, stop=True)
                                else:
                                    mm = pe.matmul(o, pm[:, g, hh, :], Tt[:, g, hh, :], start=True, stop=True)
                        mm.then_inc(made.h, 1)

                @block.vector
                def _(dve):
                    chain = Chain(dve, dve_chain)
                    for n, (kind, hf, g, l) in enumerate(order):
                        dve.wait_ge(made.h, n + 1)
                        acc = flat(bank[n % 8][:, :])
                        if kind == "nt":
                            ins = dve.tensor_tensor(nt[:, g, :, :], acc, m4(before[:, :]), ALU.mult)
                        elif kind == "p0":
                            chain(dve.tensor_tensor(pm[:, g, :, :], acc, m4(level[:, 0, :]), ALU.mult))
                            ins = dve.tensor_tensor(T[:, g, :, :], pm[:, g, :, :], i4, ALU.add)
                        elif kind == "t0":
                            ins = dve.tensor_tensor(Tt[:, g, :, :], acc, i4, ALU.add)
                        elif kind == "p":
                            ins = dve.tensor_tensor(pm[:, g, :, :], acc, m4(level[:, l, :]), ALU.mult)
                        elif kind == "t":
                            ins = dve.tensor_tensor(T[:, g, :, :], acc, T[:, g, :, :], ALU.add)
                        elif kind == "tt":
                            ins = dve.tensor_tensor(Tt[:, g, :, :], acc, Tt[:, g, :, :], ALU.add)
                        elif kind == "ak":
                            ins = dve.tensor_tensor(pm[:, g, :, :], acc, m4(before[:, :]), ALU.mult)
                        elif kind == "y":
                            ins = dve.tensor_copy(nt[:, g, :, :].rearrange("p a b -> p (a b)"), bank[n % 8][:, :])
                        elif kind == "u":
                            ins = dve.tensor_copy(u0[:, hf * 2 + g, :, :].rearrange("p a b -> p (a b)"), bank[n % 8][:, :])
                        else:
                            ins = dve.tensor_copy(wt[:, hf * 2 + g, :, :], acc)
                        ins.then_inc(took.h, 1)
            with ExitStack() as c3:
                zn = sb(c3, "zn", [P, 4, HD])
                read, u_done, kv_, z_done, zero = sig("read"), sig("u_done"), sig("kv"), sig("z_done"), sig("zero")
                block = c3.enter_context(stage())

                def rng(c):
                    return c * C // P, c * C % P, c * C % P + C

                @block.tensor
                def _(pe):
                    for c in range(NCH - 1):
                        t, r0, r1 = rng(c)
                        pe.wait_ge(z_done.h, c + 1)
                        for h in range(NH):
                            p0 = h % 2 * HD
                            mm = pe.matmul(bank[c % 2 * 2 + h % 2][:, h // 2 * HD:(h // 2 + 1) * HD], wt[p0:p0 + HD, t, h // 2, :],
                                           z[p0:p0 + HD, c, h // 2, :], start=True, stop=True)
                        mm.then_inc(read.h, 1)
                        pe.wait_ge(u_done.h, c + 1)
                        for h in range(NH):
                            p0 = h % 2 * HD
                            o = bank[4 + c % 2][p0:p0 + HD, h // 2 * HD:(h // 2 + 1) * HD]
                            pe.matmul(o, kt[r0:r1, t, h * HD:(h + 1) * HD], vt[r0:r1, t, h * HD:(h + 1) * HD], start=True, stop=False)
                            mm = pe.matmul(o, bt[r0:r1, t, h * HD:(h + 1) * HD], u_of(h, t, r0, r1), start=False, stop=True)
                        mm.then_inc(kv_.h, 1)
                    pe.wait_ge(z_done.h, NCH)
                    c = NCH - 1
                    t, r0, r1 = rng(c)
                    for h in range(NH):
                        p0 = h % 2 * HD
                        mm = pe.matmul(bank[c % 2 * 2 + h % 2][:, h // 2 * HD:(h // 2 + 1) * HD], wt[p0:p0 + HD, t, h // 2, :],
                                       z[p0:p0 + HD, c, h // 2, :], start=True, stop=True)
                    mm.then_inc(read.h, 1)

                @block.vector
                def _(dve):
                    chain = Chain(dve, dve_chain)
                    dve.memset(z[:, 0, :, :], 0.0).then_inc(z_done.h, 1)
                    for c in range(NCH):
                        t, r0, r1 = rng(c)
                        dve.wait_ge(read.h, c + 1)
                        dve.tensor_tensor(u0[r0:r1, t, :, :], banks[r0:r1, c % 2 * 2:c % 2 * 2 + 2, 0:4 * HD], u0[r0:r1, t, :, :], ALU.add).then_inc(u_done.h, 1)
                        if c == NCH - 1:
                            break
                        dve.wait_ge(kv_.h, c + 1)
                        chain(dve.tensor_tensor(zn[:, :, :], bank[4 + c % 2][:, 0:4 * HD].rearrange("p (a b) -> p a b", a=4),
                                                z[:, c, :, :], ALU.add))
                        dve.tensor_tensor(z[:, c + 1, :, :], zn[:, :, :],
                                          pc[:, :, c:c + 1].broadcast_to([P, 4, HD]), ALU.mult).then_inc(z_done.h, 1)
            with ExitStack() as c4:
                rb = [sb(c4, f"rb{i}", [P, 4, P]) for i in range(4)]
                made, took, summed, otk = sig("made"), sig("took"), sig("summed"), sig("otk")
                block = c4.enter_context(stage())
                m4 = lambda mask: mask.rearrange("p (o n) -> p o n", o=1).broadcast_to([P, 4, P])
                groups = [(t, q) for t in range(NT) for q in range(2)]

                @block.tensor
                def _(pe):
                    for n in range(len(groups) + 1):
                        if n < len(groups):
                            t, q = groups[n]
                            for x, src in enumerate((aa, k)):
                                if n >= 2:
                                    pe.wait_ge(took.h, 2 * (n - 2) + x + 1)
                                for hh in range(4):
                                    h = 2 * hh + q
                                    mm = pe.matmul(bank[n % 2 * 2 + x][:, hh * P:(hh + 1) * P], head(src, h, t), head(r, h, t), start=True, stop=True)
                                mm.then_inc(made.h, 1)
                        if n >= 1:
                            t, q = groups[n - 1]
                            pe.wait_ge(took.h, 2 * n)
                            if n >= 3:
                                pe.wait_ge(otk.h, n - 2)
                            for hh in range(4):
                                h = 2 * hh + q
                                p0 = q * HD
                                lo_ = hh * P
                                b = bank[4 + (n - 1) % 2]
                                pe.matmul(b[p0:p0 + HD, lo_:lo_ + P], vt[:, t, h * HD:(h + 1) * HD], rb[(n - 1) % 2 * 2 + 1][:, hh, :], start=True, stop=False, skip_group_check=True)
                                pe.matmul(b[p0:p0 + HD, lo_:lo_ + P], u_of(h, t), rb[(n - 1) % 2 * 2][:, hh, :], start=False, stop=False, skip_group_check=True)
                                for c in range(t * P // C, (t + 1) * P // C):
                                    o0 = c * C - t * P
                                    mm = pe.matmul(b[p0:p0 + HD, lo_ + o0:lo_ + o0 + C], z[p0:p0 + HD, c, h // 2, :],
                                                   r[p0:p0 + HD, h // 2, c * C:(c + 1) * C], start=False, stop=c == (t + 1) * P // C - 1, skip_group_check=True)
                            mm.then_inc(summed.h, 1)

                @block.vector
                def _(dve):
                    for n in range(len(groups)):
                        for x in range(2):
                            dve.wait_ge(made.h, 2 * n + x + 1)
                            if n >= 2:
                                dve.wait_ge(summed.h, n - 1)
                            dve.tensor_tensor(rb[n % 2 * 2 + x][:, :, :], bank[n % 2 * 2 + x][:, :].rearrange("p (h n) -> p h n", h=4),
                                              m4(upto[:, :]), ALU.mult).then_inc(took.h, 1)

                @block.scalar
                def _(act):
                    for n in range(len(groups)):
                        t, q = groups[n]
                        act.wait_ge(summed.h, n + 1)
                        act.activation(oT[q * HD:q * HD + HD, :, t * P:(t + 1) * P], bank[4 + n % 2][q * HD:q * HD + HD, :].rearrange("p (a b) -> p a b", a=4),
                                       ACT.Copy).then_inc(otk.h, 1)
            with ExitStack() as c5:
                gm, gd, g1, g2, g3, g4 = (sig(n) for n in ("gm", "gd", "g1", "g2", "g3", "g4"))
                dd, sqd, rt = kk, aa, ep
                block = c5.enter_context(stage())

                @block.tensor
                def _(pe):
                    for m in range(4):
                        pe.matmul(bank[m][:, :], pair, oT[:, m, :], start=True, stop=True).then_inc(gm.h, 1)
                    for m in range(4):
                        pe.wait_ge(g1.h, m + 1)
                        pe.matmul(bank[4 + m][:, :], pair, sqd[:, m, :], start=True, stop=True).then_inc(g2.h, 1)
                    for m in range(4):
                        pe.matmul(bank[m][:, :], wgu[:, m * P:(m + 1) * P], zg[:, :], start=True, stop=True).then_inc(g4.h, 1)

                @block.scalar
                def _(act):
                    for m in range(4):
                        act.wait_ge(gd.h, m + 1)
                        act.activation(sqd[:, m, :], dd[:, m, :], ACT.Square).then_inc(g1.h, 1)
                    for m in range(4):
                        act.wait_ge(g3.h, m + 1)
                        act.activation(rt[:, m, :], tmp[:, m, :], ACT.Sqrt).then_inc(g1.h, 1)

                @block.vector
                def _(dve):
                    chain = Chain(dve, dve_chain)
                    for m in range(4):
                        dve.wait_ge(gm.h, m + 1)
                        dve.scalar_tensor_tensor(dd[:, m, :], bank[m][:, :], -1.0 / HD, oT[:, m, :], ALU.mult, ALU.add).then_inc(gd.h, 1)
                    for m in range(4):
                        dve.wait_ge(g2.h, m + 1)
                        dve.tensor_scalar(tmp[:, m, :], bank[4 + m][:, :], 1.0 / HD, GN_EPS, ALU.mult, ALU.add).then_inc(g3.h, 1)
                    for m in range(4):
                        dve.wait_ge(g1.h, 4 + m + 1)
                        chain(dve.reciprocal(em[:, m, :], rt[:, m, :]))
                        chain(dve.scalar_tensor_tensor(dd[:, m, :], dd[:, m, :], col("ln_g", m), em[:, m, :], ALU.mult, ALU.mult))
                        chain(dve.scalar_tensor_tensor(dd[:, m, :], dd[:, m, :], col("ln_b", m), cs[:, m, :], ALU.add, ALU.add))
                        dve.wait_ge(g4.h, m + 1)
                        chain(dve.tensor_tensor(oT[:, m, :], dd[:, m, :], bank[m][:, :], ALU.mult))

    def local_attention(qT, kd, vT, oT):
        with ExitStack() as ctx:
            vt = sb(ctx, "vt", [P, 1, 4, P])
            bias = sb(ctx, "bias", [P, NH, 2 * P])
            sinks = sb(ctx, "sinks", [P, NH])
            with ExitStack() as c1:
                table = sb(c1, "table", [BUCKETS + 1, NH])
                hot = sb(c1, "hot", [BUCKETS + 1, RLEN])
                row = sb(c1, "row", [NH, RLEN])
                got, m, c, w = sig("got"), sig("m"), sig("c"), sig("w")
                block = c1.enter_context(stage())

                @block.sync
                def _(sp):
                    sp.dma_start(table[0:BUCKETS, :], a["rel_bias"]).then_inc(got.h, 16)
                    lo_ = CST["ones"][0]
                    sp.dma_start(table[BUCKETS:BUCKETS + 1, :], a["cst"][0:1, lo_:lo_ + NH]).then_inc(got.h, 16)
                    cst_dma(sp, hot[:, :], "onehot", got, BUCKETS + 1)
                    sp.dma_start(sinks[:, :], a["sinks"][0:1, :].broadcast_to([P, NH])).then_inc(w.h, 16)
                    sp.wait_ge(c.h, 1)
                    sp.dma_start(scratch[:, :, :], row[:, :].rearrange("h (o x) -> h o x", o=1).broadcast_to([NH, P, RLEN])).then_inc(w.h, 16)
                    sp.wait_ge(w.h, 32)
                    flat = scratch[:, :, :].rearrange("h q x -> h (q x)")
                    sp.dma_start(bias[:, :, :], flat[:, P - 1:P - 1 + P * (RLEN - 1)].rearrange("h (q x) -> q h x", x=RLEN - 1)[:, :, 0:2 * P]).then_inc(w.h, 16)
                    sp.wait_ge(w.h, 48)

                @block.tensor
                def _(pe):
                    pe.wait_ge(got.h, 48)
                    pe.matmul(bank[0][0:NH, 0:RLEN], table[:, :], hot[:, :], start=True, stop=True).then_inc(m.h, 1)

                @block.vector
                def _(dve):
                    dve.wait_ge(m.h, 1)
                    dve.tensor_copy(row[:, :], bank[0][0:NH, 0:RLEN]).then_inc(c.h, 1)
            turn([(vt[:, 0, :, :], [vT[:, t * P:(t + 1) * P] for t in range(NT)])])
            units, dst = [], []
            for h in range(NH):
                p0, g = h % 2 * HD, h // 4
                for n in range(NT):
                    lo_ = max(n - 1, 0) * P
                    hi_ = (n + 1) * P
                    w = hi_ - lo_
                    units.append(([[(qT[p0:p0 + HD, h // 2, n * P:hi_], kd[p0:p0 + HD, g, lo_:hi_])]], w,
                                  (bias[:, h, 2 * P - w:2 * P], None),
                                  [vt[:, 0, b, g * HD:(g + 1) * HD] for b in range(lo_ // P, n + 1)], (p0, p0 + HD)))
                    dst.append(oT[p0:p0 + HD, h // 2, n * P:hi_])
            attend(units, lambda u: dst[u], sink=lambda i: sinks[:, i // NT:i // NT + 1])

    def add_normed(src, name):
        with ExitStack() as ctx:
            y = sb(ctx, "y", [P, 2, S])

            def finish(dve, chain, k, rstd):
                chain(dve.scalar_tensor_tensor(y[:, k % 2, :], src[:, k, :], col(name, k), rstd, ALU.mult, ALU.mult))
                chain(dve.tensor_tensor(xT[:, k, :], y[:, k % 2, :], xT[:, k, :], ALU.add))
            norm(lambda k: src[:, k, :], KD, None, None, D, EPS, finish)

    def tables(cosT, sinT):
        with ExitStack() as ctx:
            pi = sb(ctx, "pi", [P, S], mybir.dt.int32)
            fr = sb(ctx, "fr", [P, 2])
            ang, n, r = (sb(ctx, x, [P, S]) for x in ("ang", "n", "r"))
            got, reduced, sined = sig("got"), sig("reduced"), sig("sined")
            MAGIC = 1.5 * 2.0 ** 23
            C1 = 6.28125
            C2 = 0.00193500518798828125
            C3 = 2 * math.pi - C1 - C2
            block = ctx.enter_context(stage())

            @block.sync
            def _(sp):
                sp.dma_start(pi[:, :], a["positions_2"][0:1, :].broadcast_to([P, S])).then_inc(got.h, 16)
                cst_dma(sp, fr[:, :], "freq", got)

            @block.vector
            def _(dve):
                chain = Chain(dve, dve_chain)
                dve.wait_ge(got.h, 32)
                chain(dve.tensor_copy(ang[:, :], pi[:, :]))
                chain(dve.tensor_scalar(ang[:, :], ang[:, :], fr[:, 0:1], None, ALU.mult))
                chain(dve.tensor_scalar(n[:, :], ang[:, :], 1 / (2 * math.pi), None, ALU.mult))
                chain(dve.tensor_scalar(n[:, :], n[:, :], MAGIC, None, ALU.add))
                chain(dve.tensor_scalar(n[:, :], n[:, :], -MAGIC, None, ALU.add))
                for c in (C1, C2, C3):
                    chain(dve.scalar_tensor_tensor(ang[:, :], n[:, :], -c, ang[:, :], ALU.mult, ALU.add))
                chain(dve.tensor_scalar(ang[:, :], ang[:, :], 3.1415925, -3.1415925, ALU.min, ALU.max))
                reduced.by(dve.tensor_scalar(r[:, :], ang[:, :], 0.5, None, ALU.mult))
                dve.wait_ge(sined.h, 2)
                chain(dve.tensor_tensor(r[:, :], r[:, :], r[:, :], ALU.mult))
                chain(dve.tensor_scalar(cosT[:, :], r[:, :], -2.0, 1.0, ALU.mult, ALU.add))
                chain(dve.tensor_scalar(sinT[:, :], sinT[:, :], fr[:, 1:2], None, ALU.mult))

            @block.scalar
            def _(act):
                act.wait_ge(reduced.h, 1)
                act.activation(sinT[:, :], ang[:, :], ACT.Sin).then_inc(sined.h, 1)
                act.activation(r[:, :], r[:, :], ACT.Sin).then_inc(sined.h, 1)

    def rope(tiles, cosT, sinT):
        with ExitStack() as ctx:
            sw = sb(ctx, "sw", [P, P])
            t_ = sb(ctx, "t_", [P, 2, S])
            got, swapped, used = sig("got"), sig("swapped"), sig("used")
            block = ctx.enter_context(stage())

            @block.sync
            def _(sp):
                cst_dma(sp, sw[:, :], "swap", got)

            @block.tensor
            def _(pe):
                pe.wait_ge(got.h, 16)
                for n, x in enumerate(tiles):
                    if n >= 8:
                        pe.wait_ge(used.h, n - 7)
                    pe.matmul(bank[n % 8][:, :], sw[:, :], x, start=True, stop=True).then_inc(swapped.h, 1)

            @block.vector
            def _(dve):
                chain = Chain(dve, dve_chain)
                for n, x in enumerate(tiles):
                    dve.wait_ge(swapped.h, n + 1)
                    used.by(dve.tensor_tensor(t_[:, n % 2, :], bank[n % 8][:, :], sinT[:, :], ALU.mult))
                    chain(dve.tensor_tensor(x, x, cosT[:, :], ALU.mult))
                    dve.wait_ge(used.h, n + 1)
                    chain(dve.tensor_tensor(x, x, t_[:, n % 2, :], ALU.add))

    def even_mixer(cosT, sinT, oT):
        with ExitStack() as ctx:
            bq, bk, bv = (sb(ctx, n, [P, 4, S]) for n in ("bq", "bk", "bv"))
            with ExitStack() as fx:
                aq, ak, av = (sb(fx, n, [P, 4, S]) for n in ("aq", "ak", "av"))
                af = sb(fx, "af", [P, S])
                with ExitStack() as pr:
                    hi, lo = sb(pr, "hi", [P, KD, S], F32R), sb(pr, "lo", [P, KD, S], F32R)
                    norm_split(lambda k: ("attn_norm", k), hi, lo)
                    dsts = [t[:, m, :] for t in (aq, ak, av) for m in range(4)] + [af[:, :]] + [t[:, m, :] for t in (bq, bk, bv) for m in range(4)]
                    project(25, hi, lo, lambda act, m, acc: act.activation(dsts[m], acc, ACT.Copy))
                forget = sb(fx, "forget", [P, NH, S])
                with ExitStack() as c1:
                    fb = sb(c1, "fb", [NH, 1])
                    x, y, w, one = (sb(c1, n, [NH, S]) for n in ("x", "y", "w", "one"))
                    pick = sb(c1, "pick", [NH, NH, P])
                    got, made, did, spread = sig("got"), sig("made"), sig("did"), sig("spread")
                    block = c1.enter_context(stage())

                    @block.sync
                    def _(sp):
                        sp.dma_start(fb[:, :], a["ev_fgate_b_2"].rearrange("o h -> h o")).then_inc(got.h, 16)

                    @block.vector
                    def _(dve):
                        chain = Chain(dve, dve_chain)
                        dve.wait_ge(got.h, 16)
                        chain(dve.memset(one[:, :], 1.0))
                        chain(dve.tensor_copy(pick[:, :, :], ident[0:NH, 0:NH].rearrange("p (h o) -> p h o", o=1).broadcast_to([NH, NH, P])))
                        made.by(dve.tensor_scalar(x[:, :], af[0:NH, :], fb[:, 0:1], None, ALU.add))
                        dve.wait_ge(did.h, 1)
                        chain(dve.tensor_scalar(w[:, :], x[:, :], 0.0, None, ALU.min))
                        chain(dve.tensor_tensor(y[:, :], y[:, :], w[:, :], ALU.subtract))
                        made.by(dve.tensor_tensor_scan(w[:, :], one[:, :], y[:, :], 0.0, ALU.mult, ALU.add))
                        for h in range(NH):
                            dve.wait_ge(spread.h, h + 1)
                            dve.tensor_copy(forget[:, h, :], bank[h][:, :])

                    @block.scalar
                    def _(act):
                        chain = Chain(act, act_chain)
                        act.wait_ge(made.h, 1)
                        chain(act.activation(y[:, :], x[:, :], ACT.Abs))
                        chain(act.activation(y[:, :], y[:, :], ACT.Exp, scale=-1.0))
                        did.by(act.activation(y[:, :], y[:, :], ACT.Ln, bias=1.0))

                    @block.tensor
                    def _(pe):
                        pe.wait_ge(made.h, 2)
                        for h in range(NH):
                            pe.matmul(bank[h][:, :], pick[:, h, :], w[:, :], start=True, stop=True).then_inc(spread.h, 1)
                vt = sb(fx, "vt", [P, NT, 4, P])
                future = sb(fx, "future", [P, P])
                load_cst(future[:, :], "future")
                turn([(vt[:, t, :, :], [av[:, m, t * P:(t + 1) * P] for m in range(4)]) for t in range(NT)])
                units, dst = [], []
                for h in range(NH):
                    p0 = h % 2 * HD
                    for n in range(NT):
                        w = (n + 1) * P
                        units.append(([[(aq[p0:p0 + HD, h // 2, n * P:w], ak[p0:p0 + HD, h // 2, 0:w])]], w,
                                      (forget[:, h, 0:w], future[:, :]),
                                      [vt[:, b, h // 2, p0:p0 + HD] for b in range(n + 1)], (p0, p0 + HD)))
                        dst.append(oT[p0:p0 + HD, h // 2, n * P:w])
                attend(units, lambda u: dst[u])
            rope([t[:, m, :] for t in (bq, bk) for m in range(4)], cosT, sinT)
            vt = sb(ctx, "vt", [P, NT, 4, P])
            mask = sb(ctx, "mask", [P, S])
            lam = sb(ctx, "lam", [P, 1])
            ob = sb(ctx, "ob", [P, 4, S])
            lam_init = 0.8 - 0.6 * math.exp(-0.3 * 0)
            with ExitStack() as c1:
                ls = sb(c1, "ls", [P, 4, HD])
                pr2 = sb(c1, "pr2", [P, 2, HD])
                sm2 = sb(c1, "sm2", [P, 2])
                got, summed, exped = sig("got"), sig("summed"), sig("exped")
                block = c1.enter_context(stage())

                @block.sync
                def _(sp):
                    for i, n in enumerate(("q1", "q2", "k1", "k2")):
                        sp.dma_start(ls[:, i, :], a[f"ev_lambda_{n}_2"][0:1, :].broadcast_to([P, HD])).then_inc(got.h, 16)
                    cst_dma(sp, mask[:, S - P:S], "future", got)

                @block.vector
                def _(dve):
                    chain = Chain(dve, dve_chain)
                    dve.memset(mask[:, 0:S - P], 0.0)
                    dve.wait_ge(got.h, 80)
                    chain(dve.tensor_tensor(pr2[:, :, :], ls[:, 0:2, :], ls[:, 2:4, :], ALU.mult))
                    summed.by(dve.tensor_reduce(sm2[:, :], pr2[:, :, :], AX.X, ALU.add))
                    dve.wait_ge(exped.h, 1)
                    chain(dve.tensor_scalar(lam[:, :], sm2[:, 0:1], sm2[:, 1:2], lam_init, ALU.subtract, ALU.add))

                @block.scalar
                def _(act):
                    act.wait_ge(summed.h, 1)
                    exped.by(act.activation(sm2[:, :], sm2[:, :], ACT.Exp))
            turn([(vt[:, t, :, :], [bv[:, m, t * P:(t + 1) * P] for m in range(4)]) for t in range(NT)])
            units, dst = [], []
            for h in range(4):
                for n in range(NT):
                    w = (n + 1) * P
                    units.append(([[(bq[p0:p0 + HD, h, n * P:w], bk[p0:p0 + HD, h, 0:w])] for p0 in (0, HD)], w,
                                  (mask[:, S - w:S], None), [vt[:, b, h, :] for b in range(n + 1)], (0, P)))
                    dst.append(ob[:, h, n * P:w])
            attend(units, lambda u: dst[u], lam=lam[:, 0:1])

            def finish(dve, chain, k, rstd):
                chain(dve.scalar_tensor_tensor(bq[:, k, :], ob[:, k, :], col("subln"), rstd, ALU.mult, ALU.mult))
                chain(dve.tensor_scalar(oT[:, 4 + k, :], bq[:, k, :], 1.0 - lam_init, None, ALU.mult))
            norm(lambda k: ob[:, k, :], 4, None, None, 2 * HD, EPS, finish, groups=4)

    def load_cst(dst, name):
        with ExitStack() as ctx:
            got = sig("got")
            block = ctx.enter_context(stage())

            @block.sync
            def _(sp):
                cst_dma(sp, dst, name, got)
                sp.wait_ge(got.h, 16)

    def odd_mixer(cosT, sinT, oT):
        with ExitStack() as ctx:
            sq_, sk_, sv_ = (sb(ctx, n, [P, 4, S]) for n in ("sq", "sk", "sv"))
            with ExitStack() as ds:
                cq = sb(ds, "cq", [P, 4, S])
                ckv, kr, ciw, ik = (sb(ds, n, [P, 1, S]) for n in ("ckv", "kr", "ciw", "ik"))
                iq = sb(ds, "iq", [P, 2, S])
                with ExitStack() as pr:
                    hi, lo = sb(pr, "hi", [P, KD, S], F32R), sb(pr, "lo", [P, KD, S], F32R)
                    norm_split(lambda k: ("attn_norm", KD + k), hi, lo)
                    dsts = [cq[:, m, :] for m in range(4)] + [ckv[:, 0, :], kr[:, 0, :], iq[:, 0, :], iq[:, 1, :], ciw[:, 0, :], ik[:, 0, :]] \
                        + [t[:, m, :] for t in (sq_, sk_, sv_) for m in range(4)]
                    project(22, hi, lo, lambda act, m, acc: act.activation(dsts[m], acc, ACT.Copy))
                rope([cq[:, m, :] for m in range(4)] + [kr[:, 0, :], iq[:, 0, :], iq[:, 1, :], ik[:, 0, :]], cosT, sinT)

                def finish(dve, chain, k, rstd):
                    chain(dve.scalar_tensor_tensor(ckv[:, 0, :], ckv[:, 0, :], col("kv_norm"), rstd, ALU.mult, ALU.mult))
                norm(lambda k: ckv[:, 0, :], 1, None, None, P, EPS, finish)
                ukp = sb(ds, "ukp", [P, NH, HD])
                uk = sb(ds, "uk", [P, 1, 4, P])
                wuv = sb(ds, "wuv", [P, NH, HD])
                future = sb(ds, "future", [P, P])
                one = sb(ds, "one", [P, S])
                with ExitStack() as c1:
                    got = sig("got")
                    zeroed = sig("zeroed")
                    block = c1.enter_context(stage())

                    @block.vector
                    def _(dve):
                        dve.memset(one[:, :], 1.0)
                        dve.memset(ukp[:, :, 0:ROT], 0.0)

                    @block.sync
                    def _(sp):
                        sp.dma_start(ukp[:, :, ROT:HD], a["od_w_uk_2"][0]).then_inc(got.h, 16)
                        sp.dma_start(wuv[:, :, :], a["od_w_uv_2"][0]).then_inc(got.h, 16)
                        cst_dma(sp, future[:, :], "future", got)
                        sp.wait_ge(got.h, 48)
                ct = sb(ds, "ct", [P, 1, 4, P])
                iwt = sb(ds, "iwt", [P, 1, 4, P])
                turn([(uk[:, 0, :, :], [ukp[:, 2 * m:2 * m + 2, :].rearrange("p h n -> p (h n)") for m in range(4)]),
                      (ct[:, 0, :, :], [ckv[:, 0, t * P:(t + 1) * P] for t in range(NT)]),
                      (iwt[:, 0, :, :], [ciw[:, 0, t * P:(t + 1) * P] for t in range(NT)])])
                keep = sb(ds, "keep", [P, NT - 1, S])
                with ExitStack() as c1:
                    score = sb(c1, "score", [P, NT - 1, S])
                    work = sb(c1, "work", [P, NT - 1, S])
                    part = sb(c1, "part", [P, 2, S])
                    top = sb(c1, "top", [P, NT - 1, 8])
                    cnt = sb(c1, "cnt", [P, NT - 1])
                    logit, taken = sig("logit"), sig("taken")
                    block = c1.enter_context(stage())

                    @block.tensor
                    def _(pe):
                        for n in range(1, NT):
                            for h in range(4):
                                x = (n - 1) * 4 + h
                                if x >= 8:
                                    pe.wait_ge(taken.h, x - 7)
                                p0 = h % 2 * HD
                                pe.matmul(bank[x % 8][:, 0:(n + 1) * P], iq[p0:p0 + HD, h // 2, n * P:(n + 1) * P], ik[p0:p0 + HD, 0, 0:(n + 1) * P],
                                          start=True, stop=True).then_inc(logit.h, 1)

                    @block.vector
                    def _(dve):
                        chain = Chain(dve, dve_chain)
                        chain(dve.tensor_scalar(iwt[:, 0, :, 0:4], iwt[:, 0, :, 0:4], 0.5, None, ALU.mult))
                        for n in range(1, NT):
                            w = (n + 1) * P
                            sc, wk, kp = score[:, n - 1, 0:w], work[:, n - 1, 0:w], keep[:, n - 1, 0:w]
                            for h in range(4):
                                dve.wait_ge(logit.h, (n - 1) * 4 + h + 1)
                                taken.by(dve.tensor_scalar(sc if h == 0 else part[:, h % 2, 0:w], bank[((n - 1) * 4 + h) % 8][:, 0:w], 0.0,
                                                           iwt[:, 0, n, h:h + 1], ALU.max, ALU.mult))
                                dve.wait_ge(taken.h, (n - 1) * 4 + h + 1)
                                if h:
                                    chain(dve.tensor_tensor(sc, sc, part[:, h % 2, 0:w], ALU.add))
                            chain(dve.tensor_tensor(score[:, n - 1, w - P:w], score[:, n - 1, w - P:w], future[:, :], ALU.add))
                            for i in range(TOPK // 8):
                                chain(dve.max(top[:, n - 1, :], sc if i == 0 else wk))
                                if i < TOPK // 8 - 1:
                                    chain(dve.match_replace(wk, top[:, n - 1, :], sc if i == 0 else wk, -3e38))
                            thr = top[:, n - 1, 7:8]
                            chain(dve.tensor_scalar(kp, sc, thr, None, ALU.is_gt))
                            chain(dve.tensor_reduce(cnt[:, n - 1:n], kp, AX.X, ALU.add))
                            chain(dve.tensor_scalar(cnt[:, n - 1:n], cnt[:, n - 1:n], -1.0, float(TOPK), ALU.mult, ALU.add))
                            chain(dve.tensor_scalar(sc, sc, thr, None, ALU.is_equal))
                            chain(dve.tensor_tensor_scan(wk, one[:, 0:w], sc, 0.0, ALU.mult, ALU.add))
                            chain(dve.tensor_scalar(wk, wk, cnt[:, n - 1:n], None, ALU.is_le))
                            chain(dve.tensor_tensor(wk, wk, sc, ALU.mult))
                            chain(dve.tensor_tensor(kp, kp, wk, ALU.add))
                            chain(dve.tensor_scalar(kp, kp, -1.0, 1e30, ALU.add, ALU.mult))
                qa = sb(ds, "qa", [P, NH, S])
                with ExitStack() as c1:
                    made = sig("made")
                    block = c1.enter_context(stage())

                    @block.tensor
                    def _(pe):
                        for h in range(NH):
                            p0 = h % 2 * HD
                            pe.matmul(bank[h][:, :], uk[p0:p0 + HD, 0, h // 2, :], cq[p0:p0 + HD, h // 2, :], start=True, stop=True).then_inc(made.h, 1)

                    @block.vector
                    def _(dve):
                        for h in range(NH):
                            dve.wait_ge(made.h, h + 1)
                            dve.tensor_copy(qa[:, h, :], bank[h][:, :])
                ol = sb(ds, "ol", [P, NH, S])
                units, dst = [], []
                for h in range(NH):
                    p0 = h % 2 * HD
                    for n in range(NT):
                        w = (n + 1) * P
                        units.append(([[(qa[:, h, n * P:w], ckv[:, 0, 0:w]),
                                        (cq[p0:p0 + ROT, h // 2, n * P:w], kr[p0:p0 + ROT, 0, 0:w])]], w,
                                      (future[:, :] if n == 0 else keep[:, n - 1, 0:w], None),
                                      [ct[:, 0, b, :] for b in range(n + 1)], (0, P)))
                        dst.append(ol[:, h, n * P:w])
                attend(units, lambda u: dst[u])
                with ExitStack() as c1:
                    made = sig("made")
                    block = c1.enter_context(stage())

                    @block.tensor
                    def _(pe):
                        for h in range(NH):
                            p0 = h % 2 * HD
                            pe.matmul(bank[h][p0:p0 + HD, :], wuv[:, h, :], ol[:, h, :], start=True, stop=True).then_inc(made.h, 1)

                    @block.vector
                    def _(dve):
                        for h in range(NH):
                            p0 = h % 2 * HD
                            dve.wait_ge(made.h, h + 1)
                            dve.tensor_copy(oT[p0:p0 + HD, h // 2, :], bank[h][p0:p0 + HD, :])
            stick_breaking(sq_, sk_, sv_, oT)

    def stick_breaking(q, k, v, oT):
        W = [S - b * P for b in range(NT)]
        at_b = [sum(W[:b]) for b in range(NT)]
        ALL = sum(W)
        with ExitStack() as ctx:
            vt = sb(ctx, "vt", [P, NT, 4, P])
            past, after = sb(ctx, "past", [P, P]), sb(ctx, "after", [P, P])
            load_cst(past[:, :], "past_t")
            load_cst(after[:, :], "after_t")
            turn([(vt[:, t, :, :], [v[:, m, t * P:(t + 1) * P] for m in range(4)]) for t in range(NT)])
            zs = [sb(ctx, f"zs{i}", [P, ALL]) for i in range(3)]
            sp_ = [sb(ctx, f"sp{i}", [P, ALL]) for i in range(2)]
            aw = [sb(ctx, f"aw{i}", [P, ALL]) for i in range(2)]
            zed, logs, masked, summed, args_, exped, cut, weighed, otk = (
                sig(n) for n in ("zed", "logs", "masked", "summed", "args", "exped", "cut", "weighed", "otk"))
            zcopied = sig("zcopied")
            block = ctx.enter_context(stage())

            @block.tensor
            def _(pe):
                for i in range(NH + 2):
                    if i < NH:
                        p0 = i % 2 * HD
                        for b in range(NT):
                            if i >= 1:
                                pe.wait_ge(zcopied.h, (i - 1) * NT + b + 1)
                            pe.matmul(bank[b][:, 0:W[b]], k[p0:p0 + HD, i // 2, b * P:(b + 1) * P], q[p0:p0 + HD, i // 2, b * P:S],
                                      start=True, stop=True).then_inc(zed.h, 1)
                    u = i - 1
                    if 0 <= u < NH:
                        pe.wait_ge(masked.h, u + 1)
                        for b in range(NT):
                            x = u * NT + b
                            if x >= 3:
                                pe.wait_ge(args_.h, x - 2)
                            o = bank[4 + x % 3]
                            mm = pe.matmul(o[:, 0:W[b]], after[:, :], sp_[u % 2][:, at_b[b]:at_b[b] + W[b]], start=True, stop=b == NT - 1)
                            for c in range(b + 1, NT):
                                mm = pe.matmul(o[:, (c - b) * P:W[b]], ones, sp_[u % 2][:, at_b[c]:at_b[c] + W[c]], start=False, stop=c == NT - 1)
                            mm.then_inc(summed.h, 1)
                    u = i - 2
                    if 0 <= u < NH:
                        p0 = u % 2 * HD
                        pe.wait_ge(cut.h, u + 1)
                        if u >= 1:
                            pe.wait_ge(otk.h, u)
                        for b in range(NT):
                            mm = pe.matmul(bank[7][p0:p0 + HD, b * P:S], vt[:, b, u // 2, p0:p0 + HD], aw[u % 2][:, at_b[b]:at_b[b] + W[b]],
                                           start=b == 0, stop=b == NT - 1)
                        mm.then_inc(weighed.h, 1)

            @block.scalar
            def _(act):
                chain = Chain(act, act_chain)
                act.preload_act_table_set("natural_log_exp_and_others")
                for i in range(NH + 2):
                    if i < NH:
                        if i >= 3:
                            act.wait_ge(args_.h, (i - 2) * NT)
                        if i >= 2:
                            act.wait_ge(summed.h, (i - 1) * NT)
                        for b in range(NT):
                            act.wait_ge(zed.h, i * NT + b + 1)
                            zcopied.by(act.activation(zs[i % 3][:, at_b[b]:at_b[b] + W[b]], bank[b][:, 0:W[b]], ACT.Copy, scale=HD ** -0.5))
                        act.wait_ge(zcopied.h, (i + 1) * NT)
                        s = sp_[i % 2][:, :]
                        chain(act.activation(s, zs[i % 3][:, :], ACT.Abs))
                        chain(act.activation(s, s, ACT.Exp, scale=-1.0))
                        logs.by(act.activation(s, s, ACT.Ln, bias=1.0))
                    u = i - 1
                    if 0 <= u < NH:
                        act.wait_ge(args_.h, (u + 1) * NT)
                        exped.by(act.activation(aw[u % 2][:, :], aw[u % 2][:, :], ACT.Exp))
                    u = i - 2
                    if 0 <= u < NH:
                        p0 = u % 2 * HD
                        act.wait_ge(weighed.h, u + 1)
                        otk.by(act.activation(oT[p0:p0 + HD, 4 + u // 2, :], bank[7][p0:p0 + HD, :], ACT.Copy))

            @block.vector
            def _(dve):
                chain = Chain(dve, dve_chain)
                for i in range(NH + 1):
                    if i < NH:
                        s = sp_[i % 2]
                        dve.wait_ge(logs.h, i + 1)
                        chain(dve.scalar_tensor_tensor(s[:, :], zs[i % 3][:, :], 0.0, s[:, :], ALU.max, ALU.add))
                        for b in range(NT):
                            ins = dve.tensor_tensor(s[:, at_b[b]:at_b[b] + P], s[:, at_b[b]:at_b[b] + P], past[:, :], ALU.mult)
                        masked.by(ins)
                    u = i - 1
                    if 0 <= u < NH:
                        w = aw[u % 2]
                        if u >= 2:
                            dve.wait_ge(weighed.h, u - 1)
                        for b in range(NT):
                            dve.wait_ge(summed.h, u * NT + b + 1)
                            x = slice(at_b[b], at_b[b] + W[b])
                            chain(dve.tensor_tensor(w[:, x], zs[u % 3][:, x], bank[4 + (u * NT + b) % 3][:, 0:W[b]], ALU.subtract))
                            args_.by(dve.tensor_scalar(w[:, x], w[:, x], 0.0, None, ALU.min))
                        dve.wait_ge(exped.h, u + 1)
                        for b in range(NT):
                            ins = dve.tensor_tensor(w[:, at_b[b]:at_b[b] + P], w[:, at_b[b]:at_b[b] + P], past[:, :], ALU.mult)
                        cut.by(ins)

    def final():
        with ExitStack() as ctx:
            y = sb(ctx, "y", [P, KD, S])
            res = sb(ctx, "res", [P, NT, 2, 4, P])

            def finish(dve, chain, k, rstd):
                chain(dve.scalar_tensor_tensor(y[:, k, :], xT[:, k, :], col("final_norm", k), rstd, ALU.mult, ALU.mult))
            norm(lambda k: xT[:, k, :], KD, None, None, D, EPS, finish)
            turn([(res[:, t, q, :, :], [y[:, 4 * q + m, t * P:(t + 1) * P] for m in range(4)]) for t in range(NT) for q in range(2)])
            stored = sig("stored")
            block = ctx.enter_context(stage())

            @block.sync
            def _(sp):
                sp.dma_start(out[0].rearrange("(t p) d -> p t d", p=P), res[:, :, :, :, :].rearrange("p t q m n -> p t (q m n)")).then_inc(stored.h, 16)
                sp.wait_ge(stored.h, 16)

    setup()

    def layer_one():
        with ExitStack() as st:
            oT = sb(st, "oT", [P, KD, S])
            with ExitStack() as rw:
                r, k, v = (sb(rw, n, [P, 4, S]) for n in "rkv")
                zt, zg = sb(rw, "zt", [P, S]), sb(rw, "zg", [P, S])
                with ExitStack() as at:
                    qT, kd, vT = sb(at, "qT", [P, 4, S]), sb(at, "kd", [P, 2, S]), sb(at, "vT", [P, S])
                    with ExitStack() as pr:
                        hi, lo = sb(pr, "hi", [P, KD, S], F32R), sb(pr, "lo", [P, KD, S], F32R)
                        norm_split(lambda k: ("norm_mix_pre", k), hi, lo)
                        pad = [sb(pr, f"pad{i}", [P, S + 1]) for i in range(2)]
                        df = sb(pr, "df", [P, S])
                        shifted = sig("shifted")
                        s0 = state["s"]

                        def dst(m):
                            return (qT[:, m, :] if m < 4 else kd[:, m - 4, :] if m < 6 else vT[:, :] if m == 6
                                    else r[:, m - 7, :] if m < 11 else k[:, m - 11, :] if m < 15
                                    else v[:, m - 15, :] if m < 19 else (zt, zg)[m - 19][:, :])

                        def put(act, m, acc):
                            if m < 7:
                                return act.activation(dst(m), acc, ACT.Copy)
                            if m >= 9:
                                act.wait_ge(shifted.h, m - 8)
                            return act.activation(pad[m % 2][:, 1:S + 1], acc, ACT.Copy)

                        def post(dve, chain, m):
                            if m == 0:
                                chain(dve.memset(pad[0][:, 0:1], 0.0))
                                chain(dve.memset(pad[1][:, 0:1], 0.0))
                            if m < 7:
                                return
                            x = pad[m % 2]
                            chain(dve.tensor_tensor(df[:, :], x[:, 0:S], x[:, 1:S + 1], ALU.subtract))
                            shifted.by(dve.scalar_tensor_tensor(dst(m), df[:, :], col("mix", m - 7), x[:, 1:S + 1], ALU.mult, ALU.add))
                            dve.wait_ge(shifted.h, m - 6)
                        project(21, hi, lo, put, post)
                    local_attention(qT, kd, vT, oT)
                rwkv(r, k, v, zt, zg, oT[:, 4:8, :], rw)

            with ExitStack() as pr:
                hi, lo, mixed = sb(pr, "hi", [P, KD, S], F32R), sb(pr, "lo", [P, KD, S], F32R), sb(pr, "mixed", [P, KD, S])
                split(lambda k: oT[:, k, :], KD, hi, lo)
                project(8, hi, lo, lambda act, m, acc: act.activation(mixed[:, m, :], acc, ACT.Copy))
                add_normed(mixed, "norm_mix_post")
    layer_one()
    with ExitStack() as st:
        f = sb(st, "f", [P, KD, S])
        with ExitStack() as ff:
            hi, lo = sb(ff, "hi", [P, KD, S], F32R), sb(ff, "lo", [P, KD, S], F32R)
            norm_split(lambda k: ("norm_ffn_pre", k), hi, lo)
            for ch in range(2):
                ffn(wu1, FF1, wd1, conv1, 16 * ch, 16, PARTS1, hi, lo, ACT.Gelu_apprx_tanh, ch == 1, f)
        add_normed(f, "norm_ffn_post")
    with ExitStack() as two:
        cosT, sinT = sb(two, "cosT", [P, S]), sb(two, "sinT", [P, S])
        tables(cosT, sinT)
        for layer in range(2):
            with ExitStack() as st:
                oT = sb(st, "oT", [P, KD, S])
                (even_mixer, odd_mixer)[layer](cosT, sinT, oT)
                with ExitStack() as pr:
                    hi, lo = sb(pr, "hi", [P, KD, S], F32R), sb(pr, "lo", [P, KD, S], F32R)
                    split(lambda k: oT[:, k, :], KD, hi, lo)
                    project(8, hi, lo, None, lambda dve, chain, m, acc: dve.tensor_tensor(xT[:, m, :], acc, xT[:, m, :], ALU.add))
            with ExitStack() as ff:
                hi, lo = sb(ff, "hi", [P, KD, S], F32R), sb(ff, "lo", [P, KD, S], F32R)
                norm_split(lambda k: ("ffn_norm", KD * layer + k), hi, lo)
                ffn(wu2[layer], FF2, wd2[layer], conv2[layer], 0, 22, PARTS2, hi, lo, ACT.Silu, True, xT)
    final()


_OUTS = [((1, S, D), "float32")]


def kernel(**inputs):
    import numpy as _np
    import concourse.bacc as _bacc
    from concourse import mybir as _mybir
    from concourse.bass_utils import run_bass_kernel_spmd as _run

    nc = _bacc.Bacc("TRN2", target_bir_lowering=False, num_devices=1)
    arrays, args = {}, {}
    inputs["cst"] = constants()
    for name, value in inputs.items():
        v = _np.ascontiguousarray(value)
        arrays[f"in_{name}_dram"] = v
        args[name] = nc.dram_tensor(f"in_{name}_dram", v.shape, _mybir.dt.from_np(v.dtype), kind="ExternalInput").ap()
    out = nc.dram_tensor("out_0_dram", (1, S, D), F32, kind="ExternalOutput").ap()
    program(nc, args, out)
    r = _run(nc, [arrays], core_ids=[0])
    return r.results[0]["out_0_dram"]
```

```python
from contextlib import ExitStack, contextmanager
import math

import numpy as np
import concourse.bass as bass
from concourse import mybir

ALU = mybir.AluOpType
ACT = mybir.ActivationFunctionType
AX = mybir.AxisListType
F32 = mybir.dt.float32
F32R = mybir.dt.float32r

P = 128
D = 1024
KD = D // P
S = 512
NT = S // P
HD = 64
NH = 8
C = 64
NCH = S // C
LEVELS = int(math.log2(C))
FF1, FF2 = 4096, 2816
TOPK = 128
ROT = 16
NEG = -1e30
BUCKETS, WINDOW = 32, 128
RLEN = 384
EPS = 1e-6
GN_EPS = 64e-5
EHALF = math.exp(-0.5)

CST = {}
_at = 0
for _name, _w in (("ident", P), ("ones", P), ("pair", P), ("swap", P), ("level", P * LEVELS),
                  ("before", P), ("upto", P), ("future", P), ("past_t", P), ("after_t", P),
                  ("inside", S), ("freq", 2), ("onehot", RLEN)):
    CST[_name] = (_at, _at + _w)
    _at += _w
CST_W = _at


def t5_bucket(n):
    exact = BUCKETS // 2
    if n < exact:
        return n
    f = np.float32
    large = exact + int(f(np.log(f(n) / f(exact))) / f(math.log(P / exact)) * f(BUCKETS - exact))
    return min(large, BUCKETS - 1)


def constants():
    c = np.zeros((P, CST_W), np.float32)

    def put(name, a):
        lo, hi = CST[name]
        c[:a.shape[0], lo:hi] = a

    i = np.arange(P)
    row, col = i[:, None], i[None, :]
    same = row // C == col // C
    put("ident", np.eye(P))
    put("ones", np.ones((P, P)))
    put("pair", row // HD == col // HD)
    half = ROT // 2
    swap = np.zeros((P, P))
    for m in range(P):
        if m % HD < ROT:
            swap[m - m % HD + (m % HD + half) % ROT, m] = 1
    put("swap", swap)
    put("level", np.concatenate(
        [(row >> l + 1 == col >> l + 1) & (row >> l & 1 == 1) & (col >> l & 1 == 0) for l in range(LEVELS)], 1))
    put("before", same & (row < col))
    put("upto", same & (row <= col))
    put("future", np.where(col > row, NEG, 0))
    put("past_t", row < col)
    put("after_t", row >= col)
    put("inside", np.tile(np.arange(S) % C != 0, (P, 1)))
    inv = np.float32(500000.0) ** (-np.arange(0, ROT, 2, dtype=np.float32) / np.float32(ROT))
    f = np.zeros((P, 2), np.float32)
    for m in range(P):
        if m % HD < ROT:
            f[m] = inv[m % HD % half], (-1 if m % HD < half else 1)
    put("freq", f)
    hot = np.zeros((BUCKETS + 1, RLEN), np.float32)
    for x in range(RLEN):
        n = 2 * P - 1 - x
        if 0 <= n < WINDOW:
            hot[t5_bucket(n), x] = 1
        else:
            hot[BUCKETS, x] = NEG
    put("onehot", hot)
    return c


class Signal:

    def __init__(self, handle):
        self.h, self.n = handle, 0

    def by(self, ins):
        ins.then_inc(self.h, 1)
        self.n += 1
        return ins


class Chain:

    def __init__(self, eng, signal, turn=None):
        self.eng, self.s, self.turn = eng, signal, turn

    def __call__(self, ins):
        self.s.by(ins)
        self.eng.wait_ge(self.s.h, self.s.n if self.turn is None else self.turn + self.s.n)


def program(nc, a, out):
    whole = ExitStack()
    with whole:
        _program(nc, a, out, whole)


def _program(nc, a, out, whole):
    names = [0]

    def sb(ctx, name, shape, dt=F32):
        names[0] += 1
        return ctx.enter_context(nc.sbuf_tensor(f"{name}_{names[0]}", shape, dt))

    here, stale, clear = [], [], []

    def sig(name, kept=False):
        names[0] += 1
        h = clear.pop() if clear and not kept else whole.enter_context(nc.semaphore(f"{name}_{names[0]}"))
        if not kept:
            here.append(h)
        return Signal(h)

    @contextmanager
    def stage(params=None):
        with nc.Block() as block:
            yield block
            old = list(stale)

            @block.gpsimd
            def _(pool):
                for h in old:
                    pool.sem_clear(h)
                if params:
                    params(pool)
        clear.extend(stale)
        stale[:] = here
        here.clear()

    banks = whole.enter_context(nc.psum_tensor("banks", [P, 8, 512], F32))
    bank = [banks[:, i, :] for i in range(8)]

    scratch = nc.dram_tensor("scratch", (NH, P, RLEN), F32, kind="Internal").ap()
    xT = sb(whole, "xT", [P, KD, S])
    cst = sb(whole, "cst", [P, 3 * P])
    ident, ones, pair = (cst[:, i * P:(i + 1) * P] for i in range(3))
    NROW = 116
    pcol = sb(whole, "pcol", [P, NROW])
    conv1 = sb(whole, "conv1", [P, 4, 2 * FF1 // P])
    conv2 = [sb(whole, f"conv2{i}", [P, 4, 2 * FF2 // P]) for i in range(2)]

    vec, rows_of = {}, []
    at = 0
    for name, ap in (("norm_mix_pre", a["norm_mix_pre"]), ("norm_mix_post", a["norm_mix_post"]),
                     ("norm_ffn_pre", a["norm_ffn_pre"]), ("norm_ffn_post", a["norm_ffn_post"]),
                     ("mix", a["rwkv_shift_mix"]), ("w0", a["w0"]), ("a0", a["a0"]), ("k_k", a["k_k"]),
                     ("k_a", a["k_a"]), ("r_k", a["r_k"].rearrange("a h d -> a (h d)")),
                     ("ln_g", a["ln_x_g"]), ("ln_b", a["ln_x_b"]),
                     ("attn_norm", a["attn_norm_2"].rearrange("(o l) d -> o (l d)", o=1)),
                     ("ffn_norm", a["ffn_norm_2"].rearrange("(o l) d -> o (l d)", o=1)),
                     ("final_norm", a["final_norm_2"].rearrange("(o d) -> o d", o=1)),
                     ("subln", a["ev_subln_2"]), ("kv_norm", a["od_kv_norm_2"])):
        n = ap.shape[1] // P
        vec[name] = at
        rows_of.append((at, n, ap.rearrange("o (m p) -> (o m) p", p=P)))
        at += n
    assert at == NROW, at

    def col(name, m=0):
        return pcol[:, vec[name] + m:vec[name] + m + 1]

    RAW, CUT, AHEAD = 2, 4, 2
    LOADED = RAW + AHEAD
    raw = [sb(whole, f"raw{i}", [P, KD, P]) for i in range(RAW)]
    whi = [sb(whole, f"whi{i}", [P, KD, P], F32R) for i in range(CUT)]
    wlo = [sb(whole, f"wlo{i}", [P, KD, P], F32R) for i in range(CUT)]
    loaded = [sig(f"w_loaded{i}", True) for i in range(RAW)]
    w_hi, w_lo, w_used = (sig(n, True) for n in ("w_hi", "w_lo", "w_used"))

    def rows(w, r0, nr, c0, nc_=P):
        return w[r0:r0 + nr * P, bass.ds(c0, nc_)].rearrange("(k p) n -> p k n", p=P)

    def tile_of(w, c0, r0=0, nr=KD):
        return lambda slot: [(slot[:, 0:nr, :], rows(w, r0, nr, c0))]

    def twice(w, c0):
        return lambda slot: [(slot[:, :, 0:HD], rows(w, 0, KD, c0, HD)), (slot[:, :, HD:P], rows(w, 0, KD, c0, HD))]

    w1, wo1 = a["w_in"][0], a["w_out"][0]
    wu1, wd1 = a["w_ffn_up"][0], a["w_ffn_down"][0]
    we, woe = a["ev_w_in_2"][0], a["ev_w_out_2"][0]
    wd, wod = a["od_w_in_2"][0], a["od_w_out_2"][0]
    wu2, wd2 = a["ffn_w_in_2"], a["ffn_w_out_2"]

    in1 = [tile_of(w1, 128 * m) for m in range(4)] + [twice(w1, 512), twice(w1, 576), tile_of(w1, 640)] \
        + [tile_of(w1, 768 + 128 * m) for m in range(14)]
    in_ev = [tile_of(we, c0) for c0 in [1536] + [o + 128 * m for o in (1024, 0, 512, 2568, 1544, 2056) for m in range(4)]]
    in_od = [tile_of(wd, 656 + 128 * m) for m in range(2)] + [twice(wd, 916), tile_of(wd, 912)] \
        + [tile_of(wd, 128 * m) for m in range(4)] + [twice(wd, 640), tile_of(wd, 512)] \
        + [tile_of(wd, 980 + 128 * m) for m in range(12)]

    def up_slots(w, ff, first, pairs):
        return [tile_of(w, o + 128 * (first + m)) for m in range(pairs) for o in (0, ff)]

    def down_slots(w, first, parts):
        return [tile_of(w, 128 * m, 128 * (first + k), n) for m in range(KD) for k, n in parts]

    PARTS1 = [(0, 8), (8, 8)]
    PARTS2 = [(0, 6), (6, 6), (12, 5), (17, 5)]
    plan = list(in1) + [tile_of(wo1, 128 * m) for m in range(8)]
    for ch in range(2):
        plan += up_slots(wu1, FF1, 16 * ch, 16) + down_slots(wd1, 16 * ch, PARTS1)
    for layer in range(2):
        plan += (in_ev, in_od)[layer] + [tile_of((woe, wod)[layer], 128 * m) for m in range(8)]
        plan += up_slots(wu2[layer], FF2, 0, 22) + down_slots(wd2[layer], 0, PARTS2)
    state = {"s": 0}

    def load(sp, s):
        if s >= len(plan):
            return
        if s >= RAW:
            sp.wait_ge(w_lo.h, s - RAW + 1)
        for dst, src in plan[s](raw[s % RAW]):
            sp.dma_start(dst, src).then_inc(loaded[s % RAW].h, 16)

    arrived = {}
    for s_ in range(len(plan)):
        n_ = len(plan[s_](raw[s_ % RAW]))
        arrived[s_] = (arrived[s_ - RAW] if s_ >= RAW else 0) + 16 * n_

    height = [plan[s_](raw[s_ % RAW])[0][0].shape[1] for s_ in range(len(plan))]

    def split_hi(act, s):
        if s >= len(plan):
            return
        act.wait_ge(loaded[s % RAW].h, arrived[s])
        if s >= CUT:
            act.wait_ge(w_used.h, s - CUT + 1)
        n = height[s]
        w_hi.by(act.activation(whi[s % CUT][:, 0:n, :], raw[s % RAW][:, 0:n, :], ACT.Copy))

    def lower(pool, b, c, n):
        return pool.tensor_tensor(wlo[c][:, 0:n, :], raw[b][:, 0:n, :], whi[c][:, 0:n, :].bitcast(F32), ALU.subtract)

    def split_lo(pool, s):
        if s >= len(plan):
            return
        pool.wait_ge(w_hi.h, s + 1)
        w_lo.by(lower(pool, s % RAW, s % CUT, height[s]))

    def three_passes(pe, acc, b, n, hi, lo, first, last, ready=None):
        for k in range(n):
            if ready:
                pe.wait_ge(ready.h, k + 1)
            pe.matmul(acc, whi[b][:, k, :], hi(k), start=first and k == 0, stop=False)
            pe.matmul(acc, whi[b][:, k, :], lo(k), start=False, stop=False)
            mm = pe.matmul(acc, wlo[b][:, k, :], hi(k), start=False, stop=last and k == n - 1)
        return mm

    act_chain, dve_chain = sig("act_chain", True), sig("dve_chain", True)

    def cst_dma(sp, dst, name, signal, rows_=P):
        lo, hi = CST[name]
        sp.dma_start(dst, a["cst"][0:rows_, lo:hi]).then_inc(signal.h, 16)

    def setup():
        with ExitStack() as ctx:
            xin = sb(ctx, "xin", [P, NT, D])
            prow = sb(ctx, "prow", [P, P])
            c1row = sb(ctx, "c1row", [2 * FF1 // P, 4, P])
            c2row = sb(ctx, "c2row", [2 * FF2 // P, 2, 4, P])
            s_x, s_p, turned, taken = sig("s_x"), sig("s_p", True), sig("turned"), sig("taken")

            def params(pool):
                for first, n, ap in rows_of:
                    pool.dma_start(prow[first:first + n, :], ap).then_inc(s_p.h, 16)
                for t in range(3):
                    pool.dma_start(c1row[:, t, :], a["conv_w"][0, t:t + 1, :].rearrange("o (m p) -> (o m) p", p=P)).then_inc(s_p.h, 16)
                pool.dma_start(c1row[:, 3, :], a["conv_b"][0:1, :].rearrange("o (m p) -> (o m) p", p=P)).then_inc(s_p.h, 16)
                for l in range(2):
                    for t in range(3):
                        pool.dma_start(c2row[:, l, t, :], a["ffn_conv_w_2"][l, t:t + 1, :].rearrange("o (m p) -> (o m) p", p=P)).then_inc(s_p.h, 16)
                    pool.dma_start(c2row[:, l, 3, :], a["ffn_conv_b_2"][l:l + 1, :].rearrange("o (m p) -> (o m) p", p=P)).then_inc(s_p.h, 16)
                for s in range(AHEAD):
                    split_lo(pool, s)
            block = ctx.enter_context(stage(params))

            @block.sync
            def _(sp):
                sp.dma_start(cst[:, :], a["cst"][:, 0:3 * P]).then_inc(s_x.h, 16)
                sp.dma_start(xin[:, :, :], a["x"][0].rearrange("(t p) d -> p t d", p=P)).then_inc(s_x.h, 16)
                for s in range(LOADED):
                    load(sp, s)

            n_params = 16 * (len(rows_of) + 12)

            @block.tensor
            def _(pe):
                pe.wait_ge(s_x.h, 32)
                for k in range(KD):
                    for t in range(NT):
                        mm = pe.transpose(bank[k][:, t * P:(t + 1) * P], xin[:, t, k * P:(k + 1) * P], ident)
                    mm.then_inc(turned.h, 1)
                pe.wait_ge(s_p.h, n_params)
                pe.wait_ge(taken.h, 4)
                mm = pe.transpose(bank[0][:, 0:NROW], prow[0:NROW, :], ident[0:NROW, 0:NROW])
                mm.then_inc(turned.h, 1)
                n1, n2 = 2 * FF1 // P, 2 * FF2 // P
                for t in range(4):
                    mm = pe.transpose(bank[1][:, t * n1:(t + 1) * n1], c1row[:, t, :], ident[0:n1, 0:n1])
                mm.then_inc(turned.h, 1)
                for l in range(2):
                    for t in range(4):
                        mm = pe.transpose(bank[2 + l][:, t * n2:(t + 1) * n2], c2row[:, l, t, :], ident[0:n2, 0:n2])
                    mm.then_inc(turned.h, 1)

            @block.vector
            def _(dve):
                for k in range(KD):
                    dve.wait_ge(turned.h, k + 1)
                    dve.tensor_copy(xT[:, k, :], bank[k][:, :]).then_inc(taken.h, 1)
                n1, n2 = 2 * FF1 // P, 2 * FF2 // P
                dve.wait_ge(turned.h, KD + 1)
                dve.tensor_copy(pcol[:, :], bank[0][:, 0:NROW])
                dve.wait_ge(turned.h, KD + 2)
                dve.tensor_copy(conv1[:, :, :].rearrange("p t n -> p (t n)"), bank[1][:, 0:4 * n1])
                dve.wait_ge(turned.h, KD + 4)
                for l in range(2):
                    dve.tensor_copy(conv2[l][:, :, :].rearrange("p t n -> p (t n)"), bank[2 + l][:, 0:4 * n2])

            @block.scalar
            def _(act):
                for s in range(AHEAD):
                    split_hi(act, s)

    def norm(src, n, g, gname_m, width, eps, finish, groups=1, stat=None):
        stat = ones if stat is None else stat
        with ExitStack() as ctx:
            sq = sb(ctx, "sq", [P, n, S])
            ms = sb(ctx, "ms", [P, groups, S])
            rt = sb(ctx, "rt", [P, groups, S])
            rstd = sb(ctx, "rstd", [P, groups, S])
            squared, summed, meaned, rooted = sig("squared"), sig("summed"), sig("meaned"), sig("rooted")
            per = n // groups
            block = ctx.enter_context(stage())

            @block.sync
            def _(sp):
                pass

            @block.scalar
            def _(act):
                for k in range(n):
                    squared.by(act.activation(sq[:, k, :], src(k), ACT.Square))
                for q in range(groups):
                    act.wait_ge(meaned.h, q + 1)
                    rooted.by(act.activation(rt[:, q, :], ms[:, q, :], ACT.Sqrt))

            @block.tensor
            def _(pe):
                for k in range(n):
                    pe.wait_ge(squared.h, k + 1)
                    mm = pe.matmul(bank[k // per][:, :], stat, sq[:, k, :], start=k % per == 0, stop=k % per == per - 1)
                    if k % per == per - 1:
                        summed.by(mm)

            @block.vector
            def _(dve):
                chain = Chain(dve, dve_chain)
                for q in range(groups):
                    dve.wait_ge(summed.h, q + 1)
                    meaned.by(dve.tensor_scalar(ms[:, q, :], bank[q][:, :], 1.0 / width, eps, ALU.mult, ALU.add))
                for q in range(groups):
                    dve.wait_ge(rooted.h, q + 1)
                    chain(dve.reciprocal(rstd[:, q, :], rt[:, q, :]))
                for k in range(n):
                    finish(dve, chain, k, rstd[:, k // per, :])

    class Lead:

        def __init__(self, scale, hi, lo, scratch, src=None, src_scale=None):
            self.scale, self.hi, self.lo, self.src, self.src_scale = scale, hi, lo, src, src_scale
            self.sq, self.h, (self.ms, self.rt, self.rstd, self.y) = scratch[0:2], scratch[2:4], scratch[4:8]
            self.squared, self.summed, self.meaned, self.rooted = sig("squared"), sig("summed"), sig("meaned"), sig("rooted")
            self.updated, self.scaled, self.uppered, self.ready = sig("updated"), sig("scaled"), sig("uppered"), sig("ready")
            self.rounds = 2 if src is not None else 1

        def pe(self, pe):
            for r in range(self.rounds):
                for k in range(KD):
                    pe.wait_ge(self.squared.h, r * KD + k + 1)
                    pe.matmul(bank[7 - r][:, :], ones, self.sq[k % 2], start=k == 0, stop=k == KD - 1).then_inc(self.summed.h, 1)

        def act(self, act):
            for r in range(self.rounds):
                post = r < self.rounds - 1
                for k in range(KD):
                    n = r * KD + k
                    if n >= 2:
                        act.wait_ge(self.summed.h, n - 1)
                    if r == 1:
                        act.wait_ge(self.updated.h, k + 1)
                    act.activation(self.sq[k % 2], self.src[:, k, :] if post else xT[:, k, :], ACT.Square).then_inc(self.squared.h, 1)
                act.wait_ge(self.meaned.h, r + 1)
                act.activation(self.rt, self.ms, ACT.Sqrt).then_inc(self.rooted.h, 1)
            for k in range(KD):
                act.wait_ge(self.scaled.h, k + 1)
                act.activation(self.hi[:, k, :], self.h[k % 2], ACT.Copy).then_inc(self.uppered.h, 1)

        def dve(self, dve, chain):
            for r in range(self.rounds):
                dve.wait_ge(self.summed.h, (r + 1) * KD)
                dve.tensor_scalar(self.ms, bank[7 - r][:, :], 1.0 / D, EPS, ALU.mult, ALU.add).then_inc(self.meaned.h, 1)
                dve.wait_ge(self.rooted.h, r + 1)
                chain(dve.reciprocal(self.rstd, self.rt))
                if r < self.rounds - 1:
                    for k in range(KD):
                        chain(dve.scalar_tensor_tensor(self.y, self.src[:, k, :], self.src_scale(k), self.rstd, ALU.mult, ALU.mult))
                        dve.tensor_tensor(xT[:, k, :], self.y, xT[:, k, :], ALU.add).then_inc(self.updated.h, 1)
                        dve.wait_ge(self.updated.h, k + 1)
            for k in range(KD + 1):
                if k < KD:
                    dve.scalar_tensor_tensor(self.h[k % 2], xT[:, k, :], self.scale(k), self.rstd, ALU.mult, ALU.mult).then_inc(self.scaled.h, 1)
                if k >= 1:
                    dve.wait_ge(self.uppered.h, k)
                    dve.tensor_tensor(self.lo[:, k - 1, :], self.h[(k - 1) % 2], self.hi[:, k - 1, :].bitcast(F32), ALU.subtract)\
                       .then_inc(self.ready.h, 1)
                    dve.wait_ge(self.ready.h, k)

    class Cut:

        def __init__(self, src, hi, lo):
            self.src, self.hi, self.lo, self.uppered, self.ready = src, hi, lo, sig("uppered"), sig("ready")

        def pe(self, pe):
            pass

        def act(self, act):
            for k in range(KD):
                act.activation(self.hi[:, k, :], self.src[:, k, :], ACT.Copy).then_inc(self.uppered.h, 1)

        def dve(self, dve, chain):
            for k in range(KD):
                dve.wait_ge(self.uppered.h, k + 1)
                dve.tensor_tensor(self.lo[:, k, :], self.src[:, k, :], self.hi[:, k, :].bitcast(F32), ALU.subtract).then_inc(self.ready.h, 1)

    class Side:

        def sp(self, sp):
            pass

        def first_pe(self, pe):
            pass

        def pe(self, pe, free, m):
            pass

        def first_act(self, act):
            pass

        def act(self, act, m):
            pass

        def dve(self, dve, chain, free):
            pass

    class Rotate:

        def __init__(self, ctx, cosT, sinT):
            self.sw, self.t = sb(ctx, "sw", [P, P]), sb(ctx, "rotated", [P, 2, S])
            self.cosT, self.sinT, self.n, self.m = cosT, sinT, 0, 0
            self.got, self.swapped, self.used, self.turned = sig("got"), sig("swapped"), sig("used"), sig("turned")

        def sp(self, sp):
            cst_dma(sp, self.sw[:, :], "swap", self.got)

        def pe(self, pe, x):
            n, self.n = self.n, self.n + 1
            if n == 0:
                pe.wait_ge(self.got.h, 16)
            if n >= 3:
                pe.wait_ge(self.used.h, n - 2)
            pe.matmul(bank[4 + n % 3][:, :], self.sw[:, :], x, start=True, stop=True).then_inc(self.swapped.h, 1)

        def dve(self, dve, x):
            n, self.m = self.m, self.m + 1
            dve.wait_ge(self.swapped.h, n + 1)
            if n >= 2:
                dve.wait_ge(self.turned.h, 2 * n - 2)
            self.used.by(dve.tensor_tensor(self.t[:, n % 2, :], bank[4 + n % 3][:, :], self.sinT[:, :], ALU.mult))
            self.turned.by(dve.tensor_tensor(x, x, self.cosT[:, :], ALU.mult))
            dve.wait_ge(self.used.h, n + 1)
            dve.wait_ge(self.turned.h, 2 * n + 1)
            self.turned.by(dve.tensor_tensor(x, x, self.t[:, n % 2, :], ALU.add))

    def project(n, hi, lo, put, post=None, lead=None, side=None):
        s0 = state["s"]
        done, free = sig("done"), sig("free")
        side = side or Side()
        with ExitStack() as ctx:
            def pool_part(pool):
                for m in range(n):
                    split_lo(pool, s0 + m + AHEAD)
            block = ctx.enter_context(stage(pool_part))

            @block.sync
            def _(sp):
                side.sp(sp)
                for m in range(n):
                    load(sp, s0 + LOADED + m)

            @block.tensor
            def _(pe):
                if lead:
                    lead.pe(pe)
                side.first_pe(pe)
                for m in range(n):
                    s = s0 + m
                    pe.wait_ge(w_lo.h, s + 1)
                    if m >= 4:
                        pe.wait_ge(free.h, m - 3)
                    w_used.by(three_passes(pe, bank[m % 4][:, :], s % CUT, KD, lambda k: hi[:, k, :], lambda k: lo[:, k, :], True, True,
                                           lead.ready if lead and m == 0 else None))
                    if m >= 1:
                        side.pe(pe, free, m - 1)
                side.pe(pe, free, n - 1)

            @block.scalar
            def _(act):
                if lead:
                    lead.act(act)
                side.first_act(act)
                for m in range(n):
                    split_hi(act, s0 + m + AHEAD)
                    if put:
                        act.wait_ge(w_used.h, s0 + m + 1)
                        free.by(put(act, m, bank[m % 4][:, :]))
                        side.act(act, m)

            @block.vector
            def _(dve):
                chain = Chain(dve, dve_chain)
                if lead:
                    lead.dve(dve, chain)
                side.dve(dve, chain, free)
                for m in range(n if post else 0):
                    if not put:
                        dve.wait_ge(w_used.h, s0 + m + 1)
                        free.by(post(dve, chain, m, bank[m % 4][:, :]))
                    else:
                        dve.wait_ge(free.h, m + 1)
                        post(dve, chain, m)
        state["s"] += n

    def ffn(w_up, ff, w_down, conv, first, pairs, parts, hi, lo, func, add, acc_to, make_lead=None):
        with ExitStack() as ctx:
            ghi = sb(ctx, "ghi", [P, pairs, S], F32R)
            glo = sb(ctx, "glo", [P, pairs, S], F32R)
            cb = [sb(ctx, f"cb{j}", [P, S]) for j in range(4)]
            gate = [sb(ctx, f"gate{j}", [P, S]) for j in range(2)]
            gv = [sb(ctx, f"gv{j}", [P, S]) for j in range(2)]
            lead = make_lead([t[:, :] for t in cb + gate + gv]) if make_lead else None
            tapped, conved, gated, products, upper, split_ = (sig(n) for n in ("tapped", "conved", "gated", "products", "upper", "split"))
            taken = sig("taken")
            chain0 = dve_chain.n
            ff_tiles = ff // P
            up0, ups = state["s"], pairs // 2
            half = [0, ff_tiles, 1, ff_tiles + 1]
            dn0 = up0 + 4 * ups
            mts = 4 // len(parts)
            slots = [(mt, k0, n) for mt in range(mts) for k0, n in parts]
            dns = KD // mts
            end = dn0 + 4 * dns

            PER = 4 // RAW * 16

            def hi_in_loop(act, s, i, n):
                act.wait_ge(loaded[s % RAW].h, i * PER + arrived[s])
                act.wait_ge(w_used.h, i * 4 + (s - CUT + 1))
                act.activation(whi[s % CUT][:, 0:n, :], raw[s % RAW][:, 0:n, :], ACT.Copy).then_inc(w_hi.h, 1)

            def lo_in_loop(pool, s, i, n):
                pool.wait_ge(w_hi.h, i * 4 + (s + 1))
                lower(pool, s % RAW, s % CUT, n).then_inc(w_lo.h, 1)

            def pool_part(pool):
                with pool.Fori(0, ups - 1) as i:
                    for j in range(4):
                        lo_in_loop(pool, up0 + j + AHEAD, i, KD)
                w_lo.n += 4 * (ups - 1)
                for s in range(dn0 - 4 + AHEAD, dn0 + AHEAD):
                    split_lo(pool, s)
                with pool.Fori(0, dns - 1) as i:
                    for j in range(4):
                        lo_in_loop(pool, dn0 + j + AHEAD, i, height[dn0 + j + AHEAD])
                w_lo.n += 4 * (dns - 1)
                for s in range(end - 4 + AHEAD, end + AHEAD):
                    split_lo(pool, s)
            block = ctx.enter_context(stage(pool_part))

            @block.sync
            def _(sp):
                def load_turns(s0, turns, src):
                    with sp.Fori(1, turns) as i:
                        for j in range(4):
                            sp.wait_ge(w_lo.h, i * 4 + (s0 + j - RAW + 1))
                            b, n = (s0 + j) % RAW, height[s0 + j]
                            sp.dma_start(raw[b][:, 0:n, :], src(i, j, n)).then_inc(loaded[b].h, 16)
                load_turns(up0, ups, lambda i, j, n: rows(w_up, 0, n, i * (2 * P) + P * (first + half[j])))
                for s in range(dn0, dn0 + LOADED):
                    load(sp, s)
                load_turns(dn0, dns, lambda i, j, n: rows(w_down, P * (first + slots[j][1]), n, i * (mts * P) + P * slots[j][0]))
                for s in range(end, end + LOADED):
                    load(sp, s)

            @block.tensor
            def _(pe):
                def up(i, hold):
                    for j in range(4):
                        pe.wait_ge(w_lo.h, i * 4 + (up0 + j + 1))
                        if hold:
                            pe.wait_ge(conved.h, i * 4 + (j - 3))
                        three_passes(pe, bank[j][:, :], (up0 + j) % CUT, KD, lambda k: hi[:, k, :], lambda k: lo[:, k, :], True, True,
                                     lead.ready if lead and not hold and j == 0 else None).then_inc(w_used.h, 1)
                if lead:
                    lead.pe(pe)
                up(0, False)
                with pe.Fori(1, ups) as i:
                    up(i, True)

                def down(i, hold):
                    for j, (mt, k0, n) in enumerate(slots):
                        pe.wait_ge(w_lo.h, i * 4 + (dn0 + j + 1))
                        if hold and k0 == 0:
                            pe.wait_ge(taken.h, (i - 1) * mts + (mt + 1))
                        if not hold:
                            pe.wait_ge(split_.h, k0 + n)
                        three_passes(pe, bank[4 + mt][:, :], (dn0 + j) % CUT, n, lambda k: ghi[:, k0 + k, :],
                                     lambda k: glo[:, k0 + k, :], k0 == 0, k0 + n == pairs).then_inc(w_used.h, 1)
                down(0, False)
                with pe.Fori(1, dns) as i:
                    down(i, True)

            @block.scalar
            def _(act):
                def turn(i, hold, last=False):
                    for j in range(4):
                        if last:
                            split_hi(act, dn0 - 4 + j + AHEAD)
                        else:
                            hi_in_loop(act, up0 + j + AHEAD, i, KD)
                        if j % 2 == 1:
                            act.wait_ge(conved.h, i * 4 + j)
                            act.activation(gate[j // 2][:, :], cb[j - 1][:, :], func).then_inc(gated.h, 1)
                        act.wait_ge(w_used.h, i * 4 + (up0 + j + 1))
                        if hold:
                            act.wait_ge(products.h, i * 2 + (j // 2 - 1))
                        c = i * 2 + (first + half[j])
                        act.activation(cb[j][:, :], bank[j][:, :], ACT.Identity,
                                       scale=conv[:, 2, bass.ds(c, 1)], bias=conv[:, 3, bass.ds(c, 1)])\
                           .then_inc(tapped.h, 1)
                if lead:
                    lead.act(act)
                turn(0, False)
                with act.Fori(1, ups - 1) as i:
                    turn(i, True)
                w_hi.n += 4 * (ups - 1)
                turn(ups - 1, True, True)
                with act.Fori(0, dns - 1) as i:
                    for j in range(4):
                        hi_in_loop(act, dn0 + j + AHEAD, i, height[dn0 + j + AHEAD])
                w_hi.n += 4 * (dns - 1)
                for s in range(end - 4 + AHEAD, end + AHEAD):
                    split_hi(act, s)

            @block.vector
            def _(dve):
                if lead:
                    lead.dve(dve, Chain(dve, dve_chain))
                chain0 = dve_chain.n

                def turn(i, base):
                    chain = Chain(dve, dve_chain, base)
                    for j in range(4):
                        dve.wait_ge(tapped.h, i * 4 + (j + 1))
                        c = i * 2 + (first + half[j])
                        chain(dve.scalar_tensor_tensor(cb[j][:, 1:S], bank[j][:, 0:S - 1], conv[:, 1, bass.ds(c, 1)],
                                                       cb[j][:, 1:S], ALU.mult, ALU.add))
                        dve.scalar_tensor_tensor(cb[j][:, 2:S], bank[j][:, 0:S - 2], conv[:, 0, bass.ds(c, 1)],
                                                 cb[j][:, 2:S], ALU.mult, ALU.add).then_inc(conved.h, 1)
                        if j % 2 == 1:
                            q = j // 2
                            dve.wait_ge(conved.h, i * 4 + (j + 1))
                            dve.wait_ge(gated.h, i * 2 + (q + 1))
                            dve.tensor_tensor(gv[q][:, :], gate[q][:, :], cb[j][:, :], ALU.mult).then_inc(products.h, 1)
                            dve.wait_ge(products.h, i * 2 + (q + 1))
                            dve.tensor_copy(ghi[:, i * 2 + q, :], gv[q][:, :]).then_inc(upper.h, 1)
                            dve.wait_ge(upper.h, i * 2 + (q + 1))
                            dve.tensor_tensor(glo[:, i * 2 + q, :], gv[q][:, :], ghi[:, i * 2 + q, :].bitcast(F32), ALU.subtract)\
                               .then_inc(split_.h, 1)
                            dve.wait_ge(split_.h, i * 2 + (q + 1))
                turn(0, 0)
                per = dve_chain.n - chain0
                dve_chain.n = chain0
                with dve.Fori(1, ups) as i:
                    turn(i, i * per)
                dve_chain.n = chain0 + per * ups
                with dve.Fori(0, dns) as i:
                    for j, (mt, k0, n) in enumerate(slots):
                        if k0 + n == pairs:
                            dve.wait_ge(w_used.h, i * 4 + (dn0 + j + 1))
                            m = i * mts + mt
                            if add:
                                dve.tensor_tensor(acc_to[:, m, :], bank[4 + mt][:, :], acc_to[:, m, :], ALU.add).then_inc(taken.h, 1)
                            else:
                                dve.tensor_copy(acc_to[:, m, :], bank[4 + mt][:, :]).then_inc(taken.h, 1)
            w_used.n += end - up0
            state["s"] = end

    def attend(units, dst_of, sink=None, lam=None):
        U, G = len(units), len(units[0][0])
        NB = 4 // G
        scored, ready, exped, normed, flipped, ptaken, weighed, otaken = (
            sig(n) for n in ("scored", "ready", "exped", "normed", "flipped", "ptaken", "weighed", "otaken"))
        with ExitStack() as ctx:
            sm = [sb(ctx, f"sm{i}", [P, G, S]) for i in range(2)]
            ex = [sb(ctx, f"ex{i}", [P, G, S]) for i in range(3)]
            pt = [sb(ctx, f"pt{i}", [P, S]) for i in range(2)]
            mx = [sb(ctx, f"mx{i}", [P, 5 * G]) for i in range(3)]
            block = ctx.enter_context(stage())

            def f(i, what, g=None):
                o = ("neg", "sum", "sink", "den", "inv").index(what) * G
                return mx[i % 3][:, o:o + G] if g is None else mx[i % 3][:, o + g:o + g + 1]

            @block.tensor
            def _(pe):
                for i in range(U + 3):
                    if i < U:
                        maps, w = units[i][0], units[i][1]
                        if i >= NB:
                            pe.wait_ge(ready.h, i - NB + 1)
                        for g, products in enumerate(maps):
                            for n, (q, k, c0) in enumerate(products):
                                mm = pe.matmul(bank[i % NB * G + g][:, c0:w], q, k, start=n == 0, stop=n == len(products) - 1,
                                               skip_group_check=len(products) > 1)
                        mm.then_inc(scored.h, 1)
                    u = i - 2
                    if 0 <= u < U:
                        pe.wait_ge(normed.h, u + 1)
                        if u >= 2:
                            pe.wait_ge(ptaken.h, u - 1)
                        for b in range(units[u][1] // P):
                            mm = pe.transpose(bank[4 + u % 2][:, b * P:(b + 1) * P], ex[u % 3][:, 0, b * P:(b + 1) * P], ident)
                        mm.then_inc(flipped.h, 1)
                    u = i - 3
                    if 0 <= u < U:
                        _, w, _, values, (r0, r1) = units[u]
                        pe.wait_ge(ptaken.h, u + 1)
                        if u >= 2:
                            pe.wait_ge(otaken.h, u - 1)
                        for b, v in enumerate(values):
                            mm = pe.matmul(bank[6 + u % 2][r0:r1, 0:P], v, pt[u % 2][:, b * P:(b + 1) * P],
                                           start=b == 0, stop=b == len(values) - 1)
                        mm.then_inc(weighed.h, 1)

            @block.vector
            def _(dve):
                chain = Chain(dve, dve_chain)
                for i in range(U + 1):
                    if i < U:
                        _, w, bias, _, _ = units[i]
                        dve.wait_ge(scored.h, i + 1)
                        if i >= 2:
                            dve.wait_ge(exped.h, i - 1)
                        for g in range(G):
                            ins = dve.tensor_tensor_reduce(sm[i % 2][:, g, 0:w], bank[i % NB * G + g][:, 0:w], bias, -HD ** -0.5,
                                                           3e38 if sink is None else sink(i)[1], ALU.add, ALU.min, f(i, "neg", g))
                        ready.by(ins)
                    u = i - 1
                    if 0 <= u < U:
                        w = units[u][1]
                        dve.wait_ge(exped.h, u + 1)
                        den = f(u, "sum")
                        if sink is not None:
                            chain(dve.tensor_tensor(f(u, "den"), f(u, "sum"), f(u, "sink"), ALU.add))
                            den = f(u, "den")
                        chain(dve.reciprocal(f(u, "inv"), den))
                        e = ex[u % 3]
                        if G == 1:
                            normed.by(dve.tensor_scalar(e[:, 0, 0:w], e[:, 0, 0:w], f(u, "inv"), None, ALU.mult))
                        else:
                            dve.tensor_scalar(f(u, "den", 1), f(u, "inv", 1), lam, None, ALU.mult)
                            chain(dve.tensor_scalar(e[:, 0, 0:w], e[:, 0, 0:w], f(u, "inv", 0), None, ALU.mult))
                            normed.by(dve.scalar_tensor_tensor(e[:, 0, 0:w], e[:, 1, 0:w], f(u, "den", 1), e[:, 0, 0:w],
                                                               ALU.mult, ALU.add))

            @block.scalar
            def _(act):
                for i in range(U + 3):
                    if i < U:
                        w = units[i][1]
                        act.wait_ge(ready.h, i + 1)
                        if i >= 3:
                            act.wait_ge(flipped.h, i - 2)
                        if sink is not None:
                            act.activation(f(i, "sink"), sink(i)[0], ACT.Exp, bias=f(i, "neg"))
                        for g in range(G):
                            ins = act.activation(ex[i % 3][:, g, 0:w], sm[i % 2][:, g, 0:w], ACT.Exp, bias=f(i, "neg", g), scale=-1.0,
                                                 accum_out=f(i, "sum", g))
                        exped.by(ins)
                    u = i - 2
                    if 0 <= u < U:
                        w = units[u][1]
                        act.wait_ge(flipped.h, u + 1)
                        if u >= 2:
                            act.wait_ge(weighed.h, u - 1)
                        ptaken.by(act.activation(pt[u % 2][:, 0:w], bank[4 + u % 2][:, 0:w], ACT.Copy))
                    u = i - 3
                    if 0 <= u < U:
                        r0, r1 = units[u][4]
                        act.wait_ge(weighed.h, u + 1)
                        otaken.by(act.activation(dst_of(u), bank[6 + u % 2][r0:r1, 0:P], ACT.Copy))

    def turn(pairs):
        flipped, taken = sig("flipped"), sig("taken")
        with ExitStack() as ctx:
            block = ctx.enter_context(stage())

            @block.tensor
            def _(pe):
                for n, (_, srcs) in enumerate(pairs):
                    if n >= 8:
                        pe.wait_ge(taken.h, n - 7)
                    for q, src in enumerate(srcs):
                        mm = pe.transpose(bank[n % 8][:, q * P:(q + 1) * P], src, ident)
                    mm.then_inc(flipped.h, 1)

            @block.vector
            def _(dve):
                for n, (dst, srcs) in enumerate(pairs):
                    dve.wait_ge(flipped.h, n + 1)
                    dve.tensor_copy(dst, bank[n % 8][:, 0:len(srcs) * P].rearrange("p (q c) -> p q c", q=len(srcs))).then_inc(taken.h, 1)

    def rwkv(r, k, v, zt, zg, oT, outer):
        with ExitStack() as ctx:
            cs, aa, ep, em, kk, tmp = (sb(ctx, n, [P, 4, S]) for n in ("cs", "aa", "ep", "em", "kk", "tmp"))
            lora = sb(ctx, "lora", [P, S])
            level = sb(ctx, "level", [P, LEVELS, P])
            before, upto = sb(ctx, "before", [P, P]), sb(ctx, "upto", [P, P])
            pc = sb(ctx, "pc", [P, 4, NCH])
            with ExitStack() as c1:
                inside = sb(c1, "inside", [P, S])
                s_in, pre, sg1, sg2, scan, expd, sq, sm_, mxd, rtd, pr, bsum = (
                    sig(n) for n in ("s_in", "pre", "sg1", "sg2", "scan", "expd", "sq", "sm_", "mxd", "rtd", "pr", "bsum"))
                block = c1.enter_context(stage())

                @block.sync
                def _(sp):
                    sp.dma_start(lora[0:HD, :], a["w_decay_up"][0]).then_inc(s_in.h, 16)
                    sp.dma_start(lora[HD:P, :], a["w_iclr_up"][0]).then_inc(s_in.h, 16)
                    cst_dma(sp, level[:, :, :].rearrange("p l n -> p (l n)"), "level", s_in)
                    cst_dma(sp, before[:, :], "before", s_in)
                    cst_dma(sp, upto[:, :], "upto", s_in)
                    cst_dma(sp, inside[:, :], "inside", s_in)

                @block.scalar
                def _(act):
                    act.activation(zt[0:HD, :], zt[0:HD, :], ACT.Tanh).then_inc(sg1.h, 1)
                    act.activation(zg[:, :], zg[:, :], ACT.Sigmoid)
                    for m in range(8):
                        act.wait_ge(pre.h, m + 1)
                        dst, b = (cs, "w0") if m < 4 else (aa, "a0")
                        act.activation(dst[:, m % 4, :], bank[m][:, :], ACT.Sigmoid, bias=col(b, m % 4)).then_inc(sg2.h, 1)
                    for m in range(4):
                        act.wait_ge(scan.h, m + 1)
                        act.activation(ep[:, m, :], tmp[:, m, :], ACT.Exp, scale=-EHALF).then_inc(expd.h, 1)
                        act.activation(em[:, m, :], tmp[:, m, :], ACT.Exp, scale=EHALF).then_inc(expd.h, 1)
                    for m in range(4):
                        act.wait_ge(mxd.h, m + 1)
                        act.activation(cs[:, m, :], cs[:, m, :], ACT.Sqrt).then_inc(rtd.h, 1)

                @block.tensor
                def _(pe):
                    pe.wait_ge(s_in.h, 16 * 6)
                    pe.wait_ge(sg1.h, 1)
                    for m in range(8):
                        lo_, hi_ = (0, HD) if m < 4 else (HD, P)
                        pe.matmul(bank[m][:, :], lora[lo_:hi_, (m % 4) * P:(m % 4 + 1) * P], zt[lo_:hi_, :],
                                  start=True, stop=True).then_inc(pre.h, 1)
                    for m in range(4):
                        pe.wait_ge(sq.h, m + 1)
                        pe.wait_ge(sg2.h, m + 1)
                        pe.matmul(bank[m][:, :], pair, cs[:, m, :], start=True, stop=True).then_inc(sm_.h, 1)
                    for m in range(4):
                        pe.wait_ge(pr.h, m + 1)
                        pe.wait_ge(sg2.h, 4 + m + 1)
                        pe.matmul(bank[4 + m][:, :], pair, cs[:, m, :], start=True, stop=True).then_inc(bsum.h, 1)

                @block.vector
                def _(dve):
                    chain = Chain(dve, dve_chain)
                    dve.wait_ge(s_in.h, 16 * 6)
                    for m in range(4):
                        chain(dve.tensor_scalar(kk[:, m, :], k[:, m, :], col("k_k", m), None, ALU.mult))
                    for m in range(4):
                        dve.wait_ge(sg2.h, m + 1)
                        scan.by(dve.tensor_tensor_scan(tmp[:, m, :], inside[:, :], cs[:, m, :], 0.0, ALU.mult, ALU.add))
                    dve.wait_ge(scan.h, 4)
                    for m in range(4):
                        sq.by(dve.tensor_tensor(cs[:, m, :], kk[:, m, :], kk[:, m, :], ALU.mult))
                    for m in range(4):
                        dve.wait_ge(sm_.h, m + 1)
                        mxd.by(dve.tensor_scalar(cs[:, m, :], bank[m][:, :], 1e-24, None, ALU.max))
                    dve.wait_ge(expd.h, 8)
                    for m in range(4):
                        dve.wait_ge(rtd.h, m + 1)
                        chain(dve.reciprocal(tmp[:, m, :], cs[:, m, :]))
                        chain(dve.tensor_tensor(kk[:, m, :], kk[:, m, :], tmp[:, m, :], ALU.mult))
                    for m in range(4):
                        dve.wait_ge(sg2.h, 4 + m + 1)
                        chain(dve.tensor_scalar(tmp[:, m, :], aa[:, m, :], -1.0, col("k_a", m), ALU.add, ALU.mult))
                        chain(dve.scalar_tensor_tensor(k[:, m, :], tmp[:, m, :], 1.0, k[:, m, :], ALU.add, ALU.mult))
                        pr.by(dve.scalar_tensor_tensor(cs[:, m, :], r[:, m, :], col("r_k", m), k[:, m, :], ALU.mult, ALU.mult))
                    for m in range(4):
                        chain(dve.tensor_tensor(aa[:, m, :], aa[:, m, :], kk[:, m, :], ALU.mult))
                    dve.wait_ge(pr.h, 4)
                    chain(dve.tensor_tensor(r[:, :, :], r[:, :, :], ep[:, :, :], ALU.mult))
                    chain(dve.tensor_tensor(k[:, :, :], k[:, :, :], em[:, :, :], ALU.mult))
                    chain(dve.tensor_tensor(aa[:, :, :], aa[:, :, :], em[:, :, :], ALU.mult))
                    for m in range(4):
                        kc = kk[:, m, :].rearrange("p (c t) -> p c t", t=C)
                        ec = ep[:, m, :].rearrange("p (c t) -> p c t", t=C)
                        chain(dve.tensor_scalar(kk[:, m, :], kk[:, m, :], -1.0, None, ALU.mult))
                        chain(dve.tensor_tensor(kc[:, :, 1:C], kc[:, :, 1:C], ec[:, :, 0:C - 1], ALU.mult))
                        chain(dve.tensor_copy(pc[:, m, :], ec[:, :, C - 1]))
                    for m in range(4):
                        dve.wait_ge(bsum.h, m + 1)
                        chain(dve.tensor_tensor(cs[:, m, :], bank[4 + m][:, :], v[:, m, :], ALU.mult))
            vt, kt, bt, at_ = tmp, ep, em, v
            turn([(dst[:, t, :].rearrange("p (q c) -> p q c", q=4), [src[:, m, t * P:(t + 1) * P] for m in range(4)])
                  for dst, src in ((vt, v), (kt, k), (bt, aa)) for t in range(NT)])
            turn([(at_[:, t, :].rearrange("p (q c) -> p q c", q=4), [kk[:, m, t * P:(t + 1) * P] for m in range(4)])
                  for t in range(NT)])
            wt = sb(ctx, "wt", [P, NT, 4, P])
            u0 = sb(ctx, "u0", [P, NT, 2, 4 * HD])
            z = sb(ctx, "z", [P, NCH, 4, HD])

            def uat(h):
                return slice(h % 2 * 4 * HD + h // 2 * HD, h % 2 * 4 * HD + h // 2 * HD + HD)

            def u_of(h, t, r0=0, r1=P):
                return u0[r0:r1, t, h % 2, h // 2 * HD:(h // 2 + 1) * HD]

            def head(x, h, t):
                return x[h % 2 * HD:h % 2 * HD + HD, h // 2, t * P:(t + 1) * P]

            with ExitStack() as c2:
                NG = 4
                T, Tt, pm = (sb(c2, n, [P, NG, 4, P]) for n in ("T", "Tt", "pm"))
                nt = oT.rearrange("p g (h n) -> p g h n", h=4)
                made, took = sig("made"), sig("took")
                block = c2.enter_context(stage())
                i4 = ident.rearrange("p (o n) -> p o n", o=1).broadcast_to([P, 4, P])
                flat = lambda b: b.rearrange("p (h n) -> p h n", h=4)

                def m4(mask):
                    return mask.rearrange("p (o n) -> p o n", o=1).broadcast_to([P, 4, P])

                order = []
                for hf in range(2):
                    for kind in ("nt", "p0", "t0"):
                        order += [(kind, hf, g, 0) for g in range(NG)]
                    for l in range(1, LEVELS):
                        for kind in ("p", "t", "tt") if l < LEVELS - 1 else ("p", "tt"):
                            order += [(kind, hf, g, l) for g in range(NG)]
                    order += [("ak", hf, g, 0) for g in range(NG)]
                    order += [("y", hf, x, 0) for x in range(2)]
                    order += [("u", hf, x, 0) for x in range(2)]
                    order += [("w", hf, x, 0) for x in range(2)]
                where = {x: n for n, x in enumerate(order)}

                def halves(x, l, which):
                    return x.rearrange("p (b s e) -> p b s e", s=2, e=2 ** l)[:, :, which, :]

                @block.tensor
                def _(pe):
                    for n, (kind, hf, g, l) in enumerate(order):
                        t = hf * 2 + g // 2
                        need = n - 7
                        if kind == "t0":
                            need = max(need, where["p0", hf, g, 0] + 1)
                        elif kind == "p":
                            need = max(need, where["t0" if l == 1 else "tt", hf, g, l - 1] + 1)
                        elif kind in ("t", "tt"):
                            need = max(need, where["p", hf, g, l] + 1)
                        elif kind == "y":
                            need = max(need, where["ak", hf, 2 * g + 1, 0] + 1)
                        elif kind in ("u", "w"):
                            need = max(need, where["y", hf, g, 0] + 1)
                        if need > 0:
                            pe.wait_ge(took.h, need)
                        acc = bank[n % 8]
                        if kind in ("y", "u", "w"):
                            t = hf * 2 + g
                            for h in range(NH):
                                gg, hh = 2 * g + h % 2, h // 2
                                if kind == "y":
                                    mm = pe.matmul(acc[:, h * HD:(h + 1) * HD], pm[:, gg, hh, :], vt[:, t, h * HD:(h + 1) * HD],
                                                   start=True, stop=True)
                                elif kind == "u":
                                    mm = pe.matmul(acc[:, uat(h)], Tt[:, gg, hh, :], nt[:, g, :, :].rearrange("p a b -> p (a b)")[:, h * HD:(h + 1) * HD],
                                                   start=True, stop=True)
                                else:
                                    mm = pe.matmul(acc[h % 2 * HD:h % 2 * HD + HD, h // 2 * P:(h // 2 + 1) * P],
                                                   at_[:, t, h * HD:(h + 1) * HD], Tt[:, gg, hh, :], start=True, stop=True)
                        else:
                            for hh in range(4):
                                h = 2 * hh + g % 2
                                o = acc[:, hh * P:(hh + 1) * P]
                                if kind == "nt":
                                    mm = pe.matmul(o, head(aa, h, t), head(kk, h, t), start=True, stop=True)
                                elif kind == "p0":
                                    mm = pe.matmul(o, head(kk, h, t), head(aa, h, t), start=True, stop=True)
                                elif kind == "ak":
                                    mm = pe.matmul(o, head(k, h, t), head(kk, h, t), start=True, stop=True)
                                elif kind == "t0":
                                    mm = pe.matmul(o, pm[:, g, hh, :], ident, start=True, stop=True)
                                elif kind == "p":
                                    mm = pe.matmul(o, nt[:, g, hh, :], T[:, g, hh, :], start=True, stop=True)
                                elif kind == "t":
                                    mm = pe.matmul(halves(o, l, 0), Tt[:, g, hh, :], halves(pm[:, g, hh, :], l, 0), start=True, stop=True)
                                else:
                                    mm = pe.matmul(halves(o, l, 1), pm[:, g, hh, :], halves(Tt[:, g, hh, :], l, 1), start=True, stop=True)
                        mm.then_inc(made.h, 1)

                @block.vector
                def _(dve):
                    chain = Chain(dve, dve_chain)
                    for n, (kind, hf, g, l) in enumerate(order):
                        dve.wait_ge(made.h, n + 1)
                        acc = flat(bank[n % 8][:, :])
                        if kind == "nt":
                            ins = dve.tensor_tensor(nt[:, g, :, :], acc, m4(before[:, :]), ALU.mult)
                        elif kind == "p0":
                            chain(dve.tensor_tensor(pm[:, g, :, :], acc, m4(level[:, 0, :]), ALU.mult))
                            ins = dve.tensor_tensor(T[:, g, :, :], pm[:, g, :, :], i4, ALU.add)
                        elif kind == "t0":
                            ins = dve.tensor_tensor(Tt[:, g, :, :], acc, i4, ALU.add)
                        elif kind == "p":
                            ins = dve.tensor_tensor(pm[:, g, :, :], acc, m4(level[:, l, :]), ALU.mult)
                        elif kind == "t":
                            x = halves(T[:, g, :, :].rearrange("p h n -> p (h n)"), l, 0)
                            ins = dve.tensor_tensor(x, halves(bank[n % 8][:, :], l, 0), x, ALU.add)
                        elif kind == "tt":
                            x = halves(Tt[:, g, :, :].rearrange("p h n -> p (h n)"), l, 1)
                            ins = dve.tensor_tensor(x, halves(bank[n % 8][:, :], l, 1), x, ALU.add)
                        elif kind == "ak":
                            ins = dve.tensor_tensor(pm[:, g, :, :], acc, m4(before[:, :]), ALU.mult)
                        elif kind == "y":
                            ins = dve.tensor_copy(nt[:, g, :, :].rearrange("p a b -> p (a b)"), bank[n % 8][:, :])
                        elif kind == "u":
                            ins = dve.tensor_copy(u0[:, hf * 2 + g, :, :].rearrange("p a b -> p (a b)"), bank[n % 8][:, :])
                        else:
                            ins = dve.tensor_copy(wt[:, hf * 2 + g, :, :], acc)
                        ins.then_inc(took.h, 1)
            with ExitStack() as c3:
                zn = sb(c3, "zn", [P, 4, HD])
                read, u_done, kv_, z_done, zero = sig("read"), sig("u_done"), sig("kv"), sig("z_done"), sig("zero")
                block = c3.enter_context(stage())

                def rng(c):
                    return c * C // P, c * C % P, c * C % P + C

                @block.tensor
                def _(pe):
                    for c in range(NCH - 1):
                        t, r0, r1 = rng(c)
                        pe.wait_ge(z_done.h, c + 1)
                        for h in range(NH):
                            p0 = h % 2 * HD
                            mm = pe.matmul(bank[c % 2 * 2 + h % 2][:, h // 2 * HD:(h // 2 + 1) * HD], wt[p0:p0 + HD, t, h // 2, :],
                                           z[p0:p0 + HD, c, h // 2, :], start=True, stop=True)
                        mm.then_inc(read.h, 1)
                        pe.wait_ge(u_done.h, c + 1)
                        for h in range(NH):
                            p0 = h % 2 * HD
                            o = bank[4 + c % 2][p0:p0 + HD, h // 2 * HD:(h // 2 + 1) * HD]
                            pe.matmul(o, kt[r0:r1, t, h * HD:(h + 1) * HD], vt[r0:r1, t, h * HD:(h + 1) * HD], start=True, stop=False)
                            mm = pe.matmul(o, bt[r0:r1, t, h * HD:(h + 1) * HD], u_of(h, t, r0, r1), start=False, stop=True)
                        mm.then_inc(kv_.h, 1)
                    pe.wait_ge(z_done.h, NCH)
                    c = NCH - 1
                    t, r0, r1 = rng(c)
                    for h in range(NH):
                        p0 = h % 2 * HD
                        mm = pe.matmul(bank[c % 2 * 2 + h % 2][:, h // 2 * HD:(h // 2 + 1) * HD], wt[p0:p0 + HD, t, h // 2, :],
                                       z[p0:p0 + HD, c, h // 2, :], start=True, stop=True)
                    mm.then_inc(read.h, 1)

                @block.vector
                def _(dve):
                    chain = Chain(dve, dve_chain)
                    dve.memset(z[:, 0, :, :], 0.0).then_inc(z_done.h, 1)
                    for c in range(NCH):
                        t, r0, r1 = rng(c)
                        dve.wait_ge(read.h, c + 1)
                        dve.tensor_tensor(u0[r0:r1, t, :, :], banks[r0:r1, c % 2 * 2:c % 2 * 2 + 2, 0:4 * HD], u0[r0:r1, t, :, :], ALU.add).then_inc(u_done.h, 1)
                        if c == NCH - 1:
                            break
                        dve.wait_ge(kv_.h, c + 1)
                        chain(dve.tensor_tensor(zn[:, :, :], bank[4 + c % 2][:, 0:4 * HD].rearrange("p (a b) -> p a b", a=4),
                                                z[:, c, :, :], ALU.add))
                        dve.tensor_tensor(z[:, c + 1, :, :], zn[:, :, :],
                                          pc[:, :, c:c + 1].broadcast_to([P, 4, HD]), ALU.mult).then_inc(z_done.h, 1)
            with ExitStack() as c4:
                rb = [sb(c4, f"rb{i}", [P, 4, P]) for i in range(4)]
                made, took, summed, otk = sig("made"), sig("took"), sig("summed"), sig("otk")
                block = c4.enter_context(stage())
                m4 = lambda mask: mask.rearrange("p (o n) -> p o n", o=1).broadcast_to([P, 4, P])
                groups = [(t, q) for t in range(NT) for q in range(2)]

                @block.tensor
                def _(pe):
                    for n in range(len(groups) + 1):
                        if n < len(groups):
                            t, q = groups[n]
                            for x, src in enumerate((aa, k)):
                                if n >= 2:
                                    pe.wait_ge(took.h, 2 * (n - 2) + x + 1)
                                for hh in range(4):
                                    h = 2 * hh + q
                                    mm = pe.matmul(bank[n % 2 * 2 + x][:, hh * P:(hh + 1) * P], head(src, h, t), head(r, h, t), start=True, stop=True)
                                mm.then_inc(made.h, 1)
                        if n >= 1:
                            t, q = groups[n - 1]
                            pe.wait_ge(took.h, 2 * n)
                            if n >= 3:
                                pe.wait_ge(otk.h, n - 2)
                            for hh in range(4):
                                h = 2 * hh + q
                                p0 = q * HD
                                lo_ = hh * P
                                b = bank[4 + (n - 1) % 2]
                                pe.matmul(b[p0:p0 + HD, lo_:lo_ + P], vt[:, t, h * HD:(h + 1) * HD], rb[(n - 1) % 2 * 2 + 1][:, hh, :], start=True, stop=False, skip_group_check=True)
                                pe.matmul(b[p0:p0 + HD, lo_:lo_ + P], u_of(h, t), rb[(n - 1) % 2 * 2][:, hh, :], start=False, stop=False, skip_group_check=True)
                                for c in range(t * P // C, (t + 1) * P // C):
                                    o0 = c * C - t * P
                                    mm = pe.matmul(b[p0:p0 + HD, lo_ + o0:lo_ + o0 + C], z[p0:p0 + HD, c, h // 2, :],
                                                   r[p0:p0 + HD, h // 2, c * C:(c + 1) * C], start=False, stop=c == (t + 1) * P // C - 1, skip_group_check=True)
                            mm.then_inc(summed.h, 1)

                @block.vector
                def _(dve):
                    for n in range(len(groups)):
                        for x in range(2):
                            dve.wait_ge(made.h, 2 * n + x + 1)
                            if n >= 2:
                                dve.wait_ge(summed.h, n - 1)
                            dve.tensor_tensor(rb[n % 2 * 2 + x][:, :, :], bank[n % 2 * 2 + x][:, :].rearrange("p (h n) -> p h n", h=4),
                                              m4(upto[:, :]), ALU.mult).then_inc(took.h, 1)

                @block.scalar
                def _(act):
                    for n in range(len(groups)):
                        t, q = groups[n]
                        act.wait_ge(summed.h, n + 1)
                        act.activation(oT[q * HD:q * HD + HD, :, t * P:(t + 1) * P], bank[4 + n % 2][q * HD:q * HD + HD, :].rearrange("p (a b) -> p a b", a=4),
                                       ACT.Copy).then_inc(otk.h, 1)
            with ExitStack() as c5:
                gm, gd, g1, g2, g3, g4, got = (sig(n) for n in ("gm", "gd", "g1", "g2", "g3", "g4", "got"))
                wgu = u0[:, 0, :, :].rearrange("p a b -> p (a b)")
                dd, sqd, rt = kk, aa, ep
                block = c5.enter_context(stage())

                @block.sync
                def _(sp):
                    sp.dma_start(wgu, a["w_gate_up"][0]).then_inc(got.h, 16)

                @block.tensor
                def _(pe):
                    for m in range(4):
                        pe.matmul(bank[m][:, :], pair, oT[:, m, :], start=True, stop=True).then_inc(gm.h, 1)
                    for m in range(4):
                        pe.wait_ge(g1.h, m + 1)
                        pe.matmul(bank[4 + m][:, :], pair, sqd[:, m, :], start=True, stop=True).then_inc(g2.h, 1)
                    pe.wait_ge(got.h, 16)
                    for m in range(4):
                        pe.matmul(bank[m][:, :], wgu[:, m * P:(m + 1) * P], zg[:, :], start=True, stop=True).then_inc(g4.h, 1)

                @block.scalar
                def _(act):
                    for m in range(4):
                        act.wait_ge(gd.h, m + 1)
                        act.activation(sqd[:, m, :], dd[:, m, :], ACT.Square).then_inc(g1.h, 1)
                    for m in range(4):
                        act.wait_ge(g3.h, m + 1)
                        act.activation(rt[:, m, :], tmp[:, m, :], ACT.Sqrt).then_inc(g1.h, 1)

                @block.vector
                def _(dve):
                    chain = Chain(dve, dve_chain)
                    for m in range(4):
                        dve.wait_ge(gm.h, m + 1)
                        dve.scalar_tensor_tensor(dd[:, m, :], bank[m][:, :], -1.0 / HD, oT[:, m, :], ALU.mult, ALU.add).then_inc(gd.h, 1)
                    for m in range(4):
                        dve.wait_ge(g2.h, m + 1)
                        dve.tensor_scalar(tmp[:, m, :], bank[4 + m][:, :], 1.0 / HD, GN_EPS, ALU.mult, ALU.add).then_inc(g3.h, 1)
                    for m in range(4):
                        dve.wait_ge(g1.h, 4 + m + 1)
                        chain(dve.reciprocal(em[:, m, :], rt[:, m, :]))
                        chain(dve.scalar_tensor_tensor(dd[:, m, :], dd[:, m, :], col("ln_g", m), em[:, m, :], ALU.mult, ALU.mult))
                        chain(dve.scalar_tensor_tensor(dd[:, m, :], dd[:, m, :], col("ln_b", m), cs[:, m, :], ALU.add, ALU.add))
                        dve.wait_ge(g4.h, m + 1)
                        chain(dve.tensor_tensor(oT[:, m, :], dd[:, m, :], bank[m][:, :], ALU.mult))

    def local_attention(qT, kd, vT, oT):
        with ExitStack() as ctx:
            vt = sb(ctx, "vt", [P, 1, 4, P])
            bias = sb(ctx, "bias", [P, NH, 2 * P])
            sinks, nsinks = sb(ctx, "sinks", [P, NH]), sb(ctx, "nsinks", [P, NH])
            with ExitStack() as c1:
                table = sb(c1, "table", [BUCKETS + 1, NH])
                hot = sb(c1, "hot", [BUCKETS + 1, RLEN])
                row = sb(c1, "row", [NH, RLEN])
                got, m, c, w = sig("got"), sig("m"), sig("c"), sig("w")
                block = c1.enter_context(stage())

                @block.sync
                def _(sp):
                    sp.dma_start(table[0:BUCKETS, :], a["rel_bias"]).then_inc(got.h, 16)
                    lo_ = CST["ones"][0]
                    sp.dma_start(table[BUCKETS:BUCKETS + 1, :], a["cst"][0:1, lo_:lo_ + NH]).then_inc(got.h, 16)
                    cst_dma(sp, hot[:, :], "onehot", got, BUCKETS + 1)
                    sp.dma_start(sinks[:, :], a["sinks"][0:1, :].broadcast_to([P, NH])).then_inc(got.h, 16)
                    sp.wait_ge(c.h, 1)
                    sp.dma_start(scratch[:, :, :], row[:, :].rearrange("h (o x) -> h o x", o=1).broadcast_to([NH, P, RLEN])).then_inc(w.h, 16)
                    sp.wait_ge(w.h, 16)
                    flat = scratch[:, :, :].rearrange("h q x -> h (q x)")
                    sp.dma_start(bias[:, :, :], flat[:, P - 1:P - 1 + P * (RLEN - 1)].rearrange("h (q x) -> q h x", x=RLEN - 1)[:, :, 0:2 * P]).then_inc(w.h, 16)
                    sp.wait_ge(w.h, 32)

                @block.tensor
                def _(pe):
                    pe.wait_ge(got.h, 64)
                    pe.matmul(bank[0][0:NH, 0:RLEN], table[:, :], hot[:, :], start=True, stop=True).then_inc(m.h, 1)

                @block.vector
                def _(dve):
                    dve.wait_ge(m.h, 1)
                    dve.tensor_scalar(row[:, :], bank[0][0:NH, 0:RLEN], HD ** 0.5, None, ALU.mult).then_inc(c.h, 1)
                    dve.wait_ge(got.h, 64)
                    dve.tensor_scalar(nsinks[:, :], sinks[:, :], -1.0, None, ALU.mult)
            turn([(vt[:, 0, :, :], [vT[:, t * P:(t + 1) * P] for t in range(NT)])])
            units, dst = [], []
            for h in range(NH):
                p0, g = h % 2 * HD, h // 4
                for n in range(NT):
                    lo_ = max(n - 1, 0) * P
                    hi_ = (n + 1) * P
                    w = hi_ - lo_
                    units.append(([[(qT[p0:p0 + HD, h // 2, n * P:hi_], kd[p0:p0 + HD, g, lo_:hi_], 0)]], w,
                                  bias[:, h, 2 * P - w:2 * P],
                                  [vt[:, 0, b, g * HD:(g + 1) * HD] for b in range(lo_ // P, n + 1)], (p0, p0 + HD)))
                    dst.append(oT[p0:p0 + HD, h // 2, n * P:hi_])
            attend(units, lambda u: dst[u], sink=lambda i: (sinks[:, i // NT:i // NT + 1], nsinks[:, i // NT:i // NT + 1]))

    def add_normed(src, name):
        with ExitStack() as ctx:
            y = sb(ctx, "y", [P, 2, S])

            def finish(dve, chain, k, rstd):
                chain(dve.scalar_tensor_tensor(y[:, k % 2, :], src[:, k, :], col(name, k), rstd, ALU.mult, ALU.mult))
                chain(dve.tensor_tensor(xT[:, k, :], y[:, k % 2, :], xT[:, k, :], ALU.add))
            norm(lambda k: src[:, k, :], KD, None, None, D, EPS, finish)

    def tables(cosT, sinT):
        with ExitStack() as ctx:
            pi = sb(ctx, "pi", [P, S], mybir.dt.int32)
            fr = sb(ctx, "fr", [P, 2])
            ang, n, r = (sb(ctx, x, [P, S]) for x in ("ang", "n", "r"))
            got, reduced, sined = sig("got"), sig("reduced"), sig("sined")
            MAGIC = 1.5 * 2.0 ** 23
            C1 = 6.28125
            C2 = 0.00193500518798828125
            C3 = 2 * math.pi - C1 - C2
            block = ctx.enter_context(stage())

            @block.sync
            def _(sp):
                sp.dma_start(pi[:, :], a["positions_2"][0:1, :].broadcast_to([P, S])).then_inc(got.h, 16)
                cst_dma(sp, fr[:, :], "freq", got)

            @block.vector
            def _(dve):
                chain = Chain(dve, dve_chain)
                dve.wait_ge(got.h, 32)
                chain(dve.tensor_copy(ang[:, :], pi[:, :]))
                chain(dve.tensor_scalar(ang[:, :], ang[:, :], fr[:, 0:1], None, ALU.mult))
                chain(dve.tensor_scalar(n[:, :], ang[:, :], 1 / (2 * math.pi), None, ALU.mult))
                chain(dve.tensor_scalar(n[:, :], n[:, :], MAGIC, None, ALU.add))
                chain(dve.tensor_scalar(n[:, :], n[:, :], -MAGIC, None, ALU.add))
                for c in (C1, C2, C3):
                    chain(dve.scalar_tensor_tensor(ang[:, :], n[:, :], -c, ang[:, :], ALU.mult, ALU.add))
                chain(dve.tensor_scalar(ang[:, :], ang[:, :], 3.1415925, -3.1415925, ALU.min, ALU.max))
                reduced.by(dve.tensor_scalar(r[:, :], ang[:, :], 0.5, None, ALU.mult))
                dve.wait_ge(sined.h, 2)
                chain(dve.tensor_tensor(r[:, :], r[:, :], r[:, :], ALU.mult))
                chain(dve.tensor_scalar(cosT[:, :], r[:, :], -2.0, 1.0, ALU.mult, ALU.add))
                chain(dve.tensor_scalar(sinT[:, :], sinT[:, :], fr[:, 1:2], None, ALU.mult))

            @block.scalar
            def _(act):
                act.wait_ge(reduced.h, 1)
                act.activation(sinT[:, :], ang[:, :], ACT.Sin).then_inc(sined.h, 1)
                act.activation(r[:, :], r[:, :], ACT.Sin).then_inc(sined.h, 1)

    class EvenSide(Side):
        PICKS, TURNS_A, TURNS_B = 3, 7, 17

        def __init__(self, ctx, af, av, bv, rotated, vta, vtb, forget, mask, lam, lam_init, cosT, sinT):
            self.af, self.av, self.bv, self.rotated, self.vta, self.vtb = af, av, bv, rotated, vta, vtb
            self.forget, self.mask, self.lam, self.lam_init = forget, mask, lam, lam_init
            self.rot = Rotate(ctx, cosT, sinT)
            self.fb = sb(ctx, "fb", [NH, 1])
            self.ls, self.pr, self.sm = sb(ctx, "ls", [P, 4, HD]), sb(ctx, "pr", [P, 2, HD]), sb(ctx, "sm", [P, 2])
            flat = vtb.rearrange("p t m n -> p (t m n)")
            self.y, self.w = flat[0:NH, 0:S], flat[0:NH, S:2 * S]
            self.pick = flat[0:NH, 2 * S:2 * S + NH * P].rearrange("p (h n) -> p h n", h=NH)
            self.got, self.made, self.did, self.summed, self.exped, self.filled, self.emptied = (
                sig(n) for n in ("got", "made", "did", "summed", "exped", "filled", "emptied"))

        def sp(self, sp):
            sp.dma_start(self.fb[:, :], a["ev_fgate_b_2"].rearrange("o h -> h o")).then_inc(self.got.h, 16)
            for i, n in enumerate(("q1", "q2", "k1", "k2")):
                sp.dma_start(self.ls[:, i, :], a[f"ev_lambda_{n}_2"][0:1, :].broadcast_to([P, HD])).then_inc(self.got.h, 16)
            cst_dma(sp, self.mask[:, S - P:S], "future", self.got)
            self.rot.sp(sp)

        def act(self, act, m):
            if m == 0:
                chain = Chain(act, act_chain)
                act.wait_ge(self.summed.h, 1)
                act.activation(self.sm[:, :], self.sm[:, :], ACT.Exp).then_inc(self.exped.h, 1)
                act.wait_ge(self.made.h, 1)
                chain(act.activation(self.y, self.af[0:NH, :], ACT.Abs))
                chain(act.activation(self.y, self.y, ACT.Exp, scale=-1.0))
                act.activation(self.y, self.y, ACT.Ln, bias=1.0).then_inc(self.did.h, 1)

        def pe(self, pe, free, m):
            def turn_(dst_bank, srcs):
                for q, src in enumerate(srcs):
                    mm = pe.transpose(dst_bank[:, q * P:(q + 1) * P], src, ident)
                mm.then_inc(self.filled.h, 1)
            if self.PICKS <= m < self.TURNS_A:
                pe.wait_ge(self.made.h, 2)
                for h in (2 * (m - self.PICKS), 2 * (m - self.PICKS) + 1):
                    if h >= 4:
                        pe.wait_ge(self.emptied.h, h - 3)
                    pe.matmul(bank[4 + h % 4][:, :], self.pick[:, h, :], self.w, start=True, stop=True).then_inc(self.filled.h, 1)
            if self.TURNS_A <= m < self.TURNS_A + NT:
                t = m - self.TURNS_A
                pe.wait_ge(free.h, 5)
                pe.wait_ge(self.emptied.h, NH + t - 3)
                turn_(bank[4 + t], [self.av[:, q, t * P:(t + 1) * P] for q in range(4)])
            if self.TURNS_B <= m < self.TURNS_B + NT:
                t = m - self.TURNS_B
                pe.wait_ge(free.h, 17)
                pe.wait_ge(self.emptied.h, NH + NT + t)
                turn_(bank[7], [self.bv[:, q, t * P:(t + 1) * P] for q in range(4)])
            if m in self.rotated:
                pe.wait_ge(free.h, m + 1)
                self.rot.pe(pe, self.rotated[m])

        def dve(self, dve, chain, free):
            dve.memset(self.mask[:, 0:S - P], 0.0)
            chain(dve.tensor_copy(self.pick, ident[0:NH, 0:NH].rearrange("p (h o) -> p h o", o=1).broadcast_to([NH, NH, P])))
            dve.wait_ge(self.got.h, 96)
            chain(dve.tensor_tensor(self.pr[:, :, :], self.ls[:, 0:2, :], self.ls[:, 2:4, :], ALU.mult))
            dve.tensor_reduce(self.sm[:, :], self.pr[:, :, :], AX.X, ALU.add).then_inc(self.summed.h, 1)
            dve.wait_ge(free.h, 1)
            dve.tensor_scalar(self.af[0:NH, :], self.af[0:NH, :], self.fb[:, 0:1], None, ALU.add).then_inc(self.made.h, 1)
            dve.wait_ge(self.exped.h, 1)
            chain(dve.tensor_scalar(self.lam, self.sm[:, 1:2], self.sm[:, 0:1], self.lam_init, ALU.subtract, ALU.subtract))
            dve.wait_ge(self.did.h, 1)
            chain(dve.tensor_scalar(self.w, self.af[0:NH, :], 0.0, None, ALU.min))
            chain(dve.tensor_tensor(self.y, self.y, self.w, ALU.subtract))
            dve.tensor_tensor_scan(self.w, self.y, self.y, 0.0, ALU.add, ALU.max).then_inc(self.made.h, 1)
            for h in range(NH):
                dve.wait_ge(self.filled.h, h + 1)
                dve.tensor_scalar(self.forget[:, h, :], bank[4 + h % 4][:, :], HD ** 0.5, None, ALU.mult).then_inc(self.emptied.h, 1)

            def take(n, dst, b):
                dve.wait_ge(self.filled.h, n + 1)
                dve.tensor_copy(dst.rearrange("p m n -> p (m n)"), bank[b][:, :]).then_inc(self.emptied.h, 1)
            for t in range(NT):
                take(NH + t, self.vta[:, t, :, :], 4 + t)
            for m, x in self.rotated.items():
                t = m - self.TURNS_B
                if t < NT:
                    take(NH + NT + t, self.vtb[:, t, :, :], 7)
                self.rot.dve(dve, x)

    def even_mixer(cosT, sinT, oT):
        lam_init = 0.8 - 0.6 * math.exp(-0.3 * 0)
        with ExitStack() as ctx:
            bq, bk, bv = (sb(ctx, n, [P, 4, S]) for n in ("bq", "bk", "bv"))
            vtb = sb(ctx, "vtb", [P, NT, 4, P])
            mask = sb(ctx, "mask", [P, S])
            lam = sb(ctx, "lam", [P, 1])
            with ExitStack() as fx:
                aq, ak, av = (sb(fx, n, [P, 4, S]) for n in ("aq", "ak", "av"))
                vta = sb(fx, "vta", [P, NT, 4, P])
                forget = sb(fx, "forget", [P, NH, S])
                with ExitStack() as pr:
                    hi, lo = sb(pr, "hi", [P, KD, S], F32R), sb(pr, "lo", [P, KD, S], F32R)
                    af = sb(pr, "af", [P, S])
                    dsts = [af[:, :]] + [t[:, m, :] for t in (av, aq, ak, bv, bq, bk) for m in range(4)]
                    project(25, hi, lo, lambda act, m, acc: act.activation(dsts[m], acc, ACT.Copy),
                            lead=Lead(lambda k: col("attn_norm", k), hi, lo, dsts[17:25]),
                            side=EvenSide(pr, af, av, bv, {m: dsts[m] for m in range(17, 25)}, vta, vtb[:, :, :, :], forget, mask,
                                          lam[:, :], lam_init, cosT, sinT))
                units, dst = [], []
                for h in range(NH):
                    p0 = h % 2 * HD
                    for n in range(NT):
                        w = (n + 1) * P
                        units.append(([[(aq[p0:p0 + HD, h // 2, n * P:w], ak[p0:p0 + HD, h // 2, 0:w], 0),
                                        (ident, mask[:, S - P:S], w - P)]], w, forget[:, h, 0:w],
                                      [vta[:, b, h // 2, p0:p0 + HD] for b in range(n + 1)], (p0, p0 + HD)))
                        dst.append(oT[p0:p0 + HD, h // 2, n * P:w])
                attend(units, lambda u: dst[u])
            ob = sb(ctx, "ob", [P, 4, S])
            units, dst = [], []
            for h in range(4):
                for n in range(NT):
                    w = (n + 1) * P
                    units.append(([[(bq[p0:p0 + HD, h, n * P:w], bk[p0:p0 + HD, h, 0:w], 0)] for p0 in (0, HD)], w,
                                  mask[:, S - w:S], [vtb[:, b, h, :] for b in range(n + 1)], (0, P)))
                    dst.append(ob[:, h, n * P:w])
            attend(units, lambda u: dst[u], lam=lam[:, 0:1])

            def finish(dve, chain, k, rstd):
                chain(dve.scalar_tensor_tensor(bq[:, k, :], ob[:, k, :], col("subln"), rstd, ALU.mult, ALU.mult))
                chain(dve.tensor_scalar(oT[:, 4 + k, :], bq[:, k, :], 1.0 - lam_init, None, ALU.mult))
            norm(lambda k: ob[:, k, :], 4, None, None, 2 * HD, EPS, finish, groups=4)

    def load_cst(dst, name):
        with ExitStack() as ctx:
            got = sig("got")
            block = ctx.enter_context(stage())

            @block.sync
            def _(sp):
                cst_dma(sp, dst, name, got)
                sp.wait_ge(got.h, 16)

    class RotateTiles(Side):

        def __init__(self, ctx, tiles_, cosT, sinT):
            self.tiles, self.rot = tiles_, Rotate(ctx, cosT, sinT)

        def sp(self, sp):
            self.rot.sp(sp)

        def pe(self, pe, free, m):
            if m in self.tiles:
                pe.wait_ge(free.h, m + 1)
                self.rot.pe(pe, self.tiles[m])

        def dve(self, dve, chain, free):
            for m in self.tiles:
                self.rot.dve(dve, self.tiles[m])

    class Indexer(Side):
        ROUNDS = TOPK // 8

        def __init__(self, ctx, iq, ik, ciw, keep, future, ukp, wuv, rotated, kr_at, ckv, ckv_at, cosT, sinT):
            self.iq, self.ik, self.ciw, self.keep, self.future, self.ukp, self.wuv = iq, ik, ciw, keep, future, ukp, wuv
            self.rotated, self.kr_at, self.ckv, self.ckv_at = rotated, kr_at, ckv, ckv_at
            self.rot = Rotate(ctx, cosT, sinT)
            self.score, self.work = (sb(ctx, n, [P, NT - 1, S]) for n in ("score", "work"))
            self.part = sb(ctx, "part", [P, 3, S])
            self.top, self.cnt = sb(ctx, "top", [P, NT - 1, 8]), sb(ctx, "cnt", [P, NT - 1])
            self.iwt = sb(ctx, "iwt", [P, NT, 4])
            self.sq = sb(ctx, "sq", [P, S])
            (self.got, self.turned, self.logit, self.clipped, self.added, self.found, self.struck, self.squared, self.summed,
             self.meaned, self.rooted) = (sig(n) for n in ("got", "turned", "logit", "clipped", "added", "found", "struck",
                                                           "squared", "summed", "meaned", "rooted"))
            self.order = [(n, h) for n in range(1, NT) for h in range(4)]

        def sp(self, sp):
            self.rot.sp(sp)
            cst_dma(sp, self.future, "future", self.got)
            sp.dma_start(self.ukp[:, :, ROT:HD], a["od_w_uk_2"][0]).then_inc(self.got.h, 16)
            sp.dma_start(self.wuv[:, :, :], a["od_w_uv_2"][0]).then_inc(self.got.h, 16)

        def first_pe(self, pe):
            for t in range(NT):
                mm = pe.transpose(bank[7][:, t * P:(t + 1) * P], self.ciw[:, t * P:(t + 1) * P], ident)
            mm.then_inc(self.turned.h, 1)
            for x, (n, h) in enumerate(self.order):
                if x >= 3:
                    pe.wait_ge(self.clipped.h, x - 2)
                p0 = h % 2 * HD
                pe.matmul(bank[4 + x % 3][:, 0:(n + 1) * P], self.iq[p0:p0 + HD, h // 2, n * P:(n + 1) * P], self.ik[p0:p0 + HD, 0:(n + 1) * P],
                          start=True, stop=True).then_inc(self.logit.h, 1)

        def first_act(self, act):
            for x, (n, h) in enumerate(self.order):
                act.wait_ge(self.logit.h, x + 1)
                if x >= 3:
                    act.wait_ge(self.added.h, x - 2)
                act.activation(self.part[:, x % 3, 0:(n + 1) * P], bank[4 + x % 3][:, 0:(n + 1) * P], ACT.Relu).then_inc(self.clipped.h, 1)

        def pe(self, pe, free, m):
            if m == 1:
                pe.wait_ge(self.clipped.h, len(self.order))
            if m in self.rotated:
                pe.wait_ge(free.h, m + 1)
                self.rot.pe(pe, self.rotated[m])
            if m == self.ckv_at + 1:
                pe.wait_ge(self.squared.h, 1)
                pe.matmul(bank[7][:, :], ones, self.sq[:, :], start=True, stop=True).then_inc(self.summed.h, 1)

        def act(self, act, m):
            if m == self.ckv_at:
                act.activation(self.sq[:, :], bank[m % 4][:, :], ACT.Square).then_inc(self.squared.h, 1)
            if m == 14:
                act.wait_ge(self.meaned.h, 1)
                act.activation(self.sq[:, :], self.part[:, 0, :], ACT.Sqrt).then_inc(self.rooted.h, 1)

        def dve(self, dve, chain, free):
            dve.memset(self.ukp[:, :, 0:ROT], 0.0)
            dve.wait_ge(self.turned.h, 1)
            chain(dve.tensor_scalar(self.iwt[:, :, :], bank[7][:, :].rearrange("p (t n) -> p t n", t=NT)[:, :, 0:4], 0.5, None, ALU.mult))
            tiles_ = [(n, slice(0, (n + 1) * P)) for n in range(1, NT)]
            for x, (n, h) in enumerate(self.order):
                w = (n + 1) * P
                sc, part = self.score[:, n - 1, 0:w], self.part[:, x % 3, 0:w]
                dve.wait_ge(self.clipped.h, x + 1)
                if h == 0:
                    self.added.by(dve.tensor_scalar(sc, part, self.iwt[:, n, h:h + 1], None, ALU.mult))
                else:
                    dve.wait_ge(self.added.h, x)
                    self.added.by(dve.scalar_tensor_tensor(sc, part, self.iwt[:, n, h:h + 1], sc, ALU.mult, ALU.add))
            dve.wait_ge(self.got.h, 48)
            dve.wait_ge(self.added.h, len(self.order))
            for n, _ in tiles_:
                x = self.score[:, n - 1, n * P:(n + 1) * P]
                ins = dve.tensor_tensor(x, x, self.future, ALU.add)
            chain(ins)
            rotations = {3: 0, 5: 1, 7: 2, 9: 3, 10: self.kr_at}
            for i in range(self.ROUNDS):
                for n, w in tiles_:
                    if i:
                        dve.wait_ge(self.struck.h, 3 * (i - 1) + n)
                    dve.max(self.top[:, n - 1, :], (self.work if i else self.score)[:, n - 1, w]).then_inc(self.found.h, 1)
                for n, w in tiles_ if i < self.ROUNDS - 1 else []:
                    dve.wait_ge(self.found.h, 3 * i + n)
                    dve.match_replace(self.work[:, n - 1, w], self.top[:, n - 1, :], (self.work if i else self.score)[:, n - 1, w], -3e38)\
                       .then_inc(self.struck.h, 1)
                if i in rotations:
                    self.rot.dve(dve, self.rotated[rotations[i]])
                if i == self.ROUNDS - 5:
                    dve.wait_ge(self.summed.h, 1)
                    dve.tensor_scalar(self.part[:, 0, :], bank[7][:, :], 1.0 / P, EPS, ALU.mult, ALU.add).then_inc(self.meaned.h, 1)
            dve.wait_ge(self.found.h, 3 * self.ROUNDS)

            def each(op):
                for n, w in tiles_:
                    ins = op(self.score[:, n - 1, w], self.work[:, n - 1, w], self.keep[:, n - 1, w], self.top[:, n - 1, 7:8],
                             self.cnt[:, n - 1:n])
                chain(ins)
            each(lambda sc, wk, kp, thr, cnt: dve.tensor_scalar(kp, sc, thr, None, ALU.is_gt))
            each(lambda sc, wk, kp, thr, cnt: dve.tensor_reduce(cnt, kp, AX.X, ALU.add))
            each(lambda sc, wk, kp, thr, cnt: dve.tensor_scalar(cnt, cnt, -1.0, float(TOPK), ALU.mult, ALU.add))
            each(lambda sc, wk, kp, thr, cnt: dve.tensor_scalar(sc, sc, thr, None, ALU.is_equal))
            each(lambda sc, wk, kp, thr, cnt: dve.tensor_tensor_scan(wk, sc, sc, 0.0, ALU.add, ALU.max))
            each(lambda sc, wk, kp, thr, cnt: dve.scalar_tensor_tensor(wk, wk, cnt, sc, ALU.is_le, ALU.mult))
            each(lambda sc, wk, kp, thr, cnt: dve.tensor_tensor(kp, kp, wk, ALU.add))
            each(lambda sc, wk, kp, thr, cnt: dve.tensor_scalar(kp, kp, -1.0, 1e30, ALU.add, ALU.mult))
            dve.wait_ge(self.rooted.h, 1)
            chain(dve.reciprocal(self.part[:, 1, :], self.sq[:, :]))
            chain(dve.scalar_tensor_tensor(self.ckv, self.ckv, col("kv_norm"), self.part[:, 1, :], ALU.mult, ALU.mult))

    def odd_mixer(cosT, sinT, oT):
        with ExitStack() as ctx:
            sq_, sk_, sv_ = (sb(ctx, n, [P, 4, S]) for n in ("sq", "sk", "sv"))
            with ExitStack() as ds:
                cq = sb(ds, "cq", [P, 4, S])
                ckv, kr = sb(ds, "ckv", [P, 1, S]), sb(ds, "kr", [P, 1, S])
                ukp = sb(ds, "ukp", [P, NH, HD])
                wuv = sb(ds, "wuv", [P, NH, HD])
                future = sb(ds, "future", [P, P])
                keep = sb(ds, "keep", [P, NT - 1, S])
                with ExitStack() as pr:
                    hi, lo = sb(pr, "hi", [P, KD, S], F32R), sb(pr, "lo", [P, KD, S], F32R)
                    iq, ik, ciw = sb(pr, "iq", [P, 2, S]), sb(pr, "ik", [P, S]), sb(pr, "ciw", [P, S])
                    with ExitStack() as c1:
                        to = [iq[:, 0, :], iq[:, 1, :], ik[:, :], ciw[:, :]]
                        project(4, hi, lo, lambda act, m, acc: act.activation(to[m], acc, ACT.Copy),
                                lead=Lead(lambda k: col("attn_norm", KD + k), hi, lo, tiles(c1, 8)),
                                side=RotateTiles(c1, {m: to[m] for m in range(3)}, cosT, sinT))
                    dsts = [cq[:, m, :] for m in range(4)] + [kr[:, 0, :], ckv[:, 0, :]] + [t[:, m, :] for t in (sq_, sk_, sv_) for m in range(4)]
                    project(18, hi, lo, lambda act, m, acc: act.activation(dsts[m], acc, ACT.Copy),
                            side=Indexer(pr, iq, ik, ciw, keep, future[:, :], ukp, wuv, dict(enumerate(dsts[:5])), 4,
                                         ckv[:, 0, :], 5, cosT, sinT))
                dk, dv = sb(ds, "dk", [P, 4, S]), sb(ds, "dv", [P, NT, 4, P])
                with ExitStack() as c1:
                    made, keyed = sig("made"), sig("keyed")
                    block = c1.enter_context(stage())

                    @block.tensor
                    def _(pe):
                        for m in range(4):
                            pe.matmul(bank[m][:, :], ukp[:, 2 * m:2 * m + 2, :].rearrange("p h n -> p (h n)"), ckv[:, 0, :],
                                      start=True, stop=True).then_inc(made.h, 1)
                        for t in range(NT):
                            pe.matmul(bank[4 + t][:, :], ckv[:, 0, t * P:(t + 1) * P], wuv[:, :, :].rearrange("p h n -> p (h n)"),
                                      start=True, stop=True).then_inc(made.h, 1)

                    @block.vector
                    def _(dve):
                        for m in range(4):
                            dve.wait_ge(made.h, m + 1)
                            dve.tensor_copy(dk[:, m, :], bank[m][:, :]).then_inc(keyed.h, 1)
                        dve.wait_ge(keyed.h, 4)
                        for p0 in (0, HD):
                            dve.tensor_copy(dk[p0:p0 + ROT, :, :], kr[p0:p0 + ROT, 0:1, :].broadcast_to([ROT, 4, S]))

                    @block.scalar
                    def _(act):
                        for t in range(NT):
                            act.wait_ge(made.h, 4 + t + 1)
                            act.activation(dv[:, t, :, :].rearrange("p m n -> p (m n)"), bank[4 + t][:, :], ACT.Copy)
                units, dst = [], []
                for h in range(NH):
                    p0 = h % 2 * HD
                    for n in range(NT):
                        w = (n + 1) * P
                        units.append(([[(cq[p0:p0 + HD, h // 2, n * P:w], dk[p0:p0 + HD, h // 2, 0:w], 0)]], w,
                                      future[:, :] if n == 0 else keep[:, n - 1, 0:w],
                                      [dv[:, b, h // 2, p0:p0 + HD] for b in range(n + 1)], (p0, p0 + HD)))
                        dst.append(oT[p0:p0 + HD, h // 2, n * P:w])
                attend(units, lambda u: dst[u])
            stick_breaking(sq_, sk_, sv_, oT)

    def stick_breaking(q, k, v, oT):
        W = [S - b * P for b in range(NT)]
        at_b = [sum(W[:b]) for b in range(NT)]
        ALL = sum(W)
        with ExitStack() as ctx:
            vt = sb(ctx, "vt", [P, NT, 4, P])
            past, after = sb(ctx, "past", [P, P]), sb(ctx, "after", [P, P])
            load_cst(past[:, :], "past_t")
            load_cst(after[:, :], "after_t")
            turn([(vt[:, t, :, :], [v[:, m, t * P:(t + 1) * P] for m in range(4)]) for t in range(NT)])
            zs = [sb(ctx, f"zs{i}", [P, ALL]) for i in range(3)]
            sp_ = [sb(ctx, f"sp{i}", [P, ALL]) for i in range(2)]
            aw = [sb(ctx, f"aw{i}", [P, ALL]) for i in range(2)]
            zed, logs, masked, summed, args_, exped, cut, weighed, otk = (
                sig(n) for n in ("zed", "logs", "masked", "summed", "args", "exped", "cut", "weighed", "otk"))
            zcopied = sig("zcopied")
            block = ctx.enter_context(stage())

            @block.tensor
            def _(pe):
                for i in range(NH + 2):
                    if i < NH:
                        p0 = i % 2 * HD
                        for b in range(NT):
                            if i >= 1:
                                pe.wait_ge(zcopied.h, (i - 1) * NT + b + 1)
                            pe.matmul(bank[b][:, 0:W[b]], k[p0:p0 + HD, i // 2, b * P:(b + 1) * P], q[p0:p0 + HD, i // 2, b * P:S],
                                      start=True, stop=True).then_inc(zed.h, 1)
                    u = i - 1
                    if 0 <= u < NH:
                        pe.wait_ge(masked.h, u + 1)
                        for b in range(NT):
                            x = u * NT + b
                            if x >= 3:
                                pe.wait_ge(args_.h, x - 2)
                            o = bank[4 + x % 3]
                            mm = pe.matmul(o[:, 0:W[b]], after[:, :], sp_[u % 2][:, at_b[b]:at_b[b] + W[b]], start=True, stop=b == NT - 1)
                            for c in range(b + 1, NT):
                                mm = pe.matmul(o[:, (c - b) * P:W[b]], ones, sp_[u % 2][:, at_b[c]:at_b[c] + W[c]], start=False, stop=c == NT - 1)
                            mm.then_inc(summed.h, 1)
                    u = i - 2
                    if 0 <= u < NH:
                        p0 = u % 2 * HD
                        pe.wait_ge(cut.h, u + 1)
                        if u >= 1:
                            pe.wait_ge(otk.h, u)
                        for b in range(NT):
                            mm = pe.matmul(bank[7][p0:p0 + HD, b * P:S], vt[:, b, u // 2, p0:p0 + HD], aw[u % 2][:, at_b[b]:at_b[b] + W[b]],
                                           start=b == 0, stop=b == NT - 1)
                        mm.then_inc(weighed.h, 1)

            @block.scalar
            def _(act):
                chain = Chain(act, act_chain)
                act.preload_act_table_set("natural_log_exp_and_others")
                for i in range(NH + 2):
                    if i < NH:
                        if i >= 3:
                            act.wait_ge(args_.h, (i - 2) * NT)
                        if i >= 2:
                            act.wait_ge(summed.h, (i - 1) * NT)
                        for b in range(NT):
                            act.wait_ge(zed.h, i * NT + b + 1)
                            zcopied.by(act.activation(zs[i % 3][:, at_b[b]:at_b[b] + W[b]], bank[b][:, 0:W[b]], ACT.Copy, scale=HD ** -0.5))
                        act.wait_ge(zcopied.h, (i + 1) * NT)
                        s = sp_[i % 2][:, :]
                        chain(act.activation(s, zs[i % 3][:, :], ACT.Abs))
                        chain(act.activation(s, s, ACT.Exp, scale=-1.0))
                        logs.by(act.activation(s, s, ACT.Ln, bias=1.0))
                    u = i - 1
                    if 0 <= u < NH:
                        act.wait_ge(args_.h, (u + 1) * NT)
                        exped.by(act.activation(aw[u % 2][:, :], aw[u % 2][:, :], ACT.Exp))
                    u = i - 2
                    if 0 <= u < NH:
                        p0 = u % 2 * HD
                        act.wait_ge(weighed.h, u + 1)
                        otk.by(act.activation(oT[p0:p0 + HD, 4 + u // 2, :], bank[7][p0:p0 + HD, :], ACT.Copy))

            @block.vector
            def _(dve):
                chain = Chain(dve, dve_chain)
                for i in range(NH + 1):
                    if i < NH:
                        s = sp_[i % 2]
                        dve.wait_ge(logs.h, i + 1)
                        chain(dve.scalar_tensor_tensor(s[:, :], zs[i % 3][:, :], 0.0, s[:, :], ALU.max, ALU.add))
                        for b in range(NT):
                            ins = dve.tensor_tensor(s[:, at_b[b]:at_b[b] + P], s[:, at_b[b]:at_b[b] + P], past[:, :], ALU.mult)
                        masked.by(ins)
                    u = i - 1
                    if 0 <= u < NH:
                        w = aw[u % 2]
                        if u >= 2:
                            dve.wait_ge(weighed.h, u - 1)
                        for b in range(NT):
                            dve.wait_ge(summed.h, u * NT + b + 1)
                            x = slice(at_b[b], at_b[b] + W[b])
                            chain(dve.tensor_tensor(w[:, x], zs[u % 3][:, x], bank[4 + (u * NT + b) % 3][:, 0:W[b]], ALU.subtract))
                            args_.by(dve.tensor_scalar(w[:, x], w[:, x], 0.0, None, ALU.min))
                        dve.wait_ge(exped.h, u + 1)
                        for b in range(NT):
                            ins = dve.tensor_tensor(w[:, at_b[b]:at_b[b] + P], w[:, at_b[b]:at_b[b] + P], past[:, :], ALU.mult)
                        cut.by(ins)

    def final():
        with ExitStack() as ctx:
            y = sb(ctx, "y", [P, KD, S])
            res = sb(ctx, "res", [P, NT, 2, 4, P])

            def finish(dve, chain, k, rstd):
                chain(dve.scalar_tensor_tensor(y[:, k, :], xT[:, k, :], col("final_norm", k), rstd, ALU.mult, ALU.mult))
            norm(lambda k: xT[:, k, :], KD, None, None, D, EPS, finish)
            turn([(res[:, t, q, :, :], [y[:, 4 * q + m, t * P:(t + 1) * P] for m in range(4)]) for t in range(NT) for q in range(2)])
            stored = sig("stored")
            block = ctx.enter_context(stage())

            @block.sync
            def _(sp):
                sp.dma_start(out[0].rearrange("(t p) d -> p t d", p=P), res[:, :, :, :, :].rearrange("p t q m n -> p t (q m n)")).then_inc(stored.h, 16)
                sp.wait_ge(stored.h, 16)

    def tiles(ctx, n):
        return [sb(ctx, "tile", [P, S])[:, :] for _ in range(n)]

    setup()

    def layer_one():
        with ExitStack() as st:
            oT = sb(st, "oT", [P, KD, S])
            with ExitStack() as rw:
                r, k, v = (sb(rw, n, [P, 4, S]) for n in "rkv")
                zt, zg = sb(rw, "zt", [P, S]), sb(rw, "zg", [P, S])
                with ExitStack() as at:
                    qT, kd, vT = sb(at, "qT", [P, 4, S]), sb(at, "kd", [P, 2, S]), sb(at, "vT", [P, S])
                    with ExitStack() as pr:
                        hi, lo = sb(pr, "hi", [P, KD, S], F32R), sb(pr, "lo", [P, KD, S], F32R)
                        pad = [sb(pr, f"pad{i}", [P, S + 1]) for i in range(2)]
                        df = sb(pr, "df", [P, S])
                        shifted = sig("shifted")
                        s0 = state["s"]

                        def dst(m):
                            return (qT[:, m, :] if m < 4 else kd[:, m - 4, :] if m < 6 else vT[:, :] if m == 6
                                    else r[:, m - 7, :] if m < 11 else k[:, m - 11, :] if m < 15
                                    else v[:, m - 15, :] if m < 19 else (zt, zg)[m - 19][:, :])

                        def put(act, m, acc):
                            if m < 7:
                                return act.activation(dst(m), acc, ACT.Copy)
                            if m >= 9:
                                act.wait_ge(shifted.h, m - 8)
                            return act.activation(pad[m % 2][:, 1:S + 1], acc, ACT.Copy)

                        def post(dve, chain, m):
                            if m == 0:
                                chain(dve.memset(pad[0][:, 0:1], 0.0))
                                chain(dve.memset(pad[1][:, 0:1], 0.0))
                            if m < 7:
                                return
                            x = pad[m % 2]
                            chain(dve.tensor_tensor(df[:, :], x[:, 0:S], x[:, 1:S + 1], ALU.subtract))
                            shifted.by(dve.scalar_tensor_tensor(dst(m), df[:, :], col("mix", m - 7), x[:, 1:S + 1], ALU.mult, ALU.add))
                            dve.wait_ge(shifted.h, m - 6)
                        lead = Lead(lambda k: col("norm_mix_pre", k), hi, lo, tiles(pr, 8))
                        project(21, hi, lo, put, post, lead)
                    local_attention(qT, kd, vT, oT)
                rwkv(r, k, v, zt, zg, oT[:, 4:8, :], rw)

            with ExitStack() as pr:
                hi, lo, mixed = sb(pr, "hi", [P, KD, S], F32R), sb(pr, "lo", [P, KD, S], F32R), sb(pr, "mixed", [P, KD, S])
                project(8, hi, lo, lambda act, m, acc: act.activation(mixed[:, m, :], acc, ACT.Copy), lead=Cut(oT, hi, lo))
                add_normed(mixed, "norm_mix_post")
    layer_one()
    with ExitStack() as st:
        f = sb(st, "f", [P, KD, S])
        with ExitStack() as ff:
            hi, lo = sb(ff, "hi", [P, KD, S], F32R), sb(ff, "lo", [P, KD, S], F32R)
            for ch in range(2):
                ffn(wu1, FF1, wd1, conv1, 16 * ch, 16, PARTS1, hi, lo, ACT.Gelu_apprx_tanh, ch == 1, f,
                    (lambda scratch: Lead(lambda k: col("norm_ffn_pre", k), hi, lo, scratch)) if ch == 0 else None)
        add_normed(f, "norm_ffn_post")
    with ExitStack() as two:
        cosT, sinT = sb(two, "cosT", [P, S]), sb(two, "sinT", [P, S])
        tables(cosT, sinT)
        for layer in range(2):
            with ExitStack() as st:
                oT = sb(st, "oT", [P, KD, S])
                (even_mixer, odd_mixer)[layer](cosT, sinT, oT)
                with ExitStack() as pr:
                    hi, lo = sb(pr, "hi", [P, KD, S], F32R), sb(pr, "lo", [P, KD, S], F32R)
                    project(8, hi, lo, None, lambda dve, chain, m, acc: dve.tensor_tensor(xT[:, m, :], acc, xT[:, m, :], ALU.add),
                            Cut(oT, hi, lo))
            with ExitStack() as ff:
                hi, lo = sb(ff, "hi", [P, KD, S], F32R), sb(ff, "lo", [P, KD, S], F32R)
                ffn(wu2[layer], FF2, wd2[layer], conv2[layer], 0, 22, PARTS2, hi, lo, ACT.Silu, True, xT,
                    lambda scratch: Lead(lambda k: col("ffn_norm", KD * layer + k), hi, lo, scratch))
    final()


_OUTS = [((1, S, D), "float32")]


def kernel(**inputs):
    import numpy as _np
    import concourse.bacc as _bacc
    from concourse import mybir as _mybir
    from concourse.bass_utils import run_bass_kernel_spmd as _run

    nc = _bacc.Bacc("TRN2", target_bir_lowering=False, num_devices=1)
    arrays, args = {}, {}
    inputs["cst"] = constants()
    for name, value in inputs.items():
        v = _np.ascontiguousarray(value)
        arrays[f"in_{name}_dram"] = v
        args[name] = nc.dram_tensor(f"in_{name}_dram", v.shape, _mybir.dt.from_np(v.dtype), kind="ExternalInput").ap()
    out = nc.dram_tensor("out_0_dram", (1, S, D), F32, kind="ExternalOutput").ap()
    program(nc, args, out)
    r = _run(nc, [arrays], core_ids=[0])
    return r.results[0]["out_0_dram"]
```

```python
from contextlib import ExitStack, contextmanager
import math

import numpy as np
import concourse.bass as bass
from concourse import mybir

ALU = mybir.AluOpType
ACT = mybir.ActivationFunctionType
AX = mybir.AxisListType
F32 = mybir.dt.float32
F32R = mybir.dt.float32r

P = 128
D = 1024
KD = D // P
S = 512
NT = S // P
HD = 64
NH = 8
C = 64
NCH = S // C
LEVELS = int(math.log2(C))
FF1, FF2 = 4096, 2816
TOPK = 128
ROT = 16
NEG = -1e30
BUCKETS, WINDOW = 32, 128
RLEN = 384
EPS = 1e-6
GN_EPS = 64e-5
EHALF = math.exp(-0.5)

CST = {}
_at = 0
for _name, _w in (("ident", P), ("ones", P), ("pair", P), ("swap", P), ("level", P * LEVELS),
                  ("before", P), ("upto", P), ("future", P), ("past_t", P), ("after_t", P),
                  ("inside", S), ("freq", 2), ("onehot", RLEN)):
    CST[_name] = (_at, _at + _w)
    _at += _w
CST_W = _at


def t5_bucket(n):
    exact = BUCKETS // 2
    if n < exact:
        return n
    f = np.float32
    large = exact + int(f(np.log(f(n) / f(exact))) / f(math.log(P / exact)) * f(BUCKETS - exact))
    return min(large, BUCKETS - 1)


def constants():
    c = np.zeros((P, CST_W), np.float32)

    def put(name, a):
        lo, hi = CST[name]
        c[:a.shape[0], lo:hi] = a

    i = np.arange(P)
    row, col = i[:, None], i[None, :]
    same = row // C == col // C
    put("ident", np.eye(P))
    put("ones", np.ones((P, P)))
    put("pair", row // HD == col // HD)
    half = ROT // 2
    swap = np.zeros((P, P))
    for m in range(P):
        if m % HD < ROT:
            swap[m - m % HD + (m % HD + half) % ROT, m] = 1
    put("swap", swap)
    put("level", np.concatenate(
        [(row >> l + 1 == col >> l + 1) & (row >> l & 1 == 1) & (col >> l & 1 == 0) for l in range(LEVELS)], 1))
    put("before", same & (row < col))
    put("upto", same & (row <= col))
    put("future", np.where(col > row, NEG, 0))
    put("past_t", row < col)
    put("after_t", row >= col)
    put("inside", np.tile(np.arange(S) % C != 0, (P, 1)))
    inv = np.float32(500000.0) ** (-np.arange(0, ROT, 2, dtype=np.float32) / np.float32(ROT))
    f = np.zeros((P, 2), np.float32)
    for m in range(P):
        if m % HD < ROT:
            f[m] = inv[m % HD % half], (-1 if m % HD < half else 1)
    put("freq", f)
    hot = np.zeros((BUCKETS + 1, RLEN), np.float32)
    for x in range(RLEN):
        n = 2 * P - 1 - x
        if 0 <= n < WINDOW:
            hot[t5_bucket(n), x] = 1
        else:
            hot[BUCKETS, x] = NEG
    put("onehot", hot)
    return c


class Signal:

    def __init__(self, handle):
        self.h, self.n = handle, 0

    def by(self, ins):
        ins.then_inc(self.h, 1)
        self.n += 1
        return ins


class Chain:

    def __init__(self, eng, signal, turn=None):
        self.eng, self.s, self.turn = eng, signal, turn

    def __call__(self, ins):
        self.s.by(ins)
        self.eng.wait_ge(self.s.h, self.s.n if self.turn is None else self.turn + self.s.n)


def program(nc, a, out):
    whole = ExitStack()
    with whole:
        _program(nc, a, out, whole)


def _program(nc, a, out, whole):
    names = [0]

    def sb(ctx, name, shape, dt=F32):
        names[0] += 1
        return ctx.enter_context(nc.sbuf_tensor(f"{name}_{names[0]}", shape, dt))

    here, stale, clear = [], [], []

    def sig(name, kept=False):
        names[0] += 1
        h = clear.pop() if clear and not kept else whole.enter_context(nc.semaphore(f"{name}_{names[0]}"))
        if not kept:
            here.append(h)
        return Signal(h)

    @contextmanager
    def stage(params=None):
        with nc.Block() as block:
            yield block
            old = list(stale)

            @block.gpsimd
            def _(pool):
                for h in old:
                    pool.sem_clear(h)
                if params:
                    params(pool)
        clear.extend(stale)
        stale[:] = here
        here.clear()

    banks = whole.enter_context(nc.psum_tensor("banks", [P, 8, 512], F32))
    bank = [banks[:, i, :] for i in range(8)]

    scratch = nc.dram_tensor("scratch", (NH, P, RLEN), F32, kind="Internal").ap()
    xT = sb(whole, "xT", [P, KD, S])
    cst = sb(whole, "cst", [P, 3 * P])
    ident, ones, pair = (cst[:, i * P:(i + 1) * P] for i in range(3))
    cosT, sinT = sb(whole, "cosT", [P, S]), sb(whole, "sinT", [P, S])
    NROW = 116
    pcol = sb(whole, "pcol", [P, NROW])
    conv1 = sb(whole, "conv1", [P, 4, 2 * FF1 // P])
    conv2 = [sb(whole, f"conv2{i}", [P, 4, 2 * FF2 // P]) for i in range(2)]

    vec, rows_of = {}, []
    at = 0
    for name, ap in (("norm_mix_pre", a["norm_mix_pre"]), ("norm_mix_post", a["norm_mix_post"]),
                     ("norm_ffn_pre", a["norm_ffn_pre"]), ("norm_ffn_post", a["norm_ffn_post"]),
                     ("mix", a["rwkv_shift_mix"]), ("w0", a["w0"]), ("a0", a["a0"]), ("k_k", a["k_k"]),
                     ("k_a", a["k_a"]), ("r_k", a["r_k"].rearrange("a h d -> a (h d)")),
                     ("ln_g", a["ln_x_g"]), ("ln_b", a["ln_x_b"]),
                     ("attn_norm", a["attn_norm_2"].rearrange("(o l) d -> o (l d)", o=1)),
                     ("ffn_norm", a["ffn_norm_2"].rearrange("(o l) d -> o (l d)", o=1)),
                     ("final_norm", a["final_norm_2"].rearrange("(o d) -> o d", o=1)),
                     ("subln", a["ev_subln_2"]), ("kv_norm", a["od_kv_norm_2"])):
        n = ap.shape[1] // P
        vec[name] = at
        rows_of.append((at, n, ap.rearrange("o (m p) -> (o m) p", p=P)))
        at += n
    assert at == NROW, at

    def col(name, m=0):
        return pcol[:, vec[name] + m:vec[name] + m + 1]

    RAW, CUT, AHEAD = 2, 4, 2
    LOADED = RAW + AHEAD
    raw = [sb(whole, f"raw{i}", [P, KD, P]) for i in range(RAW)]
    whi = [sb(whole, f"whi{i}", [P, KD, P], F32R) for i in range(CUT)]
    wlo = [sb(whole, f"wlo{i}", [P, KD, P], F32R) for i in range(CUT)]
    loaded = [sig(f"w_loaded{i}", True) for i in range(RAW)]
    w_hi, w_lo, w_used = (sig(n, True) for n in ("w_hi", "w_lo", "w_used"))

    def rows(w, r0, nr, c0, nc_=P):
        return w[r0:r0 + nr * P, bass.ds(c0, nc_)].rearrange("(k p) n -> p k n", p=P)

    def tile_of(w, c0, r0=0, nr=KD):
        return lambda slot: [(slot[:, 0:nr, :], rows(w, r0, nr, c0))]

    def twice(w, c0):
        return lambda slot: [(slot[:, :, 0:HD], rows(w, 0, KD, c0, HD)), (slot[:, :, HD:P], rows(w, 0, KD, c0, HD))]

    w1, wo1 = a["w_in"][0], a["w_out"][0]
    wu1, wd1 = a["w_ffn_up"][0], a["w_ffn_down"][0]
    we, woe = a["ev_w_in_2"][0], a["ev_w_out_2"][0]
    wd, wod = a["od_w_in_2"][0], a["od_w_out_2"][0]
    wu2, wd2 = a["ffn_w_in_2"], a["ffn_w_out_2"]

    in1 = [tile_of(w1, 128 * m) for m in range(4)] + [twice(w1, 512), twice(w1, 576), tile_of(w1, 640)] \
        + [tile_of(w1, 768 + 128 * m) for m in range(14)]
    in_ev = [tile_of(we, c0) for c0 in [1536] + [o + 128 * m for o in (1024, 0, 512, 2568, 1544, 2056) for m in range(4)]]
    in_od = [tile_of(wd, 656 + 128 * m) for m in range(2)] + [twice(wd, 916), tile_of(wd, 912)] \
        + [tile_of(wd, 128 * m) for m in range(4)] + [twice(wd, 640), tile_of(wd, 512)] \
        + [tile_of(wd, 980 + 128 * m) for m in range(12)]

    def up_slots(w, ff, first, pairs):
        return [tile_of(w, o + 128 * (first + m)) for m in range(pairs) for o in (0, ff)]

    def down_slots(w, first, parts):
        return [tile_of(w, 128 * m, 128 * (first + k), n) for m in range(KD) for k, n in parts]

    PARTS1 = [(0, 8), (8, 8)]
    PARTS2 = [(0, 6), (6, 6), (12, 5), (17, 5)]
    plan = list(in1) + [tile_of(wo1, 128 * m) for m in range(8)]
    for ch in range(2):
        plan += up_slots(wu1, FF1, 16 * ch, 16) + down_slots(wd1, 16 * ch, PARTS1)
    for layer in range(2):
        plan += (in_ev, in_od)[layer] + [tile_of((woe, wod)[layer], 128 * m) for m in range(8)]
        plan += up_slots(wu2[layer], FF2, 0, 22) + down_slots(wd2[layer], 0, PARTS2)
    state = {"s": 0}

    def load(sp, s):
        if s >= len(plan):
            return
        if s >= RAW:
            sp.wait_ge(w_lo.h, s - RAW + 1)
        for dst, src in plan[s](raw[s % RAW]):
            sp.dma_start(dst, src).then_inc(loaded[s % RAW].h, 16)

    arrived = {}
    for s_ in range(len(plan)):
        n_ = len(plan[s_](raw[s_ % RAW]))
        arrived[s_] = (arrived[s_ - RAW] if s_ >= RAW else 0) + 16 * n_

    height = [plan[s_](raw[s_ % RAW])[0][0].shape[1] for s_ in range(len(plan))]

    def split_hi(act, s):
        if s >= len(plan):
            return
        act.wait_ge(loaded[s % RAW].h, arrived[s])
        if s >= CUT:
            act.wait_ge(w_used.h, s - CUT + 1)
        n = height[s]
        w_hi.by(act.activation(whi[s % CUT][:, 0:n, :], raw[s % RAW][:, 0:n, :], ACT.Copy))

    def lower(pool, b, c, n):
        return pool.tensor_tensor(wlo[c][:, 0:n, :], raw[b][:, 0:n, :], whi[c][:, 0:n, :].bitcast(F32), ALU.subtract)

    def split_lo(pool, s):
        if s >= len(plan):
            return
        pool.wait_ge(w_hi.h, s + 1)
        w_lo.by(lower(pool, s % RAW, s % CUT, height[s]))

    def three_passes(pe, acc, b, n, hi, lo, first, last, ready=None):
        for k in range(n):
            if ready:
                pe.wait_ge(ready.h, k + 1)
            pe.matmul(acc, whi[b][:, k, :], hi(k), start=first and k == 0, stop=False)
            pe.matmul(acc, whi[b][:, k, :], lo(k), start=False, stop=False)
            mm = pe.matmul(acc, wlo[b][:, k, :], hi(k), start=False, stop=last and k == n - 1)
        return mm

    act_chain, dve_chain = sig("act_chain", True), sig("dve_chain", True)

    def cst_dma(sp, dst, name, signal, rows_=P):
        lo, hi = CST[name]
        sp.dma_start(dst, a["cst"][0:rows_, lo:hi]).then_inc(signal.h, 16)

    class Tables:
        MAGIC = 1.5 * 2.0 ** 23
        C1 = 6.28125
        C2 = 0.00193500518798828125
        C3 = 2 * math.pi - C1 - C2

        def __init__(self, ctx, cosT, sinT):
            self.cosT, self.sinT = cosT[:, :], sinT[:, :]
            self.pi, self.fr = sb(ctx, "pi", [P, S], mybir.dt.int32)[:, :], sb(ctx, "fr", [P, 2])
            self.ang, self.n, self.r = (sb(ctx, x, [P, S])[:, :] for x in ("ang", "n", "r"))
            self.got, self.reduced, self.sined = sig("got"), sig("reduced"), sig("sined")

        def sp(self, sp):
            sp.dma_start(self.pi, a["positions_2"][0:1, :].broadcast_to([P, S])).then_inc(self.got.h, 16)
            cst_dma(sp, self.fr[:, :], "freq", self.got)

        def dve(self, dve, chain):
            ang, n, r = self.ang, self.n, self.r
            dve.wait_ge(self.got.h, 32)
            chain(dve.tensor_copy(ang, self.pi))
            chain(dve.tensor_scalar(ang, ang, self.fr[:, 0:1], None, ALU.mult))
            chain(dve.tensor_scalar(n, ang, 1 / (2 * math.pi), None, ALU.mult))
            chain(dve.tensor_scalar(n, n, self.MAGIC, None, ALU.add))
            chain(dve.tensor_scalar(n, n, -self.MAGIC, None, ALU.add))
            for c in (self.C1, self.C2, self.C3):
                chain(dve.scalar_tensor_tensor(ang, n, -c, ang, ALU.mult, ALU.add))
            chain(dve.tensor_scalar(ang, ang, 3.1415925, -3.1415925, ALU.min, ALU.max))
            self.reduced.by(dve.tensor_scalar(r, ang, 0.5, None, ALU.mult))

        def act(self, act):
            act.wait_ge(self.reduced.h, 1)
            act.activation(self.sinT, self.ang, ACT.Sin).then_inc(self.sined.h, 1)
            act.activation(self.r, self.r, ACT.Sin).then_inc(self.sined.h, 1)

        def last_dve(self, dve, chain):
            dve.wait_ge(self.sined.h, 2)
            chain(dve.tensor_tensor(self.r, self.r, self.r, ALU.mult))
            chain(dve.tensor_scalar(self.cosT, self.r, -2.0, 1.0, ALU.mult, ALU.add))
            chain(dve.tensor_scalar(self.sinT, self.sinT, self.fr[:, 1:2], None, ALU.mult))

    def setup():
        with ExitStack() as ctx:
            xin = sb(ctx, "xin", [P, NT, D])
            prow = sb(ctx, "prow", [P, P])
            c1row = sb(ctx, "c1row", [2 * FF1 // P, 4, P])
            c2row = sb(ctx, "c2row", [2 * FF2 // P, 2, 4, P])
            tables = Tables(ctx, cosT, sinT)
            s_x, s_p, s_c, turned, taken = sig("s_x"), sig("s_p", True), sig("s_c"), sig("turned"), sig("taken")

            def params(pool):
                for first, n, ap in rows_of:
                    pool.dma_start(prow[first:first + n, :], ap).then_inc(s_p.h, 16)
                for s in range(AHEAD):
                    split_lo(pool, s)
            block = ctx.enter_context(stage(params))

            @block.sync
            def _(sp):
                sp.dma_start(cst[:, :], a["cst"][:, 0:3 * P]).then_inc(s_x.h, 16)
                sp.dma_start(xin[:, :, :], a["x"][0].rearrange("(t p) d -> p t d", p=P)).then_inc(s_x.h, 16)
                tables.sp(sp)
                for s in range(LOADED):
                    load(sp, s)

            n_params = 16 * len(rows_of)

            @block.tensor
            def _(pe):
                pe.wait_ge(s_x.h, 32)
                for k in range(KD):
                    for t in range(NT):
                        mm = pe.transpose(bank[k][:, t * P:(t + 1) * P], xin[:, t, k * P:(k + 1) * P], ident)
                    mm.then_inc(turned.h, 1)
                pe.wait_ge(s_p.h, n_params)
                pe.wait_ge(taken.h, 4)
                mm = pe.transpose(bank[0][:, 0:NROW], prow[0:NROW, :], ident[0:NROW, 0:NROW])
                mm.then_inc(turned.h, 1)
                n1, n2 = 2 * FF1 // P, 2 * FF2 // P
                pe.wait_ge(s_c.h, 6 * 16)
                for t in range(4):
                    mm = pe.transpose(bank[1][:, t * n1:(t + 1) * n1], c1row[:, t, :], ident[0:n1, 0:n1])
                mm.then_inc(turned.h, 1)
                for l in range(2):
                    for t in range(4):
                        mm = pe.transpose(bank[2 + l][:, t * n2:(t + 1) * n2], c2row[:, l, t, :], ident[0:n2, 0:n2])
                    mm.then_inc(turned.h, 1)

            @block.vector
            def _(dve):
                chain = Chain(dve, dve_chain)
                tables.dve(dve, chain)
                for k in range(KD):
                    dve.wait_ge(turned.h, k + 1)
                    dve.tensor_copy(xT[:, k, :], bank[k][:, :]).then_inc(taken.h, 1)
                n1, n2 = 2 * FF1 // P, 2 * FF2 // P
                dve.wait_ge(turned.h, KD + 1)
                dve.tensor_copy(pcol[:, :], bank[0][:, 0:NROW])
                dve.wait_ge(turned.h, KD + 2)
                dve.tensor_copy(conv1[:, :, :].rearrange("p t n -> p (t n)"), bank[1][:, 0:4 * n1])
                dve.wait_ge(turned.h, KD + 4)
                for l in range(2):
                    dve.tensor_copy(conv2[l][:, :, :].rearrange("p t n -> p (t n)"), bank[2 + l][:, 0:4 * n2])
                tables.last_dve(dve, chain)

            @block.scalar
            def _(act):
                for dst, w, b in [(c1row[:, :, :], a["conv_w"][0], a["conv_b"][0:1])] \
                        + [(c2row[:, l, :, :], a["ffn_conv_w_2"][l], a["ffn_conv_b_2"][l:l + 1]) for l in range(2)]:
                    act.dma_start(dst[:, 0:3, :], w.rearrange("t (m p) -> m t p", p=P)).then_inc(s_c.h, 16)
                    act.dma_start(dst[:, 3, :], b.rearrange("o (m p) -> (o m) p", p=P)).then_inc(s_c.h, 16)
                tables.act(act)
                for s in range(AHEAD):
                    split_hi(act, s)

    class Rstd:

        def __init__(self, ctx, n, width, eps, base):
            self.n, self.width, self.eps, self.base = n, width, eps, base
            self.st = sb(ctx, "st", [P, 3, NT * n])
            self.ready, self.meaned, self.rooted, self.inverted, self.spread = (
                sig(x) for x in ("sums", "meaned", "rooted", "inverted", "spread"))

        def sums(self, pe, q, tile):
            for t in range(NT):
                mm = pe.matmul(bank[self.base - t][:, q:q + 1], tile[:, t * P:(t + 1) * P], ones[:, 0:1], start=True, stop=True)
            return mm

        def pe(self, pe):
            pe.wait_ge(self.inverted.h, 1)
            for q in range(self.n):
                for t in range(NT):
                    x = (NT - 1 - t) * self.n + q
                    mm = pe.matmul(bank[self.base - q][:, t * P:(t + 1) * P], self.st[:, 2, x:x + 1].broadcast_to([P, P]), ident,
                                   start=True, stop=True)
                mm.then_inc(self.spread.h, 1)

        def act(self, act):
            act.wait_ge(self.meaned.h, 1)
            act.activation(self.st[:, 1, :], self.st[:, 0, :], ACT.Sqrt).then_inc(self.rooted.h, 1)

        def dve(self, dve):
            dve.wait_ge(self.ready.h, 1)
            lowest = self.base - NT + 1
            dve.tensor_scalar(self.st[:, 0, :].rearrange("p (t q) -> p t q", t=NT), banks[:, lowest:self.base + 1, 0:self.n], 1.0 / self.width, self.eps,
                              ALU.mult, ALU.add)\
               .then_inc(self.meaned.h, 1)
            dve.wait_ge(self.rooted.h, 1)
            dve.reciprocal(self.st[:, 2, :], self.st[:, 1, :]).then_inc(self.inverted.h, 1)

        def of(self, q=0):
            return bank[self.base - q][:, :]

    def norm(src, n, width, eps, finish, groups=1):
        with ExitStack() as ctx:
            sq = sb(ctx, "sq", [P, n, S])
            squared, added = sig("squared"), sig("added")
            rs = Rstd(ctx, groups, width, eps, 7)
            per = n // groups
            block = ctx.enter_context(stage())

            @block.scalar
            def _(act):
                for k in range(n):
                    squared.by(act.activation(sq[:, k, :], src(k), ACT.Square))
                rs.act(act)

            @block.tensor
            def _(pe):
                for q in range(groups):
                    if per > 1:
                        pe.wait_ge(added.h, (q + 1) * (per - 1))
                    else:
                        pe.wait_ge(squared.h, q + 1)
                    mm = rs.sums(pe, q, sq[:, q * per, :])
                rs.ready.by(mm)
                rs.pe(pe)

            @block.vector
            def _(dve):
                chain = Chain(dve, dve_chain)
                for k in range(n):
                    if k % per:
                        x = sq[:, k - k % per, :]
                        dve.wait_ge(squared.h, k + 1)
                        dve.tensor_tensor(x, x, sq[:, k, :], ALU.add).then_inc(added.h, 1)
                        added.n += 1
                        dve.wait_ge(added.h, added.n)
                rs.dve(dve)
                for k in range(n):
                    dve.wait_ge(rs.spread.h, k // per + 1)
                    finish(dve, chain, k, rs.of(k // per))

    class Lead:

        def __init__(self, ctx, scale, hi, lo, scratch):
            self.scale, self.hi, self.lo = scale, hi, lo
            self.sq, self.h, self.acc = scratch[0:2], scratch[2:4], scratch[4]
            self.squared, self.summed, self.scaled, self.uppered, self.ready = (
                sig(n) for n in ("squared", "summed", "scaled", "uppered", "ready"))
            self.rs = Rstd(ctx, 1, D, EPS, 7)

        def pe(self, pe):
            pe.wait_ge(self.summed.h, KD - 1)
            self.rs.ready.by(self.rs.sums(pe, 0, self.acc))
            self.rs.pe(pe)

        def act(self, act):
            for k in range(KD):
                if k >= 3:
                    act.wait_ge(self.summed.h, k - 2)
                act.activation(self.sq[k % 2] if k else self.acc, xT[:, k, :], ACT.Square).then_inc(self.squared.h, 1)
            self.rs.act(act)
            for k in range(KD):
                act.wait_ge(self.scaled.h, k + 1)
                act.activation(self.hi[:, k, :], self.h[k % 2], ACT.Copy).then_inc(self.uppered.h, 1)

        def dve(self, dve, chain):
            for k in range(1, KD):
                dve.wait_ge(self.squared.h, k + 1)
                dve.tensor_tensor(self.acc, self.acc, self.sq[k % 2], ALU.add).then_inc(self.summed.h, 1)
                dve.wait_ge(self.summed.h, k)
            self.rs.dve(dve)
            dve.wait_ge(self.rs.spread.h, 1)
            for k in range(KD + 1):
                if k < KD:
                    dve.scalar_tensor_tensor(self.h[k % 2], xT[:, k, :], self.scale(k), self.rs.of(), ALU.mult, ALU.mult).then_inc(self.scaled.h, 1)
                if k >= 1:
                    dve.wait_ge(self.uppered.h, k)
                    dve.tensor_tensor(self.lo[:, k - 1, :], self.h[(k - 1) % 2], self.hi[:, k - 1, :].bitcast(F32), ALU.subtract)\
                       .then_inc(self.ready.h, 1)
                    dve.wait_ge(self.ready.h, k)

    class Cut:

        def __init__(self, src, hi, lo):
            self.src, self.hi, self.lo, self.uppered, self.ready = src, hi, lo, sig("uppered"), sig("ready")

        def pe(self, pe):
            pass

        def act(self, act):
            for k in range(KD):
                act.activation(self.hi[:, k, :], self.src[:, k, :], ACT.Copy).then_inc(self.uppered.h, 1)

        def dve(self, dve, chain):
            for k in range(KD):
                dve.wait_ge(self.uppered.h, k + 1)
                dve.tensor_tensor(self.lo[:, k, :], self.src[:, k, :], self.hi[:, k, :].bitcast(F32), ALU.subtract).then_inc(self.ready.h, 1)

    class Side:

        def sp(self, sp):
            pass

        def first_pe(self, pe):
            pass

        def pe(self, pe, free, m):
            pass

        def first_act(self, act):
            pass

        def act(self, act, m):
            pass

        def dve(self, dve, chain, free):
            pass

    class Rotate:

        def __init__(self, ctx, cosT, sinT):
            self.sw, self.t = sb(ctx, "sw", [P, P]), sb(ctx, "rotated", [P, 2, S])
            self.cosT, self.sinT, self.n, self.m = cosT, sinT, 0, 0
            self.got, self.swapped, self.used, self.turned = sig("got"), sig("swapped"), sig("used"), sig("turned")

        def sp(self, sp):
            cst_dma(sp, self.sw[:, :], "swap", self.got)

        def pe(self, pe, x):
            n, self.n = self.n, self.n + 1
            if n == 0:
                pe.wait_ge(self.got.h, 16)
            if n >= 3:
                pe.wait_ge(self.used.h, n - 2)
            pe.matmul(bank[4 + n % 3][:, :], self.sw[:, :], x, start=True, stop=True).then_inc(self.swapped.h, 1)

        def dve(self, dve, x):
            n, self.m = self.m, self.m + 1
            dve.wait_ge(self.swapped.h, n + 1)
            if n >= 2:
                dve.wait_ge(self.turned.h, 2 * n - 2)
            self.used.by(dve.tensor_tensor(self.t[:, n % 2, :], bank[4 + n % 3][:, :], self.sinT[:, :], ALU.mult))
            self.turned.by(dve.tensor_tensor(x, x, self.cosT[:, :], ALU.mult))
            dve.wait_ge(self.used.h, n + 1)
            dve.wait_ge(self.turned.h, 2 * n + 1)
            self.turned.by(dve.tensor_tensor(x, x, self.t[:, n % 2, :], ALU.add))

    def project(n, hi, lo, put, post=None, lead=None, side=None):
        s0 = state["s"]
        done, free = sig("done"), sig("free")
        side = side or Side()
        with ExitStack() as ctx:
            def pool_part(pool):
                for m in range(n):
                    split_lo(pool, s0 + m + AHEAD)
            block = ctx.enter_context(stage(pool_part))

            @block.sync
            def _(sp):
                side.sp(sp)
                for m in range(n):
                    load(sp, s0 + LOADED + m)

            @block.tensor
            def _(pe):
                if lead:
                    lead.pe(pe)
                side.first_pe(pe)
                for m in range(n):
                    s = s0 + m
                    pe.wait_ge(w_lo.h, s + 1)
                    if m >= 4:
                        pe.wait_ge(free.h, m - 3)
                    w_used.by(three_passes(pe, bank[m % 4][:, :], s % CUT, KD, lambda k: hi[:, k, :], lambda k: lo[:, k, :], True, True,
                                           lead.ready if lead and m == 0 else None))
                    if m >= 1:
                        side.pe(pe, free, m - 1)
                side.pe(pe, free, n - 1)

            @block.scalar
            def _(act):
                if lead:
                    lead.act(act)
                side.first_act(act)
                for m in range(n):
                    split_hi(act, s0 + m + AHEAD)
                    if put:
                        act.wait_ge(w_used.h, s0 + m + 1)
                        free.by(put(act, m, bank[m % 4][:, :]))
                        side.act(act, m)

            @block.vector
            def _(dve):
                chain = Chain(dve, dve_chain)
                if lead:
                    lead.dve(dve, chain)
                side.dve(dve, chain, free)
                for m in range(n if post else 0):
                    if not put:
                        dve.wait_ge(w_used.h, s0 + m + 1)
                        free.by(post(dve, chain, m, bank[m % 4][:, :]))
                    else:
                        dve.wait_ge(free.h, m + 1)
                        post(dve, chain, m)
        state["s"] += n

    def ffn(w_up, ff, w_down, conv, first, pairs, parts, hi, lo, func, add, acc_to, make_lead=None):
        with ExitStack() as ctx:
            ghi = sb(ctx, "ghi", [P, pairs, S], F32R)
            glo = sb(ctx, "glo", [P, pairs, S], F32R)
            cb = [sb(ctx, f"cb{j}", [P, S]) for j in range(4)]
            gate = [sb(ctx, f"gate{j}", [P, S]) for j in range(2)]
            gv = [sb(ctx, f"gv{j}", [P, S]) for j in range(2)]
            lead = make_lead(ctx, [t[:, :] for t in cb + gate]) if make_lead else None
            tapped, conved, gated, products, upper, split_ = (sig(n) for n in ("tapped", "conved", "gated", "products", "upper", "split"))
            taken = sig("taken")
            chain0 = dve_chain.n
            ff_tiles = ff // P
            up0, ups = state["s"], pairs // 2
            half = [0, ff_tiles, 1, ff_tiles + 1]
            dn0 = up0 + 4 * ups
            mts = 4 // len(parts)
            slots = [(mt, k0, n) for mt in range(mts) for k0, n in parts]
            dns = KD // mts
            end = dn0 + 4 * dns

            PER = 4 // RAW * 16

            def hi_in_loop(act, s, i, n):
                act.wait_ge(loaded[s % RAW].h, i * PER + arrived[s])
                act.wait_ge(w_used.h, i * 4 + (s - CUT + 1))
                act.activation(whi[s % CUT][:, 0:n, :], raw[s % RAW][:, 0:n, :], ACT.Copy).then_inc(w_hi.h, 1)

            def lo_in_loop(pool, s, i, n):
                pool.wait_ge(w_hi.h, i * 4 + (s + 1))
                lower(pool, s % RAW, s % CUT, n).then_inc(w_lo.h, 1)

            def pool_part(pool):
                with pool.Fori(0, ups - 1) as i:
                    for j in range(4):
                        lo_in_loop(pool, up0 + j + AHEAD, i, KD)
                w_lo.n += 4 * (ups - 1)
                for s in range(dn0 - 4 + AHEAD, dn0 + AHEAD):
                    split_lo(pool, s)
                with pool.Fori(0, dns - 1) as i:
                    for j in range(4):
                        lo_in_loop(pool, dn0 + j + AHEAD, i, height[dn0 + j + AHEAD])
                w_lo.n += 4 * (dns - 1)
                for s in range(end - 4 + AHEAD, end + AHEAD):
                    split_lo(pool, s)
            block = ctx.enter_context(stage(pool_part))

            @block.sync
            def _(sp):
                def load_turns(s0, turns, src):
                    with sp.Fori(1, turns) as i:
                        for j in range(4):
                            sp.wait_ge(w_lo.h, i * 4 + (s0 + j - RAW + 1))
                            b, n = (s0 + j) % RAW, height[s0 + j]
                            sp.dma_start(raw[b][:, 0:n, :], src(i, j, n)).then_inc(loaded[b].h, 16)
                load_turns(up0, ups, lambda i, j, n: rows(w_up, 0, n, i * (2 * P) + P * (first + half[j])))
                for s in range(dn0, dn0 + LOADED):
                    load(sp, s)
                load_turns(dn0, dns, lambda i, j, n: rows(w_down, P * (first + slots[j][1]), n, i * (mts * P) + P * slots[j][0]))
                for s in range(end, end + LOADED):
                    load(sp, s)

            @block.tensor
            def _(pe):
                def up(i, hold):
                    for j in range(4):
                        pe.wait_ge(w_lo.h, i * 4 + (up0 + j + 1))
                        if hold:
                            pe.wait_ge(conved.h, i * 4 + (j - 3))
                        three_passes(pe, bank[j][:, :], (up0 + j) % CUT, KD, lambda k: hi[:, k, :], lambda k: lo[:, k, :], True, True,
                                     lead.ready if lead and not hold and j == 0 else None).then_inc(w_used.h, 1)
                if lead:
                    lead.pe(pe)
                up(0, False)
                with pe.Fori(1, ups) as i:
                    up(i, True)

                def down(i, hold):
                    for j, (mt, k0, n) in enumerate(slots):
                        pe.wait_ge(w_lo.h, i * 4 + (dn0 + j + 1))
                        if hold and k0 == 0:
                            pe.wait_ge(taken.h, (i - 1) * mts + (mt + 1))
                        if not hold:
                            pe.wait_ge(split_.h, k0 + n)
                        three_passes(pe, bank[4 + mt][:, :], (dn0 + j) % CUT, n, lambda k: ghi[:, k0 + k, :],
                                     lambda k: glo[:, k0 + k, :], k0 == 0, k0 + n == pairs).then_inc(w_used.h, 1)
                down(0, False)
                with pe.Fori(1, dns) as i:
                    down(i, True)

            @block.scalar
            def _(act):
                def turn(i, hold, last=False):
                    for j in range(4):
                        if last:
                            split_hi(act, dn0 - 4 + j + AHEAD)
                        else:
                            hi_in_loop(act, up0 + j + AHEAD, i, KD)
                        if j % 2 == 1:
                            act.wait_ge(conved.h, i * 4 + j)
                            act.activation(gate[j // 2][:, :], cb[j - 1][:, :], func).then_inc(gated.h, 1)
                        act.wait_ge(w_used.h, i * 4 + (up0 + j + 1))
                        if hold:
                            act.wait_ge(products.h, i * 2 + (j // 2 - 1))
                        c = i * 2 + (first + half[j])
                        act.activation(cb[j][:, :], bank[j][:, :], ACT.Identity,
                                       scale=conv[:, 2, bass.ds(c, 1)], bias=conv[:, 3, bass.ds(c, 1)])\
                           .then_inc(tapped.h, 1)
                if lead:
                    lead.act(act)
                turn(0, False)
                with act.Fori(1, ups - 1) as i:
                    turn(i, True)
                w_hi.n += 4 * (ups - 1)
                turn(ups - 1, True, True)
                with act.Fori(0, dns - 1) as i:
                    for j in range(4):
                        hi_in_loop(act, dn0 + j + AHEAD, i, height[dn0 + j + AHEAD])
                w_hi.n += 4 * (dns - 1)
                for s in range(end - 4 + AHEAD, end + AHEAD):
                    split_hi(act, s)

            @block.vector
            def _(dve):
                if lead:
                    lead.dve(dve, Chain(dve, dve_chain))
                chain0 = dve_chain.n

                def turn(i, base):
                    chain = Chain(dve, dve_chain, base)
                    for j in range(4):
                        dve.wait_ge(tapped.h, i * 4 + (j + 1))
                        c = i * 2 + (first + half[j])
                        chain(dve.scalar_tensor_tensor(cb[j][:, 1:S], bank[j][:, 0:S - 1], conv[:, 1, bass.ds(c, 1)],
                                                       cb[j][:, 1:S], ALU.mult, ALU.add))
                        dve.scalar_tensor_tensor(cb[j][:, 2:S], bank[j][:, 0:S - 2], conv[:, 0, bass.ds(c, 1)],
                                                 cb[j][:, 2:S], ALU.mult, ALU.add).then_inc(conved.h, 1)
                        if j % 2 == 1:
                            q = j // 2
                            dve.wait_ge(conved.h, i * 4 + (j + 1))
                            dve.wait_ge(gated.h, i * 2 + (q + 1))
                            dve.tensor_tensor(gv[q][:, :], gate[q][:, :], cb[j][:, :], ALU.mult).then_inc(products.h, 1)
                            dve.wait_ge(products.h, i * 2 + (q + 1))
                            dve.tensor_copy(ghi[:, i * 2 + q, :], gv[q][:, :]).then_inc(upper.h, 1)
                            dve.wait_ge(upper.h, i * 2 + (q + 1))
                            dve.tensor_tensor(glo[:, i * 2 + q, :], gv[q][:, :], ghi[:, i * 2 + q, :].bitcast(F32), ALU.subtract)\
                               .then_inc(split_.h, 1)
                            dve.wait_ge(split_.h, i * 2 + (q + 1))
                turn(0, 0)
                per = dve_chain.n - chain0
                dve_chain.n = chain0
                with dve.Fori(1, ups) as i:
                    turn(i, i * per)
                dve_chain.n = chain0 + per * ups
                with dve.Fori(0, dns) as i:
                    for j, (mt, k0, n) in enumerate(slots):
                        if k0 + n == pairs:
                            dve.wait_ge(w_used.h, i * 4 + (dn0 + j + 1))
                            m = i * mts + mt
                            if add:
                                dve.tensor_tensor(acc_to[:, m, :], bank[4 + mt][:, :], acc_to[:, m, :], ALU.add).then_inc(taken.h, 1)
                            else:
                                dve.tensor_copy(acc_to[:, m, :], bank[4 + mt][:, :]).then_inc(taken.h, 1)
            w_used.n += end - up0
            state["s"] = end

    def attend(units, dst_of, sink=None, lam=None):
        U, G = len(units), len(units[0][0])
        NB = 4 // G
        scored, ready, exped, normed, flipped, ptaken, weighed, otaken = (
            sig(n) for n in ("scored", "ready", "exped", "normed", "flipped", "ptaken", "weighed", "otaken"))
        with ExitStack() as ctx:
            sm = [sb(ctx, f"sm{i}", [P, G, S]) for i in range(2)]
            ex = [sb(ctx, f"ex{i}", [P, G, S]) for i in range(4)]
            pt = [sb(ctx, f"pt{i}", [P, S]) for i in range(2)]
            mx = [sb(ctx, f"mx{i}", [P, 5 * G]) for i in range(4)]
            block = ctx.enter_context(stage())

            def f(i, what, g=None):
                o = ("neg", "sum", "sink", "den", "inv").index(what) * G
                return mx[i % 4][:, o:o + G] if g is None else mx[i % 4][:, o + g:o + g + 1]

            @block.tensor
            def _(pe):
                for i in range(U + 4):
                    if i < U:
                        maps, w = units[i][0], units[i][1]
                        if i >= NB:
                            pe.wait_ge(ready.h, i - NB + 1)
                        for g, products in enumerate(maps):
                            for n, (q, k, c0) in enumerate(products):
                                mm = pe.matmul(bank[i % NB * G + g][:, c0:w], q, k, start=n == 0, stop=n == len(products) - 1,
                                               skip_group_check=len(products) > 1)
                        mm.then_inc(scored.h, 1)
                    u = i - 3
                    if 0 <= u < U:
                        pe.wait_ge(normed.h, u + 1)
                        if u >= 2:
                            pe.wait_ge(ptaken.h, u - 1)
                        for b in range(units[u][1] // P):
                            mm = pe.transpose(bank[4 + u % 2][:, b * P:(b + 1) * P], ex[u % 4][:, 0, b * P:(b + 1) * P], ident)
                        mm.then_inc(flipped.h, 1)
                    u = i - 4
                    if 0 <= u < U:
                        _, w, _, values, (r0, r1) = units[u]
                        pe.wait_ge(ptaken.h, u + 1)
                        if u >= 2:
                            pe.wait_ge(otaken.h, u - 1)
                        for b, v in enumerate(values):
                            mm = pe.matmul(bank[6 + u % 2][r0:r1, 0:P], v, pt[u % 2][:, b * P:(b + 1) * P],
                                           start=b == 0, stop=b == len(values) - 1)
                        mm.then_inc(weighed.h, 1)

            @block.vector
            def _(dve):
                chain = Chain(dve, dve_chain)
                for i in range(U + 1):
                    if i < U:
                        _, w, bias, _, _ = units[i]
                        dve.wait_ge(scored.h, i + 1)
                        if i >= 2:
                            dve.wait_ge(exped.h, i - 1)
                        for g in range(G):
                            ins = dve.tensor_tensor_reduce(sm[i % 2][:, g, 0:w], bank[i % NB * G + g][:, 0:w], bias, -HD ** -0.5,
                                                           3e38 if sink is None else sink(i)[1], ALU.add, ALU.min, f(i, "neg", g))
                        ready.by(ins)
                    u = i - 1
                    if 0 <= u < U:
                        w = units[u][1]
                        dve.wait_ge(exped.h, u + 1)
                        den = f(u, "sum")
                        if sink is not None:
                            chain(dve.tensor_tensor(f(u, "den"), f(u, "sum"), f(u, "sink"), ALU.add))
                            den = f(u, "den")
                        chain(dve.reciprocal(f(u, "inv"), den))
                        e = ex[u % 4]
                        if G == 1:
                            normed.by(dve.tensor_scalar(e[:, 0, 0:w], e[:, 0, 0:w], f(u, "inv"), None, ALU.mult))
                        else:
                            dve.tensor_scalar(f(u, "den", 1), f(u, "inv", 1), lam, None, ALU.mult)
                            chain(dve.tensor_scalar(e[:, 0, 0:w], e[:, 0, 0:w], f(u, "inv", 0), None, ALU.mult))
                            normed.by(dve.scalar_tensor_tensor(e[:, 0, 0:w], e[:, 1, 0:w], f(u, "den", 1), e[:, 0, 0:w],
                                                               ALU.mult, ALU.add))

            @block.scalar
            def _(act):
                for i in range(U + 4):
                    if i < U:
                        w = units[i][1]
                        act.wait_ge(ready.h, i + 1)
                        if i >= 4:
                            act.wait_ge(flipped.h, i - 3)
                        if sink is not None:
                            act.activation(f(i, "sink"), sink(i)[0], ACT.Exp, bias=f(i, "neg"))
                        for g in range(G):
                            ins = act.activation(ex[i % 4][:, g, 0:w], sm[i % 2][:, g, 0:w], ACT.Exp, bias=f(i, "neg", g), scale=-1.0,
                                                 accum_out=f(i, "sum", g))
                        exped.by(ins)
                    u = i - 3
                    if 0 <= u < U:
                        w = units[u][1]
                        act.wait_ge(flipped.h, u + 1)
                        if u >= 2:
                            act.wait_ge(weighed.h, u - 1)
                        ptaken.by(act.activation(pt[u % 2][:, 0:w], bank[4 + u % 2][:, 0:w], ACT.Copy))
                    u = i - 4
                    if 0 <= u < U:
                        r0, r1 = units[u][4]
                        act.wait_ge(weighed.h, u + 1)
                        otaken.by(act.activation(dst_of(u), bank[6 + u % 2][r0:r1, 0:P], ACT.Copy))

    def turn(pairs):
        flipped, taken = sig("flipped"), sig("taken")
        with ExitStack() as ctx:
            block = ctx.enter_context(stage())

            @block.tensor
            def _(pe):
                for n, (_, srcs) in enumerate(pairs):
                    if n >= 8:
                        pe.wait_ge(taken.h, n - 7)
                    for q, src in enumerate(srcs):
                        mm = pe.transpose(bank[n % 8][:, q * P:(q + 1) * P], src, ident)
                    mm.then_inc(flipped.h, 1)

            @block.vector
            def _(dve):
                for n, (dst, srcs) in enumerate(pairs):
                    dve.wait_ge(flipped.h, n + 1)
                    dve.tensor_copy(dst, bank[n % 8][:, 0:len(srcs) * P].rearrange("p (q c) -> p q c", q=len(srcs))).then_inc(taken.h, 1)

    def rwkv(r, k, v, zt, zg, oT, outer):
        with ExitStack() as ctx:
            cs, aa, ep, em, kk, tmp = (sb(ctx, n, [P, 4, S]) for n in ("cs", "aa", "ep", "em", "kk", "tmp"))
            level = sb(ctx, "level", [P, LEVELS, P])
            before, upto = zt[:, 0:P], zt[:, P:2 * P]
            pc = sb(ctx, "pc", [P, 4, NCH])
            with ExitStack() as c1:
                inside = sb(c1, "inside", [P, S])
                lora = sb(c1, "lora", [P, S])
                s_in, pre, sg1, sg2, scan, expd, sq, sm_, mxd, rtd, inverted, spread, pr, bsum = (
                    sig(n) for n in ("s_in", "pre", "sg1", "sg2", "scan", "expd", "sq", "summed", "bounded", "rooted", "inverted", "spread", "pr", "bsum"))
                st = sb(c1, "st", [P, 3, NT * NH])
                decayed = sig("decayed")

                def pool_part(pool):
                    pool.wait_ge(expd.h, 8)
                    pool.wait_ge(pr.h, 4)
                    pool.tensor_tensor(r[:, :, :], r[:, :, :], ep[:, :, :], ALU.mult).then_inc(decayed.h, 1)
                block = c1.enter_context(stage(pool_part))

                @block.sync
                def _(sp):
                    sp.dma_start(lora[0:HD, :], a["w_decay_up"][0]).then_inc(s_in.h, 16)
                    sp.dma_start(lora[HD:P, :], a["w_iclr_up"][0]).then_inc(s_in.h, 16)
                    cst_dma(sp, level[:, :, :].rearrange("p l n -> p (l n)"), "level", s_in)
                    cst_dma(sp, inside[:, :], "inside", s_in)

                @block.scalar
                def _(act):
                    act.activation(zt[0:HD, :], zt[0:HD, :], ACT.Tanh).then_inc(sg1.h, 1)
                    act.activation(zg[:, :], zg[:, :], ACT.Sigmoid)
                    for m in range(8):
                        act.wait_ge(pre.h, m + 1)
                        dst, b = (cs, "w0") if m < 4 else (aa, "a0")
                        act.activation(dst[:, m % 4, :], bank[m][:, :], ACT.Sigmoid, bias=col(b, m % 4)).then_inc(sg2.h, 1)
                    act.wait_ge(mxd.h, 1)
                    act.activation(st[:, 1, :], st[:, 0, :], ACT.Sqrt).then_inc(rtd.h, 1)
                    for m in range(4):
                        act.wait_ge(scan.h, m + 1)
                        act.activation(ep[:, m, :], tmp[:, m, :], ACT.Exp, scale=-EHALF).then_inc(expd.h, 1)
                        act.activation(em[:, m, :], tmp[:, m, :], ACT.Exp, scale=EHALF).then_inc(expd.h, 1)

                @block.tensor
                def _(pe):
                    pe.wait_ge(s_in.h, 16 * 4)
                    pe.wait_ge(sg1.h, 1)
                    for m in range(8):
                        lo_, hi_ = (0, HD) if m < 4 else (HD, P)
                        pe.matmul(bank[m][:, :], lora[lo_:hi_, (m % 4) * P:(m % 4 + 1) * P], zt[lo_:hi_, :],
                                  start=True, stop=True).then_inc(pre.h, 1)
                    for m in range(4):
                        pe.wait_ge(sq.h, m + 1)
                        pe.wait_ge(sg2.h, 4)
                        for t in range(NT):
                            mm = pe.matmul(bank[t][:, 2 * m:2 * m + 2], cs[:, m, t * P:(t + 1) * P], pair[:, 0:P:HD], start=True, stop=True)
                    mm.then_inc(sm_.h, 1)
                    pe.wait_ge(inverted.h, 1)
                    for m in range(4):
                        for t in range(NT):
                            for q in range(2):
                                x = t * NH + 2 * m + q
                                mm = pe.matmul(bank[m][q * HD:(q + 1) * HD, t * P:(t + 1) * P], st[:, 2, x:x + 1].broadcast_to([P, HD]), ident,
                                               start=True, stop=True)
                        mm.then_inc(spread.h, 1)
                    for m in range(4):
                        pe.wait_ge(pr.h, m + 1)
                        pe.wait_ge(sg2.h, 4 + m + 1)
                        pe.matmul(bank[4 + m][:, :], pair, cs[:, m, :], start=True, stop=True).then_inc(bsum.h, 1)

                @block.vector
                def _(dve):
                    chain = Chain(dve, dve_chain)
                    dve.wait_ge(s_in.h, 16 * 4)
                    for m in range(4):
                        chain(dve.tensor_scalar(kk[:, m, :], k[:, m, :], col("k_k", m), None, ALU.mult))
                    for m in range(4):
                        dve.wait_ge(sg2.h, m + 1)
                        scan.by(dve.tensor_tensor_scan(tmp[:, m, :], inside[:, :], cs[:, m, :], 0.0, ALU.mult, ALU.add))
                    dve.wait_ge(scan.h, 4)
                    for m in range(4):
                        sq.by(dve.tensor_tensor(cs[:, m, :], kk[:, m, :], kk[:, m, :], ALU.mult))
                    dve.wait_ge(sm_.h, 1)
                    mxd.by(dve.tensor_scalar(st[:, 0, :].rearrange("p (t h) -> p t h", t=NT), banks[:, 0:4, 0:NH], 1e-24, None, ALU.max))
                    dve.wait_ge(rtd.h, 1)
                    dve.reciprocal(st[:, 2, :], st[:, 1, :]).then_inc(inverted.h, 1)
                    for m in range(4):
                        dve.wait_ge(sg2.h, 4 + m + 1)
                        chain(dve.tensor_scalar(cs[:, m, :], aa[:, m, :], -1.0, col("k_a", m), ALU.add, ALU.mult))
                        chain(dve.scalar_tensor_tensor(k[:, m, :], cs[:, m, :], 1.0, k[:, m, :], ALU.add, ALU.mult))
                        pr.by(dve.scalar_tensor_tensor(cs[:, m, :], r[:, m, :], col("r_k", m), k[:, m, :], ALU.mult, ALU.mult))
                    for m in range(4):
                        dve.wait_ge(spread.h, m + 1)
                        chain(dve.scalar_tensor_tensor(kk[:, m, :], kk[:, m, :], -1.0, bank[m][:, :], ALU.mult, ALU.mult))
                    dve.wait_ge(expd.h, 8)
                    for m in range(4):
                        ins = dve.scalar_tensor_tensor(aa[:, m, :], aa[:, m, :], -1.0, kk[:, m, :], ALU.mult, ALU.mult)
                    chain(ins)
                    dve.tensor_tensor(k[:, :, :], k[:, :, :], em[:, :, :], ALU.mult)
                    chain(dve.tensor_tensor(aa[:, :, :], aa[:, :, :], em[:, :, :], ALU.mult))
                    for m in range(4):
                        kc = kk[:, m, :].rearrange("p (c t) -> p c t", t=C)
                        ec = ep[:, m, :].rearrange("p (c t) -> p c t", t=C)
                        chain(dve.tensor_tensor(kc[:, :, 1:C], kc[:, :, 1:C], ec[:, :, 0:C - 1], ALU.mult))
                        chain(dve.tensor_copy(pc[:, m, :], ec[:, :, C - 1]))
                    for m in range(4):
                        dve.wait_ge(bsum.h, m + 1)
                        chain(dve.tensor_tensor(cs[:, m, :], bank[4 + m][:, :], v[:, m, :], ALU.mult))
            vt, kt, bt, at_ = tmp, ep, em, v
            turn([(dst[:, t, :].rearrange("p (q c) -> p q c", q=4), [src[:, m, t * P:(t + 1) * P] for m in range(4)])
                  for dst, src in ((vt, v), (kt, k), (bt, aa), (at_, kk)) for t in range(NT)])
            wt = sb(ctx, "wt", [P, NT, 4, P])
            u0 = sb(ctx, "u0", [P, NT, 2, 4 * HD])
            z = sb(ctx, "z", [P, NCH, 4, HD])

            def uat(h):
                return slice(h % 2 * 4 * HD + h // 2 * HD, h % 2 * 4 * HD + h // 2 * HD + HD)

            def u_of(h, t, r0=0, r1=P):
                return u0[r0:r1, t, h % 2, h // 2 * HD:(h // 2 + 1) * HD]

            def head(x, h, t):
                return x[h % 2 * HD:h % 2 * HD + HD, h // 2, t * P:(t + 1) * P]

            with ExitStack() as c2:
                NG = 4
                T, Tt, pm = (sb(c2, n, [P, NG, 4, P]) for n in ("T", "Tt", "pm"))
                nt = oT.rearrange("p g (h n) -> p g h n", h=4)
                made, took, copied, got = sig("made"), sig("took"), sig("copied"), sig("got")
                block = c2.enter_context(stage())

                @block.sync
                def _(sp):
                    cst_dma(sp, before, "before", got)
                    cst_dma(sp, upto, "upto", got)

                i4 = ident.rearrange("p (o n) -> p o n", o=1).broadcast_to([P, 4, P])
                flat = lambda b: b.rearrange("p (h n) -> p h n", h=4)

                def m4(mask):
                    return mask.rearrange("p (o n) -> p o n", o=1).broadcast_to([P, 4, P])

                order = []
                for hf in range(2):
                    for kind in ("nt", "p0", "t0"):
                        order += [(kind, hf, g, 0) for g in range(NG)]
                    for l in range(1, LEVELS):
                        order += [("p", hf, g, l) for g in range(NG)]
                        order += [("tt", hf, g, l) for g in range(NG)]
                        if l < LEVELS - 1:
                            order += [("t", hf, g, l) for g in range(NG)]
                    order += [("ak", hf, g, 0) for g in range(NG)]
                    order += [("y", hf, x, 0) for x in range(2)]
                    order += [("u", hf, x, 0) for x in range(2)]
                    order += [("w", hf, x, 0) for x in range(2)]
                where = {x: n for n, x in enumerate(order)}

                BY_ACT = ("t", "y", "u", "w")
                nth = [sum((x[0] in BY_ACT) == (kind in BY_ACT) for x in order[:n]) for n, (kind, *_) in enumerate(order)]

                def wait_taken(eng, n):
                    eng.wait_ge((copied if order[n][0] in BY_ACT else took).h, nth[n] + 1)

                @block.tensor
                def _(pe):
                    for n, (kind, hf, g, l) in enumerate(order):
                        t = hf * 2 + g // 2
                        if n >= 8:
                            wait_taken(pe, n - 8)
                        if kind == "p0":
                            wait_taken(pe, where["nt", hf, g, 0])
                        elif kind == "t0":
                            wait_taken(pe, where["p0", hf, g, 0])
                        elif kind == "p":
                            wait_taken(pe, where["t0" if l == 1 else "t", hf, g, l - 1 if l > 1 else 0])
                        elif kind == "tt":
                            wait_taken(pe, where["p", hf, g, l])
                        elif kind == "t":
                            wait_taken(pe, where["tt", hf, g, l])
                        elif kind == "y":
                            wait_taken(pe, where["ak", hf, 2 * g + 1, 0])
                        elif kind in ("u", "w"):
                            wait_taken(pe, where["y", hf, g, 0])
                        acc = bank[n % 8]
                        if kind in ("y", "u", "w"):
                            t = hf * 2 + g
                            for h in range(NH):
                                gg, hh = 2 * g + h % 2, h // 2
                                if kind == "y":
                                    mm = pe.matmul(acc[:, h * HD:(h + 1) * HD], pm[:, gg, hh, :], vt[:, t, h * HD:(h + 1) * HD],
                                                   start=True, stop=True)
                                elif kind == "u":
                                    mm = pe.matmul(acc[:, uat(h)], Tt[:, gg, hh, :], nt[:, g, :, :].rearrange("p a b -> p (a b)")[:, h * HD:(h + 1) * HD],
                                                   start=True, stop=True)
                                else:
                                    mm = pe.matmul(acc[h % 2 * HD:h % 2 * HD + HD, h // 2 * P:(h // 2 + 1) * P],
                                                   at_[:, t, h * HD:(h + 1) * HD], Tt[:, gg, hh, :], start=True, stop=True)
                        else:
                            for hh in range(4):
                                h = 2 * hh + g % 2
                                o = acc[:, hh * P:(hh + 1) * P]
                                if kind == "nt":
                                    mm = pe.matmul(o, head(aa, h, t), head(kk, h, t), start=True, stop=True)
                                elif kind == "p0":
                                    mm = pe.transpose(o, nt[:, g, hh, :], ident)
                                elif kind == "ak":
                                    mm = pe.matmul(o, head(k, h, t), head(kk, h, t), start=True, stop=True)
                                elif kind == "t0":
                                    mm = pe.transpose(o, pm[:, g, hh, :], ident)
                                elif kind == "p":
                                    mm = pe.matmul(o, nt[:, g, hh, :], T[:, g, hh, :], start=True, stop=True)
                                elif kind == "tt":
                                    mm = pe.matmul(o, pm[:, g, hh, :], Tt[:, g, hh, :], start=True, stop=True)
                                else:
                                    mm = pe.transpose(o, Tt[:, g, hh, :], ident)
                        mm.then_inc(made.h, 1)

                @block.vector
                def _(dve):
                    chain = Chain(dve, dve_chain)
                    dve.wait_ge(got.h, 32)
                    for n, (kind, hf, g, l) in enumerate(order):
                        if kind in BY_ACT:
                            continue
                        dve.wait_ge(made.h, n + 1)
                        acc = flat(bank[n % 8][:, :])
                        if kind == "nt":
                            ins = dve.tensor_tensor(nt[:, g, :, :], acc, m4(before), ALU.mult)
                        elif kind == "p0":
                            chain(dve.tensor_tensor(pm[:, g, :, :], acc, m4(level[:, 0, :]), ALU.mult))
                            ins = dve.tensor_tensor(T[:, g, :, :], pm[:, g, :, :], i4, ALU.add)
                        elif kind == "t0":
                            ins = dve.tensor_tensor(Tt[:, g, :, :], acc, i4, ALU.add)
                        elif kind == "p":
                            ins = dve.tensor_tensor(pm[:, g, :, :], acc, m4(level[:, l, :]), ALU.mult)
                        elif kind == "tt":
                            ins = dve.tensor_tensor(Tt[:, g, :, :], acc, Tt[:, g, :, :], ALU.add)
                        else:
                            ins = dve.tensor_tensor(pm[:, g, :, :], acc, m4(before), ALU.mult)
                        ins.then_inc(took.h, 1)

                @block.scalar
                def _(act):
                    for n, (kind, hf, g, l) in enumerate(order):
                        if kind not in BY_ACT:
                            continue
                        act.wait_ge(made.h, n + 1)
                        to, i = {"t": (T, g), "y": (nt, g), "u": (u0, hf * 2 + g), "w": (wt, hf * 2 + g)}[kind]
                        dst = to[:, i, :, :]
                        act.activation(dst.rearrange("p a b -> p (a b)"), bank[n % 8][:, :], ACT.Copy).then_inc(copied.h, 1)
            with ExitStack() as c3:
                zn = sb(c3, "zn", [P, 4, HD])
                rb = [sb(c3, f"rb{i}", [P, 4, P]) for i in range(4)]
                read, u_done, kv_, z_done, made, took, summed, otk = (
                    sig(n) for n in ("read", "u_done", "kv", "z_done", "made", "took", "summed", "otk"))
                block = c3.enter_context(stage())
                groups = [(t, q) for t in range(NT) for q in range(2)]

                def rng(c):
                    return c * C // P, c * C % P, c * C % P + C

                @block.tensor
                def _(pe):
                    def products(n, x, src):
                        t, q = groups[n]
                        m = 2 * n + x
                        if m >= 3:
                            pe.wait_ge(took.h, m - 2)
                        for hh in range(4):
                            h = 2 * hh + q
                            mm = pe.matmul(bank[3 + m % 3][:, hh * P:(hh + 1) * P], head(src, h, t), head(r, h, t), start=True, stop=True)
                        mm.then_inc(made.h, 1)

                    def outputs(n):
                        t, q = groups[n]
                        pe.wait_ge(took.h, 2 * n + 2)
                        pe.wait_ge(u_done.h, 2 * t + 2)
                        if n >= 2:
                            pe.wait_ge(otk.h, n - 1)
                        p0 = q * HD
                        b = bank[6 + q]
                        for hh in range(4):
                            h = 2 * hh + q
                            lo_ = hh * P
                            pe.matmul(b[p0:p0 + HD, lo_:lo_ + P], vt[:, t, h * HD:(h + 1) * HD], rb[n % 2 * 2 + 1][:, hh, :], start=True, stop=False, skip_group_check=True)
                            pe.matmul(b[p0:p0 + HD, lo_:lo_ + P], u_of(h, t), rb[n % 2 * 2][:, hh, :], start=False, stop=False, skip_group_check=True)
                            for c in range(t * P // C, (t + 1) * P // C):
                                o0 = c * C - t * P
                                mm = pe.matmul(b[p0:p0 + HD, lo_ + o0:lo_ + o0 + C], z[p0:p0 + HD, c, h // 2, :],
                                               r[p0:p0 + HD, h // 2, c * C:(c + 1) * C], start=False, stop=c == (t + 1) * P // C - 1, skip_group_check=True)
                        mm.then_inc(summed.h, 1)

                    for c in range(NCH + 2):
                        if c < NCH:
                            t, r0, r1 = rng(c)
                            pe.wait_ge(z_done.h, c + 1)
                            for h in range(NH):
                                p0 = h % 2 * HD
                                mm = pe.matmul(bank[h % 2][:, h // 2 * HD:(h // 2 + 1) * HD], wt[p0:p0 + HD, t, h // 2, :],
                                               z[p0:p0 + HD, c, h // 2, :], start=True, stop=True)
                            mm.then_inc(read.h, 1)
                            products(c, 0, aa)
                        if c < NCH - 1:
                            pe.wait_ge(u_done.h, c + 1)
                            for h in range(NH):
                                p0 = h % 2 * HD
                                o = bank[2][p0:p0 + HD, h // 2 * HD:(h // 2 + 1) * HD]
                                pe.matmul(o, kt[r0:r1, t, h * HD:(h + 1) * HD], vt[r0:r1, t, h * HD:(h + 1) * HD], start=True, stop=False)
                                mm = pe.matmul(o, bt[r0:r1, t, h * HD:(h + 1) * HD], u_of(h, t, r0, r1), start=False, stop=True)
                            mm.then_inc(kv_.h, 1)
                        if c < NCH:
                            products(c, 1, k)
                        if c >= 2:
                            outputs(c - 2)

                @block.vector
                def _(dve):
                    chain = Chain(dve, dve_chain)
                    dve.memset(z[:, 0, :, :], 0.0).then_inc(z_done.h, 1)
                    for c in range(NCH):
                        t, r0, r1 = rng(c)
                        dve.wait_ge(read.h, c + 1)
                        dve.tensor_tensor(u0[r0:r1, t, :, :], banks[r0:r1, 0:2, 0:4 * HD], u0[r0:r1, t, :, :], ALU.add).then_inc(u_done.h, 1)
                        if c < NCH - 1:
                            dve.wait_ge(kv_.h, c + 1)
                            chain(dve.tensor_tensor(zn[:, :, :], bank[2][:, 0:4 * HD].rearrange("p (a b) -> p a b", a=4),
                                                    z[:, c, :, :], ALU.add))
                            dve.tensor_tensor(z[:, c + 1, :, :], zn[:, :, :],
                                              pc[:, :, c:c + 1].broadcast_to([P, 4, HD]), ALU.mult).then_inc(z_done.h, 1)
                        if c >= 2:
                            dve.wait_ge(summed.h, c - 1)
                        for x in range(2):
                            m = 2 * c + x
                            dve.wait_ge(made.h, m + 1)
                            dve.tensor_tensor(rb[c % 2 * 2 + x][:, :, :], bank[3 + m % 3][:, :].rearrange("p (h n) -> p h n", h=4),
                                              upto.rearrange("p (o n) -> p o n", o=1).broadcast_to([P, 4, P]), ALU.mult).then_inc(took.h, 1)

                @block.scalar
                def _(act):
                    for n in range(len(groups)):
                        t, q = groups[n]
                        act.wait_ge(summed.h, n + 1)
                        act.activation(oT[q * HD:q * HD + HD, :, t * P:(t + 1) * P], bank[6 + q][q * HD:q * HD + HD, :].rearrange("p (a b) -> p a b", a=4),
                                       ACT.Copy).then_inc(otk.h, 1)
            with ExitStack() as c5:
                gm, gd, g1, g2, g3, g4, rooted, inverted, spread, got = (
                    sig(n) for n in ("mean", "centred", "squared", "summed", "meaned", "gate", "rooted", "inverted", "spread", "got"))
                st = sb(c5, "st", [P, 3, NT * NH])
                wgu = u0[:, 0, :, :].rearrange("p a b -> p (a b)")
                dd, sqd = kk, aa
                block = c5.enter_context(stage())

                @block.sync
                def _(sp):
                    sp.dma_start(wgu, a["w_gate_up"][0]).then_inc(got.h, 16)

                @block.tensor
                def _(pe):
                    for m in range(4):
                        pe.matmul(bank[m][:, :], pair, oT[:, m, :], start=True, stop=True).then_inc(gm.h, 1)
                    for m in range(4):
                        pe.wait_ge(g1.h, m + 1)
                        for t in range(NT):
                            mm = pe.matmul(bank[4 + t][:, 2 * m:2 * m + 2], sqd[:, m, t * P:(t + 1) * P], pair[:, 0:P:HD], start=True, stop=True)
                    mm.then_inc(g2.h, 1)
                    pe.wait_ge(got.h, 16)
                    for m in range(4):
                        pe.matmul(bank[m][:, :], wgu[:, m * P:(m + 1) * P], zg[:, :], start=True, stop=True).then_inc(g4.h, 1)
                    pe.wait_ge(inverted.h, 1)
                    for m in range(4):
                        for t in range(NT):
                            for q in range(2):
                                x = t * NH + 2 * m + q
                                mm = pe.matmul(bank[4 + m][q * HD:(q + 1) * HD, t * P:(t + 1) * P], st[:, 2, x:x + 1].broadcast_to([P, HD]), ident,
                                               start=True, stop=True)
                        mm.then_inc(spread.h, 1)

                @block.scalar
                def _(act):
                    for m in range(4):
                        act.wait_ge(gd.h, m + 1)
                        act.activation(sqd[:, m, :], dd[:, m, :], ACT.Square).then_inc(g1.h, 1)
                    act.wait_ge(g3.h, 1)
                    act.activation(st[:, 1, :], st[:, 0, :], ACT.Sqrt).then_inc(rooted.h, 1)

                @block.vector
                def _(dve):
                    chain = Chain(dve, dve_chain)
                    for m in range(4):
                        dve.wait_ge(gm.h, m + 1)
                        dve.scalar_tensor_tensor(dd[:, m, :], bank[m][:, :], -1.0 / HD, oT[:, m, :], ALU.mult, ALU.add).then_inc(gd.h, 1)
                    dve.wait_ge(g2.h, 1)
                    dve.tensor_scalar(st[:, 0, :].rearrange("p (t h) -> p t h", t=NT), banks[:, 4:8, 0:NH], 1.0 / HD, GN_EPS, ALU.mult, ALU.add)\
                       .then_inc(g3.h, 1)
                    dve.wait_ge(rooted.h, 1)
                    dve.reciprocal(st[:, 2, :], st[:, 1, :]).then_inc(inverted.h, 1)
                    for m in range(4):
                        dve.wait_ge(spread.h, m + 1)
                        chain(dve.scalar_tensor_tensor(dd[:, m, :], dd[:, m, :], col("ln_g", m), bank[4 + m][:, :], ALU.mult, ALU.mult))
                        chain(dve.scalar_tensor_tensor(dd[:, m, :], dd[:, m, :], col("ln_b", m), cs[:, m, :], ALU.add, ALU.add))
                        dve.wait_ge(g4.h, m + 1)
                        chain(dve.tensor_tensor(oT[:, m, :], dd[:, m, :], bank[m][:, :], ALU.mult))

    class LocalSide(Side):
        VALUES = 6

        def __init__(self, ctx, bias, sinks, nsinks, vT, vt):
            self.bias, self.sinks, self.nsinks, self.vT, self.vt = bias, sinks, nsinks, vT, vt
            self.table, self.hot, self.row = sb(ctx, "table", [BUCKETS + 1, NH]), sb(ctx, "hot", [BUCKETS + 1, RLEN]), sb(ctx, "row", [NH, RLEN])
            self.got, self.made, self.copied, self.stored, self.turned = (sig(n) for n in ("got", "made", "copied", "stored", "turned"))

        def sp(self, sp):
            sp.dma_start(self.table[0:BUCKETS, :], a["rel_bias"]).then_inc(self.got.h, 16)
            lo_ = CST["ones"][0]
            sp.dma_start(self.table[BUCKETS:BUCKETS + 1, :], a["cst"][0:1, lo_:lo_ + NH]).then_inc(self.got.h, 16)
            cst_dma(sp, self.hot[:, :], "onehot", self.got, BUCKETS + 1)
            sp.dma_start(self.sinks[:, :], a["sinks"][0:1, :].broadcast_to([P, NH])).then_inc(self.got.h, 16)

        def pe(self, pe, free, m):
            if m == 0:
                pe.wait_ge(self.got.h, 64)
                pe.matmul(bank[4][0:NH, 0:RLEN], self.table[:, :], self.hot[:, :], start=True, stop=True).then_inc(self.made.h, 1)
            if m == self.VALUES:
                pe.wait_ge(free.h, m + 1)
                for t in range(NT):
                    mm = pe.transpose(bank[5][:, t * P:(t + 1) * P], self.vT[:, t * P:(t + 1) * P], ident)
                mm.then_inc(self.turned.h, 1)

        def dve(self, dve, chain, free):
            dve.wait_ge(self.made.h, 1)
            dve.tensor_scalar(self.row[:, :], bank[4][0:NH, 0:RLEN], HD ** 0.5, None, ALU.mult).then_inc(self.copied.h, 1)
            dve.wait_ge(self.got.h, 64)
            dve.tensor_scalar(self.nsinks[:, :], self.sinks[:, :], -1.0, None, ALU.mult)

        def act(self, act, m):
            if m == 2:
                act.wait_ge(self.copied.h, 1)
                act.dma_start(scratch[:, :, :], self.row[:, :].rearrange("h (o x) -> h o x", o=1).broadcast_to([NH, P, RLEN])).then_inc(self.stored.h, 16)
            if m == self.VALUES + 1:
                act.wait_ge(self.stored.h, 16)
                flat = scratch[:, :, :].rearrange("h q x -> h (q x)")
                act.dma_start(self.bias[:, :, :], flat[:, P - 1:P - 1 + P * (RLEN - 1)].rearrange("h (q x) -> q h x", x=RLEN - 1)[:, :, 0:2 * P])\
                   .then_inc(self.stored.h, 16)
            if m == self.VALUES + 2:
                act.wait_ge(self.turned.h, 1)
                act.activation(self.vt[:, 0, :, :].rearrange("p t n -> p (t n)"), bank[5][:, :], ACT.Copy)
            if m == self.VALUES + 6:
                act.wait_ge(self.stored.h, 32)

    def local_attention(qT, kd, vt, bias, sinks, nsinks, oT):
        units, dst = [], []
        for h in range(NH):
            p0, g = h % 2 * HD, h // 4
            for n in range(NT):
                lo_ = max(n - 1, 0) * P
                hi_ = (n + 1) * P
                w = hi_ - lo_
                units.append(([[(qT[p0:p0 + HD, h // 2, n * P:hi_], kd[p0:p0 + HD, g, lo_:hi_], 0)]], w,
                              bias[:, h, 2 * P - w:2 * P],
                              [vt[:, 0, b, g * HD:(g + 1) * HD] for b in range(lo_ // P, n + 1)], (p0, p0 + HD)))
                dst.append(oT[p0:p0 + HD, h // 2, n * P:hi_])
        attend(units, lambda u: dst[u], sink=lambda i: (sinks[:, i // NT:i // NT + 1], nsinks[:, i // NT:i // NT + 1]))

    def add_normed(src, name):
        with ExitStack() as ctx:
            y = sb(ctx, "y", [P, 2, S])
            scaled, added = sig("scaled"), sig("added")

            def finish(dve, chain, k, rstd):
                if k >= 2:
                    dve.wait_ge(added.h, k - 1)
                scaled.by(dve.scalar_tensor_tensor(y[:, k % 2, :], src[:, k, :], col(name, k), rstd, ALU.mult, ALU.mult))
                for j in ([k - 1] if k else []) + ([k] if k == KD - 1 else []):
                    dve.wait_ge(scaled.h, j + 1)
                    if j == k:
                        chain(dve.tensor_tensor(xT[:, j, :], y[:, j % 2, :], xT[:, j, :], ALU.add))
                    else:
                        added.by(dve.tensor_tensor(xT[:, j, :], y[:, j % 2, :], xT[:, j, :], ALU.add))
            norm(lambda k: src[:, k, :], KD, D, EPS, finish)

    class EvenSide(Side):
        PICKS, TURNS_A, TURNS_B = 3, 7, 17

        def __init__(self, ctx, af, av, bv, rotated, vta, vtb, forget, mask, lam, lam_init, cosT, sinT):
            self.af, self.av, self.bv, self.rotated, self.vta, self.vtb = af, av, bv, rotated, vta, vtb
            self.forget, self.mask, self.lam, self.lam_init = forget, mask, lam, lam_init
            self.rot = Rotate(ctx, cosT, sinT)
            self.fb = sb(ctx, "fb", [NH, 1])
            self.ls, self.pr, self.sm = sb(ctx, "ls", [P, 4, HD]), sb(ctx, "pr", [P, 2, HD]), sb(ctx, "sm", [P, 2])
            flat = vtb.rearrange("p t m n -> p (t m n)")
            self.y, self.w = flat[0:NH, 0:S], flat[0:NH, S:2 * S]
            self.pick = flat[0:NH, 2 * S:2 * S + NH * P].rearrange("p (h n) -> p h n", h=NH)
            self.got, self.made, self.did, self.summed, self.exped, self.filled, self.emptied = (
                sig(n) for n in ("got", "made", "did", "summed", "exped", "filled", "emptied"))

        def sp(self, sp):
            sp.dma_start(self.fb[:, :], a["ev_fgate_b_2"].rearrange("o h -> h o")).then_inc(self.got.h, 16)
            for i, n in enumerate(("q1", "q2", "k1", "k2")):
                sp.dma_start(self.ls[:, i, :], a[f"ev_lambda_{n}_2"][0:1, :].broadcast_to([P, HD])).then_inc(self.got.h, 16)
            cst_dma(sp, self.mask[:, S - P:S], "future", self.got)
            self.rot.sp(sp)

        def act(self, act, m):
            if m == 0:
                chain = Chain(act, act_chain)
                act.wait_ge(self.summed.h, 1)
                act.activation(self.sm[:, :], self.sm[:, :], ACT.Exp).then_inc(self.exped.h, 1)
                act.wait_ge(self.made.h, 1)
                chain(act.activation(self.y, self.af[0:NH, :], ACT.Abs))
                chain(act.activation(self.y, self.y, ACT.Exp, scale=-1.0))
                act.activation(self.y, self.y, ACT.Ln, bias=1.0).then_inc(self.did.h, 1)

        def pe(self, pe, free, m):
            def turn_(dst_bank, srcs):
                for q, src in enumerate(srcs):
                    mm = pe.transpose(dst_bank[:, q * P:(q + 1) * P], src, ident)
                mm.then_inc(self.filled.h, 1)
            if self.PICKS <= m < self.TURNS_A:
                pe.wait_ge(self.made.h, 2)
                for h in (2 * (m - self.PICKS), 2 * (m - self.PICKS) + 1):
                    if h >= 4:
                        pe.wait_ge(self.emptied.h, h - 3)
                    pe.matmul(bank[4 + h % 4][:, :], self.pick[:, h, :], self.w, start=True, stop=True).then_inc(self.filled.h, 1)
            if self.TURNS_A <= m < self.TURNS_A + NT:
                t = m - self.TURNS_A
                pe.wait_ge(free.h, 5)
                pe.wait_ge(self.emptied.h, NH + t - 3)
                turn_(bank[4 + t], [self.av[:, q, t * P:(t + 1) * P] for q in range(4)])
            if self.TURNS_B <= m < self.TURNS_B + NT:
                t = m - self.TURNS_B
                pe.wait_ge(free.h, 17)
                pe.wait_ge(self.emptied.h, NH + NT + t)
                turn_(bank[7], [self.bv[:, q, t * P:(t + 1) * P] for q in range(4)])
            if m in self.rotated:
                pe.wait_ge(free.h, m + 1)
                self.rot.pe(pe, self.rotated[m])

        def dve(self, dve, chain, free):
            dve.memset(self.mask[:, 0:S - P], 0.0)
            chain(dve.tensor_copy(self.pick, ident[0:NH, 0:NH].rearrange("p (h o) -> p h o", o=1).broadcast_to([NH, NH, P])))
            dve.wait_ge(self.got.h, 96)
            chain(dve.tensor_tensor(self.pr[:, :, :], self.ls[:, 0:2, :], self.ls[:, 2:4, :], ALU.mult))
            dve.tensor_reduce(self.sm[:, :], self.pr[:, :, :], AX.X, ALU.add).then_inc(self.summed.h, 1)
            dve.wait_ge(free.h, 1)
            dve.tensor_scalar(self.af[0:NH, :], self.af[0:NH, :], self.fb[:, 0:1], None, ALU.add).then_inc(self.made.h, 1)
            dve.wait_ge(self.exped.h, 1)
            chain(dve.tensor_scalar(self.lam, self.sm[:, 1:2], self.sm[:, 0:1], self.lam_init, ALU.subtract, ALU.subtract))
            dve.wait_ge(self.did.h, 1)
            chain(dve.tensor_scalar(self.w, self.af[0:NH, :], 0.0, None, ALU.min))
            chain(dve.tensor_tensor(self.y, self.y, self.w, ALU.subtract))
            dve.tensor_tensor_scan(self.w, self.y, self.y, 0.0, ALU.add, ALU.max).then_inc(self.made.h, 1)
            for h in range(NH):
                dve.wait_ge(self.filled.h, h + 1)
                dve.tensor_scalar(self.forget[:, h, :], bank[4 + h % 4][:, :], HD ** 0.5, None, ALU.mult).then_inc(self.emptied.h, 1)

            def take(n, dst, b):
                dve.wait_ge(self.filled.h, n + 1)
                dve.tensor_copy(dst.rearrange("p m n -> p (m n)"), bank[b][:, :]).then_inc(self.emptied.h, 1)
            for t in range(NT):
                take(NH + t, self.vta[:, t, :, :], 4 + t)
            for m, x in self.rotated.items():
                t = m - self.TURNS_B
                if t < NT:
                    take(NH + NT + t, self.vtb[:, t, :, :], 7)
                self.rot.dve(dve, x)

    def even_mixer(cosT, sinT, oT):
        lam_init = 0.8 - 0.6 * math.exp(-0.3 * 0)
        with ExitStack() as ctx:
            bq, bk, bv = (sb(ctx, n, [P, 4, S]) for n in ("bq", "bk", "bv"))
            vtb = sb(ctx, "vtb", [P, NT, 4, P])
            mask = sb(ctx, "mask", [P, S])
            lam = sb(ctx, "lam", [P, 1])
            with ExitStack() as fx:
                aq, ak, av = (sb(fx, n, [P, 4, S]) for n in ("aq", "ak", "av"))
                vta = sb(fx, "vta", [P, NT, 4, P])
                forget = sb(fx, "forget", [P, NH, S])
                with ExitStack() as pr:
                    hi, lo = sb(pr, "hi", [P, KD, S], F32R), sb(pr, "lo", [P, KD, S], F32R)
                    af = sb(pr, "af", [P, S])
                    dsts = [af[:, :]] + [t[:, m, :] for t in (av, aq, ak, bv, bq, bk) for m in range(4)]
                    project(25, hi, lo, lambda act, m, acc: act.activation(dsts[m], acc, ACT.Copy),
                            lead=Lead(pr, lambda k: col("attn_norm", k), hi, lo, dsts[17:22]),
                            side=EvenSide(pr, af, av, bv, {m: dsts[m] for m in range(17, 25)}, vta, vtb[:, :, :, :], forget, mask,
                                          lam[:, :], lam_init, cosT, sinT))
                units, dst = [], []
                for h in range(NH):
                    p0 = h % 2 * HD
                    for n in range(NT):
                        w = (n + 1) * P
                        units.append(([[(aq[p0:p0 + HD, h // 2, n * P:w], ak[p0:p0 + HD, h // 2, 0:w], 0),
                                        (ident, mask[:, S - P:S], w - P)]], w, forget[:, h, 0:w],
                                      [vta[:, b, h // 2, p0:p0 + HD] for b in range(n + 1)], (p0, p0 + HD)))
                        dst.append(oT[p0:p0 + HD, h // 2, n * P:w])
                attend(units, lambda u: dst[u])
            ob = sb(ctx, "ob", [P, 4, S])
            units, dst = [], []
            for h in range(4):
                for n in range(NT):
                    w = (n + 1) * P
                    units.append(([[(bq[p0:p0 + HD, h, n * P:w], bk[p0:p0 + HD, h, 0:w], 0)] for p0 in (0, HD)], w,
                                  mask[:, S - w:S], [vtb[:, b, h, :] for b in range(n + 1)], (0, P)))
                    dst.append(ob[:, h, n * P:w])
            attend(units, lambda u: dst[u], lam=lam[:, 0:1])

            def finish(dve, chain, k, rstd):
                chain(dve.scalar_tensor_tensor(bq[:, k, :], ob[:, k, :], col("subln"), rstd, ALU.mult, ALU.mult))
                chain(dve.tensor_scalar(oT[:, 4 + k, :], bq[:, k, :], 1.0 - lam_init, None, ALU.mult))
            norm(lambda k: ob[:, k, :], 4, 2 * HD, EPS, finish, groups=4)

    class RotateTiles(Side):

        def __init__(self, ctx, tiles_, cosT, sinT):
            self.tiles, self.rot = tiles_, Rotate(ctx, cosT, sinT)

        def sp(self, sp):
            self.rot.sp(sp)

        def pe(self, pe, free, m):
            if m in self.tiles:
                pe.wait_ge(free.h, m + 1)
                self.rot.pe(pe, self.tiles[m])

        def dve(self, dve, chain, free):
            for m in self.tiles:
                self.rot.dve(dve, self.tiles[m])

    class Indexer(Side):
        ROUNDS = TOPK // 8

        def __init__(self, ctx, iq, ik, ciw, keep, masks, ukp, wuv, rotated, kr_at, ckv, ckv_at, cosT, sinT):
            self.iq, self.ik, self.ciw, self.keep, self.masks, self.ukp, self.wuv = iq, ik, ciw, keep, masks, ukp, wuv
            self.future = masks[0][0]
            self.rotated, self.kr_at, self.ckv, self.ckv_at = rotated, kr_at, ckv, ckv_at
            self.rot = Rotate(ctx, cosT, sinT)
            self.score, self.work = (sb(ctx, n, [P, NT - 1, S]) for n in ("score", "work"))
            self.part = sb(ctx, "part", [P, 3, S])
            self.top, self.cnt = sb(ctx, "top", [P, NT - 1, 8]), sb(ctx, "cnt", [P, NT - 1])
            self.iwt = sb(ctx, "iwt", [P, NT, 4])
            self.sq = sb(ctx, "sq", [P, S])
            (self.got, self.turned, self.logit, self.clipped, self.added, self.found, self.struck, self.squared, self.summed,
             self.meaned, self.rooted) = (sig(n) for n in ("got", "turned", "logit", "clipped", "added", "found", "struck",
                                                           "squared", "summed", "meaned", "rooted"))
            self.order = [(n, h) for n in range(1, NT) for h in range(4)]

        def sp(self, sp):
            self.rot.sp(sp)
            for dst, name in self.masks:
                cst_dma(sp, dst, name, self.got)
            sp.dma_start(self.ukp[:, :, ROT:HD], a["od_w_uk_2"][0]).then_inc(self.got.h, 16)
            sp.dma_start(self.wuv[:, :, :], a["od_w_uv_2"][0]).then_inc(self.got.h, 16)

        def first_pe(self, pe):
            for t in range(NT):
                mm = pe.transpose(bank[7][:, t * P:(t + 1) * P], self.ciw[:, t * P:(t + 1) * P], ident)
            mm.then_inc(self.turned.h, 1)
            for x, (n, h) in enumerate(self.order):
                if x >= 3:
                    pe.wait_ge(self.clipped.h, x - 2)
                p0 = h % 2 * HD
                pe.matmul(bank[4 + x % 3][:, 0:(n + 1) * P], self.iq[p0:p0 + HD, h // 2, n * P:(n + 1) * P], self.ik[p0:p0 + HD, 0:(n + 1) * P],
                          start=True, stop=True).then_inc(self.logit.h, 1)

        def first_act(self, act):
            for x, (n, h) in enumerate(self.order):
                act.wait_ge(self.logit.h, x + 1)
                if x >= 3:
                    act.wait_ge(self.added.h, x - 2)
                act.activation(self.part[:, x % 3, 0:(n + 1) * P], bank[4 + x % 3][:, 0:(n + 1) * P], ACT.Relu).then_inc(self.clipped.h, 1)

        def pe(self, pe, free, m):
            if m == 1:
                pe.wait_ge(self.clipped.h, len(self.order))
            if m in self.rotated:
                pe.wait_ge(free.h, m + 1)
                self.rot.pe(pe, self.rotated[m])
            if m == self.ckv_at + 1:
                pe.wait_ge(self.squared.h, 1)
                pe.matmul(bank[7][:, :], ones, self.sq[:, :], start=True, stop=True).then_inc(self.summed.h, 1)

        def act(self, act, m):
            if m == self.ckv_at:
                act.activation(self.sq[:, :], bank[m % 4][:, :], ACT.Square).then_inc(self.squared.h, 1)
            if m == 14:
                act.wait_ge(self.meaned.h, 1)
                act.activation(self.sq[:, :], self.part[:, 0, :], ACT.Sqrt).then_inc(self.rooted.h, 1)

        def dve(self, dve, chain, free):
            dve.memset(self.ukp[:, :, 0:ROT], 0.0)
            dve.wait_ge(self.turned.h, 1)
            chain(dve.tensor_scalar(self.iwt[:, :, :], bank[7][:, :].rearrange("p (t n) -> p t n", t=NT)[:, :, 0:4], 0.5, None, ALU.mult))
            tiles_ = [(n, slice(0, (n + 1) * P)) for n in range(1, NT)]
            for x, (n, h) in enumerate(self.order):
                w = (n + 1) * P
                sc, part = self.score[:, n - 1, 0:w], self.part[:, x % 3, 0:w]
                dve.wait_ge(self.clipped.h, x + 1)
                if h == 0:
                    self.added.by(dve.tensor_scalar(sc, part, self.iwt[:, n, h:h + 1], None, ALU.mult))
                else:
                    dve.wait_ge(self.added.h, x)
                    self.added.by(dve.scalar_tensor_tensor(sc, part, self.iwt[:, n, h:h + 1], sc, ALU.mult, ALU.add))
            dve.wait_ge(self.got.h, 80)
            dve.wait_ge(self.added.h, len(self.order))
            for n, _ in tiles_:
                x = self.score[:, n - 1, n * P:(n + 1) * P]
                ins = dve.tensor_tensor(x, x, self.future, ALU.add)
            chain(ins)
            rotations = {3: 0, 5: 1, 7: 2, 9: 3, 10: self.kr_at}
            for i in range(self.ROUNDS):
                for n, w in tiles_:
                    if i:
                        dve.wait_ge(self.struck.h, 3 * (i - 1) + n)
                    dve.max(self.top[:, n - 1, :], (self.work if i else self.score)[:, n - 1, w]).then_inc(self.found.h, 1)
                for n, w in tiles_ if i < self.ROUNDS - 1 else []:
                    dve.wait_ge(self.found.h, 3 * i + n)
                    dve.match_replace(self.work[:, n - 1, w], self.top[:, n - 1, :], (self.work if i else self.score)[:, n - 1, w], -3e38)\
                       .then_inc(self.struck.h, 1)
                if i in rotations:
                    self.rot.dve(dve, self.rotated[rotations[i]])
                if i == self.ROUNDS - 5:
                    dve.wait_ge(self.summed.h, 1)
                    dve.tensor_scalar(self.part[:, 0, :], bank[7][:, :], 1.0 / P, EPS, ALU.mult, ALU.add).then_inc(self.meaned.h, 1)
            dve.wait_ge(self.found.h, 3 * self.ROUNDS)

            def each(op):
                for n, w in tiles_:
                    ins = op(self.score[:, n - 1, w], self.work[:, n - 1, w], self.keep[:, n - 1, w], self.top[:, n - 1, 7:8],
                             self.cnt[:, n - 1:n])
                chain(ins)
            each(lambda sc, wk, kp, thr, cnt: dve.tensor_scalar(kp, sc, thr, None, ALU.is_gt))
            each(lambda sc, wk, kp, thr, cnt: dve.tensor_reduce(cnt, kp, AX.X, ALU.add))
            each(lambda sc, wk, kp, thr, cnt: dve.tensor_scalar(cnt, cnt, -1.0, float(TOPK), ALU.mult, ALU.add))
            each(lambda sc, wk, kp, thr, cnt: dve.tensor_scalar(sc, sc, thr, None, ALU.is_equal))
            each(lambda sc, wk, kp, thr, cnt: dve.tensor_tensor_scan(wk, sc, sc, 0.0, ALU.add, ALU.max))
            each(lambda sc, wk, kp, thr, cnt: dve.scalar_tensor_tensor(wk, wk, cnt, sc, ALU.is_le, ALU.mult))
            each(lambda sc, wk, kp, thr, cnt: dve.tensor_tensor(kp, kp, wk, ALU.add))
            each(lambda sc, wk, kp, thr, cnt: dve.tensor_scalar(kp, kp, -1.0, 1e30, ALU.add, ALU.mult))
            dve.wait_ge(self.rooted.h, 1)
            chain(dve.reciprocal(self.part[:, 1, :], self.sq[:, :]))
            chain(dve.scalar_tensor_tensor(self.ckv, self.ckv, col("kv_norm"), self.part[:, 1, :], ALU.mult, ALU.mult))

    def odd_mixer(cosT, sinT, oT):
        with ExitStack() as ctx:
            sq_, sk_, sv_ = (sb(ctx, n, [P, 4, S]) for n in ("sq", "sk", "sv"))
            past, after = sb(ctx, "past", [P, P]), sb(ctx, "after", [P, P])
            with ExitStack() as ds:
                cq = sb(ds, "cq", [P, 4, S])
                ckv, kr = sb(ds, "ckv", [P, 1, S]), sb(ds, "kr", [P, 1, S])
                ukp = sb(ds, "ukp", [P, NH, HD])
                wuv = sb(ds, "wuv", [P, NH, HD])
                future = sb(ds, "future", [P, P])
                keep = sb(ds, "keep", [P, NT - 1, S])
                with ExitStack() as pr:
                    hi, lo = sb(pr, "hi", [P, KD, S], F32R), sb(pr, "lo", [P, KD, S], F32R)
                    iq, ik, ciw = sb(pr, "iq", [P, 2, S]), sb(pr, "ik", [P, S]), sb(pr, "ciw", [P, S])
                    with ExitStack() as c1:
                        to = [iq[:, 0, :], iq[:, 1, :], ik[:, :], ciw[:, :]]
                        project(4, hi, lo, lambda act, m, acc: act.activation(to[m], acc, ACT.Copy),
                                lead=Lead(c1, lambda k: col("attn_norm", KD + k), hi, lo, tiles(c1, 5)),
                                side=RotateTiles(c1, {m: to[m] for m in range(3)}, cosT, sinT))
                    dsts = [cq[:, m, :] for m in range(4)] + [kr[:, 0, :], ckv[:, 0, :]] + [t[:, m, :] for t in (sq_, sk_, sv_) for m in range(4)]
                    project(18, hi, lo, lambda act, m, acc: act.activation(dsts[m], acc, ACT.Copy),
                            side=Indexer(pr, iq, ik, ciw, keep, [(future[:, :], "future"), (past[:, :], "past_t"), (after[:, :], "after_t")], ukp, wuv, dict(enumerate(dsts[:5])), 4,
                                         ckv[:, 0, :], 5, cosT, sinT))
                dk, dv = sb(ds, "dk", [P, 4, S]), sb(ds, "dv", [P, NT, 4, P])
                with ExitStack() as c1:
                    made, keyed = sig("made"), sig("keyed")
                    block = c1.enter_context(stage())

                    @block.tensor
                    def _(pe):
                        for m in range(4):
                            pe.matmul(bank[m][:, :], ukp[:, 2 * m:2 * m + 2, :].rearrange("p h n -> p (h n)"), ckv[:, 0, :],
                                      start=True, stop=True).then_inc(made.h, 1)
                        for t in range(NT):
                            pe.matmul(bank[4 + t][:, :], ckv[:, 0, t * P:(t + 1) * P], wuv[:, :, :].rearrange("p h n -> p (h n)"),
                                      start=True, stop=True).then_inc(made.h, 1)

                    @block.vector
                    def _(dve):
                        for m in range(4):
                            dve.wait_ge(made.h, m + 1)
                            dve.tensor_copy(dk[:, m, :], bank[m][:, :]).then_inc(keyed.h, 1)
                        dve.wait_ge(keyed.h, 4)
                        for p0 in (0, HD):
                            dve.tensor_copy(dk[p0:p0 + ROT, :, :], kr[p0:p0 + ROT, 0:1, :].broadcast_to([ROT, 4, S]))

                    @block.scalar
                    def _(act):
                        for t in range(NT):
                            act.wait_ge(made.h, 4 + t + 1)
                            act.activation(dv[:, t, :, :].rearrange("p m n -> p (m n)"), bank[4 + t][:, :], ACT.Copy)
                units, dst = [], []
                for h in range(NH):
                    p0 = h % 2 * HD
                    for n in range(NT):
                        w = (n + 1) * P
                        units.append(([[(cq[p0:p0 + HD, h // 2, n * P:w], dk[p0:p0 + HD, h // 2, 0:w], 0)]], w,
                                      future[:, :] if n == 0 else keep[:, n - 1, 0:w],
                                      [dv[:, b, h // 2, p0:p0 + HD] for b in range(n + 1)], (p0, p0 + HD)))
                        dst.append(oT[p0:p0 + HD, h // 2, n * P:w])
                attend(units, lambda u: dst[u])
            stick_breaking(sq_, sk_, sv_, past, after, oT)

    def stick_breaking(q, k, v, past, after, oT):
        W = [S - b * P for b in range(NT)]
        at_b = [sum(W[:b]) for b in range(NT)]
        ALL = sum(W)
        with ExitStack() as ctx:
            vt = sb(ctx, "vt", [P, NT, 4, P])
            turn([(vt[:, t, :, :], [v[:, m, t * P:(t + 1) * P] for m in range(4)]) for t in range(NT)])
            zs = [sb(ctx, f"zs{i}", [P, ALL]) for i in range(3)]
            sp_ = [sb(ctx, f"sp{i}", [P, ALL]) for i in range(2)]
            aw = [sb(ctx, f"aw{i}", [P, ALL]) for i in range(2)]
            zed, logs, masked, summed, args_, exped, cut, weighed, otk = (
                sig(n) for n in ("zed", "logs", "masked", "summed", "args", "exped", "cut", "weighed", "otk"))
            zcopied = sig("zcopied")
            block = ctx.enter_context(stage())

            @block.tensor
            def _(pe):
                for i in range(NH + 2):
                    if i < NH:
                        p0 = i % 2 * HD
                        for b in range(NT):
                            if i >= 1:
                                pe.wait_ge(zcopied.h, (i - 1) * NT + b + 1)
                            pe.matmul(bank[b][:, 0:W[b]], k[p0:p0 + HD, i // 2, b * P:(b + 1) * P], q[p0:p0 + HD, i // 2, b * P:S],
                                      start=True, stop=True).then_inc(zed.h, 1)
                    u = i - 1
                    if 0 <= u < NH:
                        pe.wait_ge(masked.h, u + 1)
                        for b in range(NT):
                            x = u * NT + b
                            if x >= 3:
                                pe.wait_ge(args_.h, x - 2)
                            o = bank[4 + x % 3]
                            mm = pe.matmul(o[:, 0:W[b]], after[:, :], sp_[u % 2][:, at_b[b]:at_b[b] + W[b]], start=True, stop=b == NT - 1)
                            for c in range(b + 1, NT):
                                mm = pe.matmul(o[:, (c - b) * P:W[b]], ones, sp_[u % 2][:, at_b[c]:at_b[c] + W[c]], start=False, stop=c == NT - 1)
                            mm.then_inc(summed.h, 1)
                    u = i - 2
                    if 0 <= u < NH:
                        p0 = u % 2 * HD
                        pe.wait_ge(cut.h, u + 1)
                        if u >= 1:
                            pe.wait_ge(otk.h, u)
                        for b in range(NT):
                            mm = pe.matmul(bank[7][p0:p0 + HD, b * P:S], vt[:, b, u // 2, p0:p0 + HD], aw[u % 2][:, at_b[b]:at_b[b] + W[b]],
                                           start=b == 0, stop=b == NT - 1)
                        mm.then_inc(weighed.h, 1)

            @block.scalar
            def _(act):
                chain = Chain(act, act_chain)
                act.preload_act_table_set("natural_log_exp_and_others")
                for i in range(NH + 2):
                    if i < NH:
                        if i >= 3:
                            act.wait_ge(args_.h, (i - 2) * NT)
                        if i >= 2:
                            act.wait_ge(summed.h, (i - 1) * NT)
                        for b in range(NT):
                            act.wait_ge(zed.h, i * NT + b + 1)
                            zcopied.by(act.activation(zs[i % 3][:, at_b[b]:at_b[b] + W[b]], bank[b][:, 0:W[b]], ACT.Copy, scale=HD ** -0.5))
                        act.wait_ge(zcopied.h, (i + 1) * NT)
                        s = sp_[i % 2][:, :]
                        chain(act.activation(s, zs[i % 3][:, :], ACT.Abs))
                        chain(act.activation(s, s, ACT.Exp, scale=-1.0))
                        logs.by(act.activation(s, s, ACT.Ln, bias=1.0))
                    u = i - 1
                    if 0 <= u < NH:
                        act.wait_ge(args_.h, (u + 1) * NT)
                        exped.by(act.activation(aw[u % 2][:, :], aw[u % 2][:, :], ACT.Exp))
                    u = i - 2
                    if 0 <= u < NH:
                        p0 = u % 2 * HD
                        act.wait_ge(weighed.h, u + 1)
                        otk.by(act.activation(oT[p0:p0 + HD, 4 + u // 2, :], bank[7][p0:p0 + HD, :], ACT.Copy))

            @block.vector
            def _(dve):
                chain = Chain(dve, dve_chain)
                for i in range(NH + 1):
                    u = i - 1
                    if 0 <= u < NH:
                        w = aw[u % 2]
                        if u >= 2:
                            dve.wait_ge(weighed.h, u - 1)
                        for b in range(NT):
                            dve.wait_ge(summed.h, u * NT + b + 1)
                            x = slice(at_b[b], at_b[b] + W[b])
                            chain(dve.tensor_tensor(w[:, x], zs[u % 3][:, x], bank[4 + (u * NT + b) % 3][:, 0:W[b]], ALU.subtract))
                            args_.by(dve.tensor_scalar(w[:, x], w[:, x], 0.0, None, ALU.min))
                    if i < NH:
                        s = sp_[i % 2]
                        dve.wait_ge(logs.h, i + 1)
                        chain(dve.scalar_tensor_tensor(s[:, :], zs[i % 3][:, :], 0.0, s[:, :], ALU.max, ALU.add))
                        for b in range(NT):
                            ins = dve.tensor_tensor(s[:, at_b[b]:at_b[b] + P], s[:, at_b[b]:at_b[b] + P], past[:, :], ALU.mult)
                        masked.by(ins)
                    if 0 <= u < NH:
                        dve.wait_ge(exped.h, u + 1)
                        for b in range(NT):
                            ins = dve.tensor_tensor(w[:, at_b[b]:at_b[b] + P], w[:, at_b[b]:at_b[b] + P], past[:, :], ALU.mult)
                        cut.by(ins)

    def final():
        with ExitStack() as ctx:
            y = sb(ctx, "y", [P, KD, S])
            res = sb(ctx, "res", [P, 2, NT, 4 * P])
            sq = sb(ctx, "sq", [P, KD, S])
            squared, added, scaled, flipped, stored = (sig(n) for n in ("squared", "added", "scaled", "flipped", "stored"))
            copied = [[sig(f"copied_{e}{q}") for e in ("act", "dve")] for q in range(2)]
            rs = Rstd(ctx, 1, D, EPS, 7)
            block = ctx.enter_context(stage())

            @block.scalar
            def _(act):
                for k in range(KD):
                    act.activation(sq[:, k, :], xT[:, k, :], ACT.Square).then_inc(squared.h, 1)
                rs.act(act)
                for n in range(0, 2 * NT, 2):
                    act.wait_ge(flipped.h, n + 1)
                    act.activation(res[:, n // NT, n % NT, :], bank[n % 7][:, :], ACT.Copy).then_inc(copied[n // NT][0].h, 1)

            @block.tensor
            def _(pe):
                pe.wait_ge(added.h, KD - 1)
                rs.ready.by(rs.sums(pe, 0, sq[:, 0, :]))
                rs.pe(pe)
                for n in range(2 * NT):
                    q, t = n // NT, n % NT
                    pe.wait_ge(scaled.h, 4 * (q + 1))
                    if n == 7:
                        pe.wait_ge(copied[0][0].h, 1)
                    for m in range(4):
                        mm = pe.transpose(bank[n % 7][:, m * P:(m + 1) * P], y[:, 4 * q + m, t * P:(t + 1) * P], ident)
                    mm.then_inc(flipped.h, 1)

            @block.vector
            def _(dve):
                for k in range(1, KD):
                    dve.wait_ge(squared.h, k + 1)
                    dve.tensor_tensor(sq[:, 0, :], sq[:, 0, :], sq[:, k, :], ALU.add).then_inc(added.h, 1)
                    dve.wait_ge(added.h, k)
                rs.dve(dve)
                dve.wait_ge(rs.spread.h, 1)
                for k in range(KD):
                    dve.scalar_tensor_tensor(y[:, k, :], xT[:, k, :], col("final_norm", k), rs.of(), ALU.mult, ALU.mult).then_inc(scaled.h, 1)
                for n in range(1, 2 * NT, 2):
                    dve.wait_ge(flipped.h, n + 1)
                    dve.tensor_copy(res[:, n // NT, n % NT, :], bank[n % 7][:, :]).then_inc(copied[n // NT][1].h, 1)

            @block.sync
            def _(sp):
                for q in range(2):
                    for c in copied[q]:
                        sp.wait_ge(c.h, NT // 2)
                    sp.dma_start(out[0].rearrange("(t p) d -> p t d", p=P)[:, :, q * 4 * P:(q + 1) * 4 * P], res[:, q, :, :]).then_inc(stored.h, 16)
                sp.wait_ge(stored.h, 32)


    def tiles(ctx, n):
        return [sb(ctx, "tile", [P, S])[:, :] for _ in range(n)]

    setup()

    def layer_one():
        with ExitStack() as st:
            oT = sb(st, "oT", [P, KD, S])
            with ExitStack() as rw:
                r, k, v = (sb(rw, n, [P, 4, S]) for n in "rkv")
                zt, zg = sb(rw, "zt", [P, S]), sb(rw, "zg", [P, S])
                with ExitStack() as at:
                    qT, kd, vT = sb(at, "qT", [P, 4, S]), sb(at, "kd", [P, 2, S]), sb(at, "vT", [P, S])
                    vt, bias = sb(at, "vt", [P, 1, 4, P]), sb(at, "bias", [P, NH, 2 * P])
                    sinks, nsinks = sb(at, "sinks", [P, NH]), sb(at, "nsinks", [P, NH])
                    with ExitStack() as pr:
                        hi, lo = sb(pr, "hi", [P, KD, S], F32R), sb(pr, "lo", [P, KD, S], F32R)
                        pad = [sb(pr, f"pad{i}", [P, S + 1]) for i in range(2)]
                        df = sb(pr, "df", [P, S])
                        shifted = sig("shifted")
                        s0 = state["s"]

                        def dst(m):
                            return (qT[:, m, :] if m < 4 else kd[:, m - 4, :] if m < 6 else vT[:, :] if m == 6
                                    else r[:, m - 7, :] if m < 11 else k[:, m - 11, :] if m < 15
                                    else v[:, m - 15, :] if m < 19 else (zt, zg)[m - 19][:, :])

                        def put(act, m, acc):
                            if m < 7:
                                return act.activation(dst(m), acc, ACT.Copy)
                            if m >= 9:
                                act.wait_ge(shifted.h, m - 8)
                            return act.activation(pad[m % 2][:, 1:S + 1], acc, ACT.Copy)

                        def post(dve, chain, m):
                            if m == 0:
                                chain(dve.memset(pad[0][:, 0:1], 0.0))
                                chain(dve.memset(pad[1][:, 0:1], 0.0))
                            if m < 7:
                                return
                            x = pad[m % 2]
                            chain(dve.tensor_tensor(df[:, :], x[:, 0:S], x[:, 1:S + 1], ALU.subtract))
                            shifted.by(dve.scalar_tensor_tensor(dst(m), df[:, :], col("mix", m - 7), x[:, 1:S + 1], ALU.mult, ALU.add))
                            dve.wait_ge(shifted.h, m - 6)
                        lead = Lead(pr, lambda k: col("norm_mix_pre", k), hi, lo, [r[:, m, :] for m in range(4)] + [zt[:, :]])
                        project(21, hi, lo, put, post, lead, LocalSide(pr, bias, sinks, nsinks, vT, vt))
                    local_attention(qT, kd, vt, bias, sinks, nsinks, oT)
                rwkv(r, k, v, zt, zg, oT[:, 4:8, :], rw)

            with ExitStack() as pr:
                hi, lo, mixed = sb(pr, "hi", [P, KD, S], F32R), sb(pr, "lo", [P, KD, S], F32R), sb(pr, "mixed", [P, KD, S])
                project(8, hi, lo, lambda act, m, acc: act.activation(mixed[:, m, :], acc, ACT.Copy), lead=Cut(oT, hi, lo))
                add_normed(mixed, "norm_mix_post")
    layer_one()
    with ExitStack() as st:
        f = sb(st, "f", [P, KD, S])
        with ExitStack() as ff:
            hi, lo = sb(ff, "hi", [P, KD, S], F32R), sb(ff, "lo", [P, KD, S], F32R)
            for ch in range(2):
                ffn(wu1, FF1, wd1, conv1, 16 * ch, 16, PARTS1, hi, lo, ACT.Gelu_apprx_tanh, ch == 1, f,
                    (lambda ctx, scratch: Lead(ctx, lambda k: col("norm_ffn_pre", k), hi, lo, scratch)) if ch == 0 else None)
        add_normed(f, "norm_ffn_post")
    for layer in range(2):
        with ExitStack() as st:
            oT = sb(st, "oT", [P, KD, S])
            (even_mixer, odd_mixer)[layer](cosT, sinT, oT)
            with ExitStack() as pr:
                hi, lo = sb(pr, "hi", [P, KD, S], F32R), sb(pr, "lo", [P, KD, S], F32R)
                project(8, hi, lo, None, lambda dve, chain, m, acc: dve.tensor_tensor(xT[:, m, :], acc, xT[:, m, :], ALU.add),
                        Cut(oT, hi, lo))
        with ExitStack() as ff:
            hi, lo = sb(ff, "hi", [P, KD, S], F32R), sb(ff, "lo", [P, KD, S], F32R)
            ffn(wu2[layer], FF2, wd2[layer], conv2[layer], 0, 22, PARTS2, hi, lo, ACT.Silu, True, xT,
                lambda ctx, scratch: Lead(ctx, lambda k: col("ffn_norm", KD * layer + k), hi, lo, scratch))
    final()


_OUTS = [((1, S, D), "float32")]


def kernel(**inputs):
    import numpy as _np
    import concourse.bacc as _bacc
    from concourse import mybir as _mybir
    from concourse.bass_utils import run_bass_kernel_spmd as _run

    nc = _bacc.Bacc("TRN2", target_bir_lowering=False, num_devices=1)
    arrays, args = {}, {}
    inputs["cst"] = constants()
    for name, value in inputs.items():
        v = _np.ascontiguousarray(value)
        arrays[f"in_{name}_dram"] = v
        args[name] = nc.dram_tensor(f"in_{name}_dram", v.shape, _mybir.dt.from_np(v.dtype), kind="ExternalInput").ap()
    out = nc.dram_tensor("out_0_dram", (1, S, D), F32, kind="ExternalOutput").ap()
    program(nc, args, out)
    r = _run(nc, [arrays], core_ids=[0])
    return r.results[0]["out_0_dram"]
```
